# Optimizing a Trainium2 kernel written in Bass

```python
import math
import jax, jax.numpy as jnp
from jax import lax
import numpy as np

D_MODEL = 1024
BATCH = 1
SEQ = 512
DEPTH = 2

GRID_W = 64
ROPE_THETA = 10000.0
Q_BLOCK = 128
EPS = 1e-6

GQA_HEADS = 8
GQA_KV_HEADS = 2
GQA_GROUP = GQA_HEADS // GQA_KV_HEADS
GQA_HEAD_DIM = D_MODEL // 16
GQA_Q_W = GQA_HEADS * GQA_HEAD_DIM
GQA_KV_W = GQA_KV_HEADS * GQA_HEAD_DIM

MLA_HEADS = 8
MLA_NOPE_DIM = D_MODEL // 16
MLA_ROPE_DIM = D_MODEL // 32
MLA_V_DIM = D_MODEL // 16
MLA_QK_DIM = MLA_NOPE_DIM + MLA_ROPE_DIM
MLA_Q_RANK = (3 * D_MODEL) // 8
MLA_KV_RANK = D_MODEL // 4
MLA_OUT_W = MLA_HEADS * MLA_V_DIM

D_FF = 4 * D_MODEL

SPLIT_SIZES = (GQA_Q_W, GQA_KV_W, GQA_KV_W, MLA_Q_RANK, MLA_KV_RANK, MLA_ROPE_DIM, 2 * D_MODEL)
IN_W = sum(SPLIT_SIZES)
SPLIT_POINTS = [int(v) for v in np.cumsum(SPLIT_SIZES)[:-1]]


def rmsnorm(x, g):
    xf = x.astype(jnp.float32)
    y = xf * lax.rsqrt(jnp.mean(xf * xf, axis=-1, keepdims=True) + EPS)
    return (y * g.astype(jnp.float32)).astype(x.dtype)

def axial_rope_tables(seq, rot_dim):
    rows = seq // GRID_W
    row = jnp.repeat(jnp.arange(rows, dtype=jnp.float32), GRID_W)
    col = jnp.tile(jnp.arange(GRID_W, dtype=jnp.float32), rows)
    half = rot_dim // 2
    inv = ROPE_THETA ** (-jnp.arange(0, half, 2, dtype=jnp.float32) / half)
    ar = row[:, None] * inv[None, :]
    ac = col[:, None] * inv[None, :]
    ang = jnp.concatenate([ar, ar, ac, ac], axis=-1)
    return jnp.cos(ang), jnp.sin(ang)

def apply_axial_rope(x, cos, sin):
    d = x.shape[-1]
    h = d // 2
    q = h // 2
    shape = (cos.shape[0],) + (1,) * (x.ndim - 3) + (d,)
    c = cos.reshape(shape).astype(x.dtype)
    s = sin.reshape(shape).astype(x.dtype)
    xr, xc = x[..., :h], x[..., h:]
    rot = lambda z: jnp.concatenate([-z[..., q:], z[..., :q]], axis=-1)
    x_rot = jnp.concatenate([rot(xr), rot(xc)], axis=-1)
    return x * c + x_rot * s

def blocked_attention(q, k, v, scale):
    b, s, hk, g, dk = q.shape
    dv = v.shape[-1]
    nb = s // Q_BLOCK
    qb = q.reshape(b, nb, Q_BLOCK, hk, g, dk).swapaxes(0, 1)

    def one_block(qblk):
        sc = jnp.einsum('bqhgd,bkhd->bhgqk', qblk, k).astype(jnp.float32) * scale
        p = jax.nn.softmax(sc, axis=-1).astype(v.dtype)
        return jnp.einsum('bhgqk,bkhd->bqhgd', p, v)

    out = lax.map(one_block, qb)
    return out.swapaxes(0, 1).reshape(b, s, hk * g * dv)

def token_mixer(u, w_in, b_gate, q_norm_g, k_norm_g, q_a_norm_g, kv_a_norm_g,
                w_q_up, w_kv_up, w_branch_a, w_branch_b, w_o,
                cos_a, sin_a, cos_b, sin_b):
    b, s, _ = u.shape
    z = u @ w_in
    qa, ka, va, cq, ckv, kr, gl = jnp.split(z, SPLIT_POINTS, axis=-1)

    qa = qa.reshape(b, s, GQA_HEADS, GQA_HEAD_DIM)
    ka = ka.reshape(b, s, GQA_KV_HEADS, GQA_HEAD_DIM)
    va = va.reshape(b, s, GQA_KV_HEADS, GQA_HEAD_DIM)
    qa = apply_axial_rope(rmsnorm(qa, q_norm_g), cos_a, sin_a)
    ka = apply_axial_rope(rmsnorm(ka, k_norm_g), cos_a, sin_a)
    qa = qa.reshape(b, s, GQA_KV_HEADS, GQA_GROUP, GQA_HEAD_DIM)
    ya = blocked_attention(qa, ka, va, 1.0 / math.sqrt(GQA_HEAD_DIM))

    qb = (rmsnorm(cq, q_a_norm_g) @ w_q_up).reshape(b, s, MLA_HEADS, MLA_QK_DIM)
    q_nope, q_rope = qb[..., :MLA_NOPE_DIM], qb[..., MLA_NOPE_DIM:]
    q_rope = apply_axial_rope(q_rope, cos_b, sin_b)
    kvb = (rmsnorm(ckv, kv_a_norm_g) @ w_kv_up).reshape(b, s, MLA_HEADS, MLA_NOPE_DIM + MLA_V_DIM)
    k_nope, vb = kvb[..., :MLA_NOPE_DIM], kvb[..., MLA_NOPE_DIM:]
    k_rope = apply_axial_rope(kr, cos_b, sin_b)
    k_rope = jnp.broadcast_to(k_rope[:, :, None, :], (b, s, MLA_HEADS, MLA_ROPE_DIM))
    qb = jnp.concatenate([q_nope, q_rope], axis=-1)[:, :, :, None, :]
    kb = jnp.concatenate([k_nope, k_rope], axis=-1)
    yb = blocked_attention(qb, kb, vb, 1.0 / math.sqrt(MLA_QK_DIM))

    gates = jax.nn.sigmoid((gl + b_gate).astype(jnp.float32)).astype(u.dtype)
    g_a, g_b = gates[..., :D_MODEL], gates[..., D_MODEL:]
    merged = g_a * (ya @ w_branch_a) + g_b * (yb @ w_branch_b)
    return merged @ w_o

def first_inputs(seed: int = 0) -> dict:
    key = jax.random.key(seed)
    ks = jax.random.split(key, 20)
    f32 = jnp.float32

    def w(k, fan_in, fan_out):
        return jax.random.normal(k, (DEPTH, fan_in, fan_out), f32) * fan_in ** -0.5

    def gain(k, n):
        return 1.0 + 0.05 * jax.random.normal(k, (DEPTH, n), f32)

    return {
        "x": jax.random.normal(ks[0], (BATCH, SEQ, D_MODEL), f32),
        "w_in": w(ks[1], D_MODEL, IN_W),
        "b_gate": 0.1 * jax.random.normal(ks[2], (DEPTH, 2 * D_MODEL), f32),
        "q_norm_g": gain(ks[3], GQA_HEAD_DIM),
        "k_norm_g": gain(ks[4], GQA_HEAD_DIM),
        "q_a_norm_g": gain(ks[5], MLA_Q_RANK),
        "kv_a_norm_g": gain(ks[6], MLA_KV_RANK),
        "w_q_up": w(ks[7], MLA_Q_RANK, MLA_HEADS * MLA_QK_DIM),
        "w_kv_up": w(ks[8], MLA_KV_RANK, MLA_HEADS * (MLA_NOPE_DIM + MLA_V_DIM)),
        "w_branch_a": w(ks[9], GQA_Q_W, D_MODEL),
        "w_branch_b": w(ks[10], MLA_OUT_W, D_MODEL),
        "w_o": w(ks[11], D_MODEL, D_MODEL),
        "w_ffn_up": w(ks[12], D_MODEL, D_FF),
        "w_ffn_down": w(ks[13], D_FF, D_MODEL),
        "pre_mix_g": gain(ks[14], D_MODEL),
        "post_mix_g": gain(ks[15], D_MODEL),
        "pre_ffn_g": gain(ks[16], D_MODEL),
        "post_ffn_g": gain(ks[17], D_MODEL),
    }

def first_block(x, w_in, b_gate, q_norm_g, k_norm_g, q_a_norm_g, kv_a_norm_g,
              w_q_up, w_kv_up, w_branch_a, w_branch_b, w_o, w_ffn_up, w_ffn_down,
              pre_mix_g, post_mix_g, pre_ffn_g, post_ffn_g):
    seq = x.shape[1]
    cos_a, sin_a = axial_rope_tables(seq, GQA_HEAD_DIM)
    cos_b, sin_b = axial_rope_tables(seq, MLA_ROPE_DIM)
    for l in range(DEPTH):
        u = rmsnorm(x, pre_mix_g[l])
        m = token_mixer(u, w_in[l], b_gate[l], q_norm_g[l], k_norm_g[l],
                        q_a_norm_g[l], kv_a_norm_g[l], w_q_up[l], w_kv_up[l],
                        w_branch_a[l], w_branch_b[l], w_o[l],
                        cos_a, sin_a, cos_b, sin_b)
        x = x + rmsnorm(m, post_mix_g[l])
        h = rmsnorm(x, pre_ffn_g[l]) @ w_ffn_up[l]
        f = jnp.square(jax.nn.relu(h)) @ w_ffn_down[l]
        x = x + rmsnorm(f, post_ffn_g[l])
    return x


N_A_LAYERS = DEPTH // 2
N_B_LAYERS = DEPTH - N_A_LAYERS
D_SSM = D_MODEL
SSM_GROUP = 16
N_GROUPS = D_SSM // SSM_GROUP
STATE = 64
N_HEADS = 16
HEAD_DIM = 64
D_ATT = N_HEADS * HEAD_DIM
D_FF_2 = 2816
CONV_W = 3
DT_MIN = 1e-3
DT_MAX = 1e-1


def rms_norm(x, g):
    xf = x.astype(jnp.float32)
    y = xf * lax.rsqrt(jnp.mean(xf * xf, axis=-1, keepdims=True) + EPS)
    return (y * g.astype(jnp.float32)).astype(x.dtype)

def s5_mixer(h, w_in, a_re, a_im, log_dt, b_re, b_im, c_re, c_im, d_skip, w_glu):
    bsz, seq, _ = h.shape
    f32 = jnp.float32
    u = (h @ w_in).astype(f32).reshape(bsz, seq, N_GROUPS, SSM_GROUP)
    a_re = a_re.astype(f32)
    a_im = a_im.astype(f32)
    dt = jnp.exp(log_dt.astype(f32))[:, None]
    mag = jnp.exp(a_re * dt)
    ab_re = mag * jnp.cos(a_im * dt)
    ab_im = mag * jnp.sin(a_im * dt)
    den = a_re * a_re + a_im * a_im
    f_re = ((ab_re - 1.0) * a_re + ab_im * a_im) / den
    f_im = (ab_im * a_re - (ab_re - 1.0) * a_im) / den
    b_re = b_re.astype(f32)
    b_im = b_im.astype(f32)
    bb_re = f_re[..., None] * b_re - f_im[..., None] * b_im
    bb_im = f_re[..., None] * b_im + f_im[..., None] * b_re
    bu_re = jnp.einsum('blgh,gph->blgp', u, bb_re)
    bu_im = jnp.einsum('blgh,gph->blgp', u, bb_im)
    shape_a = (1, seq, N_GROUPS, STATE)
    a_seq_re = jnp.broadcast_to(ab_re[None, None], shape_a)
    a_seq_im = jnp.broadcast_to(ab_im[None, None], shape_a)

    def combine(e1, e2):
        a1r, a1i, b1r, b1i = e1
        a2r, a2i, b2r, b2i = e2
        return (a2r * a1r - a2i * a1i,
                a2r * a1i + a2i * a1r,
                a2r * b1r - a2i * b1i + b2r,
                a2r * b1i + a2i * b1r + b2i)

    _, _, s_re, s_im = lax.associative_scan(
        combine, (a_seq_re, a_seq_im, bu_re, bu_im), axis=1)
    y = (jnp.einsum('blgp,ghp->blgh', s_re, c_re.astype(f32))
         - jnp.einsum('blgp,ghp->blgh', s_im, c_im.astype(f32))
         + d_skip.astype(f32) * u)
    y = jax.nn.gelu(y.reshape(bsz, seq, D_SSM)).astype(h.dtype)
    z = y @ w_glu
    return z[..., :D_MODEL] * jax.nn.sigmoid(z[..., D_MODEL:])

def stick_breaking_attention(h, w_q, k, v, w_o):
    bsz, seq, _ = h.shape
    scale = HEAD_DIM ** -0.5
    q = (h @ w_q).reshape(bsz, seq, N_HEADS, HEAD_DIM).transpose(0, 2, 1, 3) * scale
    outs = []
    for blk in range(seq // Q_BLOCK):
        t0 = blk * Q_BLOCK
        nk = t0 + Q_BLOCK
        qb = q[:, :, t0:nk]
        kb = k[:, :, :nk]
        vb = v[:, :, :nk]
        z = jnp.einsum('bhqd,bhkd->bhqk', qb, kb).astype(jnp.float32)
        t_idx = t0 + jnp.arange(Q_BLOCK)[:, None]
        s_idx = jnp.arange(nk)[None, :]
        causal = s_idx < t_idx
        log_beta = jax.nn.log_sigmoid(z)
        log_one_minus = jnp.where(causal, log_beta - z, 0.0)
        rem = lax.cumsum(log_one_minus, axis=3, reverse=True) - log_one_minus
        w = jnp.where(causal, jnp.exp(log_beta + rem), 0.0)
        outs.append(jnp.einsum('bhqk,bhkd->bhqd', w.astype(vb.dtype), vb))
    o = jnp.concatenate(outs, axis=2).transpose(0, 2, 1, 3).reshape(bsz, seq, D_ATT)
    return o @ w_o

def conv_ffn(h, w_up, conv_w, conv_b, w_down):
    gu = h @ w_up
    g = gu[..., :D_FF_2]
    u = gu[..., D_FF_2:]
    g = lax.conv_general_dilated(
        g, conv_w, window_strides=(1,), padding=[(CONV_W - 1, 0)],
        dimension_numbers=('NWC', 'WIO', 'NWC'), feature_group_count=D_FF_2) + conv_b
    return (jax.nn.silu(g) * u) @ w_down

def second_inputs(seed: int = 0) -> dict:
    key = jax.random.key(seed)
    ks = jax.random.split(key, 24)
    f32 = jnp.float32
    nrm = lambda k, shape, s: jax.random.normal(k, shape, f32) * s
    n_idx = jnp.arange(STATE, dtype=f32)
    return {
        "x": jax.random.normal(ks[0], (BATCH, SEQ, D_MODEL), f32),
        "norm_mix": 1.0 + nrm(ks[1], (DEPTH, D_MODEL), 0.02),
        "norm_ffn": 1.0 + nrm(ks[2], (DEPTH, D_MODEL), 0.02),
        "norm_kv": 1.0 + nrm(ks[3], (D_MODEL,), 0.02),
        "norm_final": 1.0 + nrm(ks[4], (D_MODEL,), 0.02),
        "ssm_w_in": nrm(ks[5], (N_A_LAYERS, D_MODEL, D_SSM), D_MODEL ** -0.5),
        "ssm_a_re": -0.5 * jnp.exp(nrm(ks[6], (N_A_LAYERS, N_GROUPS, STATE), 0.05)),
        "ssm_a_im": math.pi * n_idx + nrm(ks[7], (N_A_LAYERS, N_GROUPS, STATE), 0.01),
        "ssm_log_dt": jax.random.uniform(ks[8], (N_A_LAYERS, N_GROUPS), f32,
                                         minval=math.log(DT_MIN), maxval=math.log(DT_MAX)),
        "ssm_b_re": nrm(ks[9], (N_A_LAYERS, N_GROUPS, STATE, SSM_GROUP), (2 * SSM_GROUP) ** -0.5),
        "ssm_b_im": nrm(ks[10], (N_A_LAYERS, N_GROUPS, STATE, SSM_GROUP), (2 * SSM_GROUP) ** -0.5),
        "ssm_c_re": nrm(ks[11], (N_A_LAYERS, N_GROUPS, SSM_GROUP, STATE), (2 * STATE) ** -0.5),
        "ssm_c_im": nrm(ks[12], (N_A_LAYERS, N_GROUPS, SSM_GROUP, STATE), (2 * STATE) ** -0.5),
        "ssm_d": nrm(ks[13], (N_A_LAYERS, N_GROUPS, SSM_GROUP), 1.0),
        "ssm_w_glu": nrm(ks[14], (N_A_LAYERS, D_SSM, 2 * D_MODEL), D_SSM ** -0.5),
        "kv_w": nrm(ks[15], (D_MODEL, 2 * D_ATT), D_MODEL ** -0.5),
        "attn_w_q": nrm(ks[16], (N_B_LAYERS, D_MODEL, D_ATT), D_MODEL ** -0.5),
        "attn_w_o": nrm(ks[17], (N_B_LAYERS, D_ATT, D_MODEL), D_ATT ** -0.5),
        "ffn_w_up": nrm(ks[18], (DEPTH, D_MODEL, 2 * D_FF_2), D_MODEL ** -0.5),
        "ffn_conv_w": nrm(ks[19], (DEPTH, CONV_W, 1, D_FF_2), CONV_W ** -0.5),
        "ffn_conv_b": nrm(ks[20], (DEPTH, D_FF_2), 0.01),
        "ffn_w_down": nrm(ks[21], (DEPTH, D_FF_2, D_MODEL), D_FF_2 ** -0.5),
    }

def second_block(x, norm_mix, norm_ffn, norm_kv, norm_final,
              ssm_w_in, ssm_a_re, ssm_a_im, ssm_log_dt, ssm_b_re, ssm_b_im,
              ssm_c_re, ssm_c_im, ssm_d, ssm_w_glu,
              kv_w, attn_w_q, attn_w_o,
              ffn_w_up, ffn_conv_w, ffn_conv_b, ffn_w_down):
    bsz, seq, _ = x.shape
    k_shared = None
    v_shared = None
    for layer in range(DEPTH):
        h = rms_norm(x, norm_mix[layer])
        if layer < N_A_LAYERS:
            x = x + s5_mixer(h, ssm_w_in[layer], ssm_a_re[layer], ssm_a_im[layer],
                             ssm_log_dt[layer], ssm_b_re[layer], ssm_b_im[layer],
                             ssm_c_re[layer], ssm_c_im[layer], ssm_d[layer],
                             ssm_w_glu[layer])
        else:
            j = layer - N_A_LAYERS
            x = x + stick_breaking_attention(h, attn_w_q[j], k_shared, v_shared, attn_w_o[j])
        x = x + conv_ffn(rms_norm(x, norm_ffn[layer]), ffn_w_up[layer],
                         ffn_conv_w[layer], ffn_conv_b[layer], ffn_w_down[layer])
        if layer == N_A_LAYERS - 1:
            kv = rms_norm(x, norm_kv) @ kv_w
            k_shared = kv[..., :D_ATT].reshape(bsz, seq, N_HEADS, HEAD_DIM).transpose(0, 2, 1, 3)
            v_shared = kv[..., D_ATT:].reshape(bsz, seq, N_HEADS, HEAD_DIM).transpose(0, 2, 1, 3)
    return rms_norm(x, norm_final)


def setup_inputs(seed=0):
    out = dict(first_inputs(seed))
    for name, value in second_inputs(seed + 1).items():
        if name != "x":
            out[name + "_2"] = value
    return out


def reference(
    x, w_in, b_gate, q_norm_g, k_norm_g, q_a_norm_g, kv_a_norm_g, w_q_up, w_kv_up, w_branch_a,
    w_branch_b, w_o, w_ffn_up, w_ffn_down, pre_mix_g, post_mix_g, pre_ffn_g, post_ffn_g,
    norm_mix_2, norm_ffn_2, norm_kv_2, norm_final_2, ssm_w_in_2, ssm_a_re_2, ssm_a_im_2,
    ssm_log_dt_2, ssm_b_re_2, ssm_b_im_2, ssm_c_re_2, ssm_c_im_2, ssm_d_2, ssm_w_glu_2, kv_w_2,
    attn_w_q_2, attn_w_o_2, ffn_w_up_2, ffn_conv_w_2, ffn_conv_b_2, ffn_w_down_2,
):
    x = first_block(
        x, w_in, b_gate, q_norm_g, k_norm_g, q_a_norm_g, kv_a_norm_g, w_q_up, w_kv_up,
        w_branch_a, w_branch_b, w_o, w_ffn_up, w_ffn_down, pre_mix_g, post_mix_g, pre_ffn_g,
        post_ffn_g,
    )
    return second_block(
        x, norm_mix_2, norm_ffn_2, norm_kv_2, norm_final_2, ssm_w_in_2, ssm_a_re_2, ssm_a_im_2,
        ssm_log_dt_2, ssm_b_re_2, ssm_b_im_2, ssm_c_re_2, ssm_c_im_2, ssm_d_2, ssm_w_glu_2,
        kv_w_2, attn_w_q_2, attn_w_o_2, ffn_w_up_2, ffn_conv_w_2, ffn_conv_b_2, ffn_w_down_2,
    )


_drawn_inputs = setup_inputs


def setup_inputs(seed=0):
    import zlib

    import numpy as np

    out = dict(_drawn_inputs(seed))
    spreads = {}
    factors = {'norm_mix_2': 8.0,
     'norm_ffn_2': 5.57,
     'norm_kv_2': 8.0,
     'norm_final_2': 8.431,
     'ssm_a_re_2': 64.0,
     'ssm_a_im_2': 29.68,
     'ssm_log_dt_2': 47.024,
     'ssm_b_re_2': 33.92,
     'ssm_b_im_2': 39.44,
     'ssm_c_re_2': 40.688,
     'ssm_c_im_2': 42.56,
     'ffn_conv_b_2': 8.0}
    for name, (base, spread) in spreads.items():
        noise = np.random.default_rng([zlib.crc32(name.encode()), seed]).standard_normal(out[name].shape)
        drawn = base * np.exp(spread * noise) if base else spread * noise
        out[name] = __import__('jax').numpy.asarray(drawn.astype(out[name].dtype))
    for name, factor in factors.items():
        out[name] = (out[name] * factor).astype(out[name].dtype)
    return out
```

```python
import math
from contextlib import ExitStack

import numpy as np

import concourse.bass as bass
from concourse import mybir

F32 = mybir.dt.float32
F32R = mybir.dt.float32r
ALU = mybir.AluOpType
ACT = mybir.ActivationFunctionType
AX_X = mybir.AxisListType.X

P = 128
SEQ = 512
DM = 1024
DT = DM // P
LAYERS = 2
EPS = 1e-6
KT = SEQ // P
GRID_W = 64
ROPE_THETA = 10000.0

HEADS = 8
HD = 64
KV_HEADS = 2
QT = HEADS * HD // P
ROPE = 32
QK = HD + ROPE
Q_RANK, KV_RANK = 384, 256
CQT, CKT = Q_RANK // P, KV_RANK // P
FF_TILES = 4096 // P
HALF = FF_TILES // 2
SLOT = 8 * P

C_TILES = 2816 // P
GROUPS, STATE, GH = 64, 64, 16
PAIRS = GROUPS // 2
H2 = 16
HIDDEN = -2.0 ** 100
MAGIC = 1.5 * 2.0 ** 23
INV2PI = 1.0 / (2.0 * math.pi)
PI_A, PI_B = 6.28125, 0.0019350051879882812
PI_C = 2.0 * math.pi - PI_A - PI_B
CHUNKS_L = 124
CHUNKS = 2 * CHUNKS_L + 192

RAW = 4
CUT = 2


RC_LAST, POST_MIX, POST_FFN = 3 + QT, 4 + QT, 6 + QT


class Signal:

    def __init__(self, sem, per_layer, slots=0):
        self.sem, self.per_layer, self.slots = sem, per_layer, slots

    def after(self, l, k):
        return l * self.per_layer + (k + 1 + self.slots)

    def room(self, l, k):
        return l * self.per_layer + (k + 1)


class Step:

    def __init__(self, kind, add=None, b=None, c=None, cg=None, cn=None, cols=None, cu=None, done=None, eu=None, ff=None,
                 first=None, g=None, gain=None, ge=None, gg=None, group=None, h=None, i=None, j=None, kt=None,
                 kv=None, last_s=None, last_use=None, layer=None, m=None, mg=None, mk=None, mt=None, n=None,
                 o=None, p=None, pv=None, q2=None, qk=None, rhs=None, ro=None, rot=None, rows=None, s=None,
                 sc=None, sn=None, so=None, stat=None, sums=None, t=None, tb=None, u=None, up=None, v2=None,
                 version=None, vh=None, what=None, x=None, z=None):
        self.kind, self.add, self.b, self.c, self.cg, self.cn, self.cols, self.cu = kind, add, b, c, cg, cn, cols, cu
        self.done, self.eu, self.ff, self.first, self.g, self.gain, self.ge, self.gg = done, eu, ff, first, g, gain, ge, gg
        self.group, self.h, self.i, self.j, self.kt, self.kv, self.last_s, self.last_use = group, h, i, j, kt, kv, last_s, last_use
        self.layer, self.m, self.mg, self.mk, self.mt, self.n, self.o, self.p = layer, m, mg, mk, mt, n, o, p
        self.pv, self.q2, self.qk, self.rhs, self.ro, self.rot, self.rows, self.s = pv, q2, qk, rhs, ro, rot, rows, s
        self.sc, self.sn, self.so, self.stat, self.sums, self.t, self.tb, self.u = sc, sn, so, stat, sums, t, tb, u
        self.up, self.v2, self.version, self.vh, self.what, self.x, self.z = up, v2, version, vh, what, x, z


class Plan:

    def __init__(self):
        self.steps, self.total = [], {}

    def add(self, kind, take="", **info):
        at = {}
        for item in take.split():
            name, n = (item.split(":") + ["1"])[:2]
            at[name] = self.total.get(name, 0)
            self.total[name] = at[name] + int(n)
        step = Step(kind, **at, **info)
        self.steps.append(step)
        return step


def linear(plan, jobs, after, lag=1):
    mm = []
    for x in range(len(jobs) + lag):
        if x < len(jobs):
            mm.append(plan.add("mm", f"c:{len(jobs[x]['kt'])} j", first=x == 0, **jobs[x]))
        if x == 0 and after.get("stat"):
            plan.add("stat", "s:8 g", version=after["stat"])
        if x >= lag:
            after["evac"](x - lag, mm[x - lag])


def done_of(mm):
    return mm.c + len(mm.kt) - 1


def attention_steps(plan):
    n = 2 * HEADS * KT
    mm = ev = None
    for x in range(n + 3):
        if x < n:
            plan.add("S", "u", h=x // KT, t=x % KT)
        if 1 <= x <= n:
            plan.add("N", u=x - 1)
        if 2 <= x <= n + 1:
            plan.add("T", u=x - 2, h=(x - 2) // KT, t=(x - 2) % KT)
        if x >= 6 and (x - 6) % KT == 0:
            plan.add("PV", "b pv", h=(x - 6) // KT)
        m = x // KT + 1 - HEADS
        if x < n and 0 <= m < HEADS:
            if x % KT == 0:
                mm = plan.add("mla_mm", "c j:2", h=m, kt=[None])
            if x % KT == 1:
                ev = plan.add("mla_evac", "rot mk", h=m, j=mm.j, done=mm.c)
            if x % KT == 2:
                plan.add("rope", "b", what="mla", h=m, rot=ev.rot, j=ev.j, i=0, rows=QK)
                plan.add("mla_v", "b vh", h=m, mk=ev.mk, j=ev.j)

def plan_layer():
    plan = Plan()
    plan.add("norm", "n:8", gain=0, version=0)
    items = [("q", i) for i in range(QT)] + [("k", 0), ("v", 0)] + [("cq", i) for i in range(CQT)]
    items += [("ckv", i) for i in range(CKT)] + [("kr", 0)]
    ev = {}

    def first_products(x, mm):
        what, i = items[x]
        take = {"q": "s rot", "k": "s rot", "v": "", "cq": "s cn", "ckv": "s cn", "kr": "rot"}[what]
        group = {"q": 1 + i, "k": 1 + QT, "cq": 2 + QT, "ckv": 3 + QT}.get(what)
        ev[x] = plan.add("evac_" + what, take, i=i, x=x, j=mm.j, done=mm.c, group=group)
        if x >= 1:
            finish(x - 1)

    def finish(x):
        what, i = items[x]
        if what in ("q", "k"):
            plan.add("rope", "b g qk", what=what, i=i, x=x, rot=ev[x].rot, s=ev[x].s, h=0, rows=P)
        elif what == "kr":
            plan.add("rope", "b", what=what, i=i, x=x, rot=ev[x].rot, j=ev[x].j, h=0, rows=QK)
        elif what == "v":
            plan.add("gqa_v", "b vh", x=x, j=ev[x].j)
        elif (what, i) in (("cq", CQT - 1), ("ckv", CKT - 1)):
            plan.add("rc_" + what, "g", s=ev[x].s)

    jobs = [dict(kt=[DT], cols=QK if what == "kr" else P, rhs="u") for what, _ in items]
    linear(plan, jobs, dict(stat="0", evac=first_products))
    finish(len(items) - 1)
    attention_steps(plan)
    plan.add("regain", "n:8", gain=0)

    def gates_and_branches(x, mm):
        what, m = ("ga", "gb", "br_a", "br_b")[x % 4], x // 4
        plan.add("evac_" + what, {"ga": "ge", "gb": "ge", "br_b": "mt"}.get(what, ""), m=m, j=mm.j,
                 done=mm.c)
        if what == "gb" and m:
            plan.add("merge", "mg", m=m - 1)

    jobs = []
    for m in range(DT):
        jobs += [dict(kt=[DT], cols=P, rhs="u"), dict(kt=[DT], cols=P, rhs="u"),
                 dict(kt=[QT], cols=P, rhs="ya"), dict(kt=[QT], cols=P, rhs="yb")]
    linear(plan, jobs, dict(evac=gates_and_branches))
    plan.add("merge", "mg", m=DT - 1)

    def into_ff(add, group=None):
        return lambda x, mm: plan.add("evac_ff", "ff" if group is None else "ff s", m=x, j=mm.j, done=done_of(mm),
                                      add=add, group=group)

    tile = dict(cols=P, kt=[DT])
    linear(plan, [dict(tile, rhs="merged")] * DT, dict(evac=into_ff(False, POST_MIX)))
    plan.add("post", "g x:8 sc:8", gain=8)
    plan.add("norm", "n:8", gain=16, version=1)
    for half in range(2):
        linear(plan, [dict(tile, rhs="u")] * HALF,
               dict(stat="" if half else "1",
                    evac=lambda x, mm: plan.add("evac_up", "up", m=x, j=mm.j, done=mm.c)))
        linear(plan, [dict(cols=P, kt=[DT, DT], rhs="hidden")] * DT, dict(evac=into_ff(half == 1, POST_FFN if half else None)))
    plan.add("post", "g x:8 sc:8", gain=24)
    return plan


def conv_ffn_steps(plan, layer, version):
    plan.add("norm", "n:8", gain=("ffn", layer), version=version)

    def hidden(x, mm):
        if x % 2 == 0:
            plan.add("evac_gate", "cg", m=x // 2, j=mm.j, done=mm.c, layer=layer)
        else:
            plan.add("evac_cup", "cu", m=x // 2, j=mm.j, done=mm.c)

    linear(plan, [dict(kt=[DT], cols=P, rhs="u")] * (2 * C_TILES), dict(stat=str(version), evac=hidden))
    linear(plan, [dict(kt=[8, 8, 6], cols=P, rhs="conv")] * DT,
           dict(evac=lambda x, mm: plan.add("evac_res", "x", m=x, j=mm.j, done=done_of(mm))))


def plan_second():
    plan = Plan()
    tile = dict(kt=[DT], cols=P)
    plan.add("norm", "n:8", gain=("mix", 0), version=0)

    def ssm_input(x, mm):
        plan.add("evac_u", "eu", m=x, j=mm.j, done=mm.c)
        if x < 5:
            plan.add(f"s5_params{x}")

    linear(plan, [dict(tile, rhs="u")] * DT, dict(stat="0", evac=ssm_input))
    for x in range(PAIRS + 6):
        if x < PAIRS:
            plan.add("s5_table", "tb", p=x)
        if 1 <= x <= PAIRS:
            plan.add("s5_rot", "ro", p=x - 1)
        if 2 <= x <= PAIRS + 1:
            plan.add("s5_scan", "sn", p=x - 2)
        if 3 <= x <= PAIRS + 2:
            plan.add("s5_out", "so", p=x - 3)
        if x >= 7 and (x - 3) % 4 == 0:
            plan.add("s5_gelu0", "", m=(x - 7) // 4)
        if x >= 8 and (x - 4) % 4 == 0:
            plan.add("s5_gelu1", "", m=(x - 8) // 4)
        if x >= 9 and (x - 5) % 4 == 0:
            plan.add("s5_gelu2", "", m=(x - 9) // 4)

    def glu(x, mm):
        if x % 2 == 0:
            plan.add("evac_glu_gate", "gg", m=x // 2, j=mm.j, done=mm.c)
        else:
            plan.add("evac_glu", "x", m=x // 2, j=mm.j, done=mm.c)

    linear(plan, [dict(tile, rhs="s5")] * (2 * DT), dict(evac=glu))
    conv_ffn_steps(plan, 0, 1)
    plan.add("norm", "n:8", gain=("kv", 0), version=2)

    turns = {}

    def keys_and_values(x, mm):
        plan.add("evac_k2" if x < DT else "evac_v2", "kv", m=x % DT, j=mm.j, done=mm.c)
        turns[x] = mm.j
        if x > DT:
            plan.add("v2_turn", "v2", m=x - 1 - DT, kv=x - 1, j=turns[x - 1])

    linear(plan, [dict(tile, rhs="u")] * (2 * DT), dict(stat="2", evac=keys_and_values))
    plan.add("v2_turn", "v2", m=DT - 1, kv=2 * DT - 1, j=turns[2 * DT - 1])
    plan.add("regain", "n:8", gain=("mix", 1))
    linear(plan, [dict(tile, rhs="u")] * DT,
           dict(evac=lambda x, mm: plan.add("evac_q2", "q2", m=x, j=mm.j, done=mm.c)))
    for x in range(H2 + 2):
        if x < H2:
            plan.add("sb_scores", "z", h=x)
        if 1 <= x <= H2:
            plan.add("sb_weights", "sums", h=x - 1)
        if x >= 2:
            plan.add("sb_out", "o", h=x - 2)
    linear(plan, [dict(tile, rhs="y2")] * DT,
           dict(evac=lambda x, mm: plan.add("evac_res", "x", m=x, j=mm.j, done=mm.c)))
    conv_ffn_steps(plan, 1, 3)
    plan.add("final", "s:8 g", version=4)
    return plan


LAYER, SECOND = plan_layer(), plan_second()
for st in LAYER.steps:
    if st.kind == "evac_ff" and st.group is not None:
        last_s = st.s
    if st.kind == "post":
        st.last_s = last_s
last_use = None
for st in SECOND.steps:
    if st.kind in ("norm", "regain"):
        st.last_use = last_use
    elif st.kind == "mm" and st.rhs in ("u", "s5"):
        last_use = done_of(st)
assert LAYER.total["c"] == CHUNKS_L and LAYER.total["c"] + CHUNKS_L + SECOND.total["c"] == CHUNKS


def words(step):
    if step.kind == "mla_mm":
        return [CQT * QK + CKT * P]
    return [k * step.cols for k in step.kt]


LAYER_WORDS = [w for s in LAYER.steps if s.kind in ("mm", "mla_mm") for w in words(s)] + [SLOT]
SECOND_WORDS = [w for s in SECOND.steps if s.kind == "mm" for w in words(s)] + [0]

COL = [0, SEQ, 2 * SEQ, SEQ + 3 * P]
WIDE = [SEQ - P * k for k in range(KT)]
LAST_PV = [t for t in LAYER.steps if t.kind == "PV"][-1]

G_BIAS = 32
G_Q, G_K, G_CQ, G_CKV = 48, 49, 50, 53
N_LAYER_PARAMS = 55
S_GAIN = {("mix", 0): 0, ("mix", 1): 8, ("ffn", 0): 16, ("ffn", 1): 24, ("kv", 0): 32, ("final", 0): 40}
S_D, S_CONV, S_A = 48, 56, 56 + 2 * C_TILES * 4
N_SECOND_PARAMS = S_A + 3 * PAIRS
MATS = ("ident", "ones", "ones_head", "rot_a", "rot_b", "neg_tri", "neg_ones", "mask")


def build(nc, weights, x, layer_params, second_params, mats, tables, steps_t, s5_b, s5_c, out):
    ctx = ExitStack()
    with ctx:
        KB = 1024
        start = 16640
        fence = ctx.enter_context(nc.sbuf_tensor("fence", [P, 53120], F32))

        def at(name, kb, shape, dt=F32):
            return nc.alloc_sbuf_tensor_at(name, shape, dt, offset=start + int(kb * KB))

        X = at("X", 0, [P, DT, SEQ])
        RSTD = at("RSTD", 16, [P, SEQ])
        RAWW = at("RAWW", 18, [P, RAW, SLOT])
        WH = at("WH", 34, [P, CUT, SLOT], F32R)
        WL = at("WL", 42, [P, CUT, SLOT], F32R)
        UH = at("UH", 50, [P, DT, SEQ], F32R)
        UL = at("UL", 66, [P, DT, SEQ], F32R)
        PHH = at("PHH", 50, [P, 2, KT, SEQ], F32R)
        PHL = at("PHL", 66, [P, 2, KT, SEQ], F32R)
        FF = at("FF", 82, [P, DT, SEQ])
        TMP = at("TMP", 98, [P, 4, SEQ])
        A0 = 106
        QH = at("QH", A0, [P, QT, SEQ], F32R)
        QL = at("QL", A0 + 8, [P, QT, SEQ], F32R)
        KH = at("KH", A0 + 16, [P, SEQ], F32R)
        KL = at("KL", A0 + 18, [P, SEQ], F32R)
        VH = at("VH", A0 + 20, [P, KT, P], F32R)
        VL = at("VL", A0 + 22, [P, KT, P], F32R)
        CH = at("CH", A0 + 24, [P, CQT + CKT, SEQ], F32R)
        CL = at("CL", A0 + 34, [P, CQT + CKT, SEQ], F32R)
        MQH = at("MQH", A0 + 44, [P, 2, SEQ], F32R)
        MQL = at("MQL", A0 + 48, [P, 2, SEQ], F32R)
        MKH = at("MKH", A0 + 52, [P, 2, SEQ], F32R)
        MKL = at("MKL", A0 + 56, [P, 2, SEQ], F32R)
        MVH = at("MVH", A0 + 60, [P, 2, KT, P], F32R)
        MVL = at("MVL", A0 + 64, [P, 2, KT, P], F32R)
        YBH = at("YBH", A0 + 68, [P, QT, SEQ], F32R)
        YBL = at("YBL", A0 + 76, [P, QT, SEQ], F32R)
        RH = at("RH", A0 + 84, [P, SEQ], F32R)
        RL = at("RL", A0 + 86, [P, SEQ], F32R)
        RKV = at("RKV", A0 + 88, [P, SEQ])
        RCQ = at("RCQ", A0 + 90, [P, SEQ])
        KVF = at("KVF", A0 + 92, [P, 2, SEQ])
        MH = at("MH", A0 + 24, [P, DT, SEQ], F32R)
        ML = at("ML", A0 + 40, [P, DT, SEQ], F32R)
        HH = at("HH", A0, [P, HALF, SEQ], F32R)
        HL = at("HL", A0 + 32, [P, HALF, SEQ], F32R)
        CHH = at("CHH", A0, [P, C_TILES, SEQ], F32R)
        CHL = at("CHL", A0 + 44, [P, C_TILES, SEQ], F32R)
        GATE = at("GATE", 82, [P, 2, 520])
        S5U = at("S5U", A0, [P, DT, SEQ])
        BBT = at("BBT", A0 + 16, [P, 2, DT, P])
        S5C = at("S5C", A0 + 24, [P, 3, PAIRS, 32])
        S5A = at("S5A", A0 + 36, [P, 24, PAIRS])
        S5AR = at("S5AR", A0 + 39, [P, PAIRS], F32R)
        S5B = at("S5B", A0 + 44, [P, 2, PAIRS, 32])
        S5BB = at("S5BB", A0 + 52, [P, 2, PAIRS, 32])
        S5BT = at("S5BT", A0 + 60, [P, 2, PAIRS, 32])
        S5T = at("S5T", A0 + 44, [P, 26, SEQ])
        K2H = at("K2H", A0, [P, DT, SEQ], F32R)
        K2L = at("K2L", A0 + 16, [P, DT, SEQ], F32R)
        V2H = at("V2H", A0 + 32, [P, KT, DM], F32R)
        V2L = at("V2L", A0 + 48, [P, KT, DM], F32R)
        Q2H = at("Q2H", A0 + 64, [P, DT, SEQ], F32R)
        Q2L = at("Q2L", A0 + 80, [P, DT, SEQ], F32R)
        TRI = SEQ * (KT + 1) * KT // 2 // KT
        SPH = at("SPH", 50, [P, TRI], F32R)
        SPL = at("SPL", 55, [P, TRI], F32R)
        WTH = at("WTH", 60, [P, TRI], F32R)
        WTL = at("WTL", 65, [P, TRI], F32R)
        SBZ = at("SBZ", 82, [P, TRI])
        SBS = at("SBS", 87, [P, TRI])
        SBW = at("SBW", 92, [P, TRI])
        MAT = at("MAT", 202, [P, 3, P])
        MATR = at("MATR", 203.5, [P, 4, P], F32R)
        LP = at("LP", 205.5, [P, N_LAYER_PARAMS])
        MASK = at("MASK", 207.1875, [P, P])
        STAT = at("STAT", 205.8125, [P, 3, 4])
        SP_ = at("SP_", 205.875, [P, N_SECOND_PARAMS])
        IDENT, ONES, ONES_HEAD = (MAT[:, k, :] for k in range(3))
        ROT_A, ROT_B, NEG_TRI, NEG_ONES = (MATR[:, k, :] for k in range(4))

        BANK = [ctx.enter_context(nc.psum_tensor(f"bank{k}", [P, SEQ], F32)) for k in range(8)]
        TURN = BANK[7]

        def stat_bank(g):
            return BANK[6 if g % 2 == 0 else 3]

        def signal(name, kind, slots=0):
            return Signal(ctx.enter_context(nc.semaphore(name)), LAYER.total.get(kind, 0), slots)

        raw_in = [ctx.enter_context(nc.semaphore(f"raw_in{k}")) for k in range(RAW)]
        hi = signal("hi", "c")
        lo = signal("lo", "c", RAW)
        used = signal("used", "c", CUT)
        bank_free = signal("bank_free", "j", 2)
        x_in, par_in, mat_in, tab_in, s5_in, y_out = (ctx.enter_context(nc.semaphore(k)) for k in (
            "x_in", "par_in", "mat_in", "tab_in", "s5_in", "y_out"))
        mats_cut = ctx.enter_context(nc.semaphore("mats_cut"))
        mv_zero = ctx.enter_context(nc.semaphore("mv_zero"))
        x_done = signal("x_done", "x", DT)
        uh, ul = signal("uh", "n"), signal("ul", "n")
        sq = signal("sq", "s")
        summed = signal("summed", "s", 2)
        logged, rstd = signal("logged", "g"), signal("rstd", "g")
        scaled = signal("scaled", "sc")
        turned_in = signal("turned_in", "qk")
        rh, rl, rcos, rdone = signal("rh", "rot"), signal("rl", "rot"), signal("rcos", "rot"), signal("rdone", "rot")
        rot_h, rot_l = signal("rot_h", "rot"), signal("rot_l", "rot")
        turn, turn_free = signal("turn", "b"), signal("turn_free", "b", 1)
        v_h, c_h, c_l = signal("v_h", "vh"), signal("c_h", "cn"), signal("c_l", "cn")
        mk_h, mk_l = signal("mk_h", "mk"), signal("mk_l", "mk")
        scores, row_max = signal("scores", "u"), signal("row_max", "u")
        expd, recip = signal("expd", "u", 2), signal("recip", "u")
        normed, probs_t = signal("normed", "u"), signal("probs_t", "u", 4)
        probs_h, probs_l = signal("probs_h", "u"), signal("probs_l", "u", 2)
        y_h = signal("y_h", "pv")
        gate = signal("gate", "ge")
        merged, merged_h, merged_l = (signal(k, "mt") for k in ("merged", "merged_h", "merged_l"))
        hid_h, hid_f, hid_l = (signal(k, "up") for k in ("hid_h", "hid_f", "hid_l"))
        cgx, cge = signal("cgx", ""), signal("cge", "")
        ct, chh, chl = (signal(k, "") for k in ("ct", "chh", "chl"))
        eu = signal("eu", "")
        sp_pool, sp_act, sp_dve, sp_pe = (signal(k, "") for k in ("sp_pool", "sp_act", "sp_dve", "sp_pe"))
        tb, tba, ro_pe, ro, ro_sum, sn, sn_q, so, ys = (signal(k, "") for k in (
            "tb", "tba", "ro_pe", "ro", "ro_sum", "sn", "sn_q", "so", "ys"))
        ge_q, ge_l, v2_l = (signal(k, "") for k in ("ge_q", "ge_l", "v2_l"))
        ge_a, ge_p, ge_h = (signal(k, "") for k in ("ge_a", "ge_p", "ge_h"))
        gge = signal("gge", "")
        kv_x, kv_h, kv_l, v2_pe, v2_h = (signal(k, "") for k in ("kv_x", "kv_h", "kv_l", "v2_pe", "v2_h"))
        q2_x, q2_h, q2_l = (signal(k, "") for k in ("q2_x", "q2_h", "q2_l"))
        z, za, ze, zl, zs, z_h, z_l = (signal(k, "") for k in ("z", "za", "ze", "zl", "zs", "z_h", "z_l"))
        w, we, w_h, w_l = (signal(k, "") for k in ("w", "we", "w_h", "w_l"))
        o, o_h, o_l = (signal(k, "") for k in ("o", "o_h", "o_l"))
        outs = signal("outs", "")

        def rotation_ready(l, st):
            if st.what in "qk":
                return turned_in.sem, turned_in.after(l, st.qk)
            return bank_free.sem, bank_free.after(l, st.j)

        def f32(ap):
            return ap.bitcast(F32)

        def slot_words(ap, slot, n):
            return ap[:, slot, 0:n]

        def s5a(k):
            return S5A[:, k, :]

        block = ctx.enter_context(nc.Block())

        @block.sync
        def _(sp):
            sp.dma_start(MAT[:], mats[:, 0:3 * P].rearrange("p (k n) -> p k n", k=3)).then_inc(mat_in, 16)
            sp.dma_start(FF[:, 0, 0:4 * P], mats[:, 3 * P:7 * P]).then_inc(mat_in, 16)
            sp.dma_start(MASK[:], mats[:, 7 * P:8 * P]).then_inc(mat_in, 16)
            sp.dma_start(SP_[:], second_params).then_inc(mat_in, 16)
            for k in range(DT):
                sp.dma_start(X[:, k, :], x[k]).then_inc(x_in, 16)
            with sp.Fori(0, CHUNKS // RAW) as it:
                for k in range(RAW):
                    sp.wait_ge(lo.sem, it * RAW + (k + 1))
                    sp.dma_start(RAWW[:, k, :], weights[bass.ds(it * RAW + k, 1)].rearrange("a p n -> (a p) n")
                                 ).then_inc(raw_in[k], 16)
            for k in range(DT):
                sp.wait_ge(outs.sem, k + 1)
                sp.dma_start(out[k], FF[:, k, :]).then_inc(y_out, 16)
            sp.wait_ge(y_out, 16 * DT)

        @block.gpsimd
        def _(pool):
            def layer_inputs(l):
                pool.wait_ge(x_done.sem, x_done.room(l, DT - 1))
                pool.wait_ge(mats_cut, 1)
                pool.dma_start(LP[:, 0:N_LAYER_PARAMS], layer_params[bass.ds(l, 1)].rearrange("a p n -> (a p) n")
                               ).then_inc(par_in, 16)
                pool.dma_start(FF[:, 0:4, :], tables.rearrange("k p n -> p k n")).then_inc(tab_in, 16)
                for k in range(2):
                    for v in (MVH, MVL):
                        ins = pool.memset(f32(v[:, k, :, HD - k * HD:P - k * HD]), 0.0)
                ins.then_inc(mv_zero, 1)

            def step(l, st):
                if st.kind == "rope":
                    pool.wait_ge(*rotation_ready(l, st))
                    if st.rot == 0:
                        pool.wait_ge(tab_in, l * 16 + 16)
                    cos = 0 if st.what in "qk" else 2
                    pool.tensor_tensor(FF[0:st.rows, 4 + st.rot % 2, :], FF[0:st.rows, 6 + st.rot % 2, :],
                                       FF[0:st.rows, cos, :], ALU.mult).then_inc(rcos.sem, 1)
                elif st.kind == "N":
                    pool.wait_ge(recip.sem, recip.after(l, st.u))
                    pool.tensor_tensor(TMP[:, st.u % 4, :], TMP[:, st.u % 4, :],
                                       STAT[:, 2, st.u % 4:st.u % 4 + 1].to_broadcast([P, SEQ]), ALU.mult
                                       ).then_inc(normed.sem, 1)
                elif st.kind == "evac_br_b":
                    pool.wait_ge(bank_free.sem, bank_free.after(l, st.j))
                    pool.tensor_tensor(FF[:, 4 + st.m % 2, :], FF[:, 4 + st.m % 2, :], FF[:, 6 + st.m % 2, :],
                                       ALU.add).then_inc(merged.sem, 1)
                elif st.kind == "evac_up":
                    pool.wait_ge(bank_free.sem, bank_free.after(l, st.j))
                    pool.tensor_tensor(TMP[:, st.m % 2, :], TMP[:, 2 + st.m % 2, :], TMP[:, 2 + st.m % 2, :],
                                       ALU.mult).then_inc(hid_f.sem, 1)
                    pool.wait_ge(hid_f.sem, hid_f.after(l, st.up))
                    pool.wait_ge(hid_h.sem, hid_h.after(l, st.up))
                    pool.tensor_tensor(HL[:, st.m, :], TMP[:, st.m % 2, :], f32(HH[:, st.m, :]),
                                       ALU.subtract).then_inc(hid_l.sem, 1)

            def second_block():
                (A_RE, A_IM, LDT) = (SP_[:, S_A + k * PAIRS:S_A + (k + 1) * PAIRS] for k in range(3))
                n = [0]

                def chain(ins):
                    ins.then_inc(sp_pool.sem, 1)
                    n[0] += 1
                    pool.wait_ge(sp_pool.sem, n[0])

                def tt(out_, a, b, op):
                    chain(pool.tensor_tensor(out_, a, b, op))

                def ts(out_, a, s1, s2, op0, op1=None):
                    if op1 is None:
                        chain(pool.tensor_scalar(out_, a, s1, None, op0))
                    else:
                        chain(pool.tensor_scalar(out_, a, s1, s2, op0, op1))

                def wide(k):
                    return s5a(k).unsqueeze(2).to_broadcast([P, PAIRS, 32])

                for st in SECOND.steps:
                    if st.kind == "s5_params0":
                        pool.wait_ge(x_done.sem, x_done.room(2, DT - 1))
                        pool.dma_start(S5B[:], s5_b.rearrange("k p (j h) -> p k j h", h=32)).then_inc(s5_in, 16)
                        pool.dma_start(S5C[:, 0:2], s5_c.rearrange("k p (j h) -> p k j h", h=32)).then_inc(s5_in, 16)
                        pool.dma_start(TMP[:, 2, :], steps_t).then_inc(s5_in, 16)
                        pool.wait_ge(sp_act.sem, 1)
                        tt(s5a(1), A_RE, s5a(0), ALU.mult)
                        tt(s5a(2), A_IM, s5a(0), ALU.mult)
                    elif st.kind == "s5_params1":
                        ts(s5a(3), s5a(2), INV2PI, MAGIC, ALU.mult, ALU.add)
                        ts(s5a(3), s5a(3), MAGIC, None, ALU.subtract)
                        for part in (PI_A, PI_B, PI_C):
                            ts(s5a(4), s5a(3), part, None, ALU.mult)
                            tt(s5a(2), s5a(2), s5a(4), ALU.subtract)
                        ts(s5a(2), s5a(2), 3.1415925, -3.1415925, ALU.min, ALU.max)
                        ts(s5a(5), s5a(2), INV2PI, None, ALU.mult)
                    elif st.kind == "s5_params2":
                        pool.wait_ge(sp_act.sem, 6)
                        tt(s5a(6), s5a(5), f32(S5AR[:]), ALU.subtract)
                        tt(s5a(11), s5a(7), s5a(10), ALU.mult)
                        tt(s5a(12), s5a(7), s5a(8), ALU.mult)
                        tt(s5a(13), A_RE, A_RE, ALU.mult)
                        tt(s5a(14), A_IM, A_IM, ALU.mult)
                        tt(s5a(13), s5a(13), s5a(14), ALU.add)
                        ts(s5a(11), s5a(11), 1.0, None, ALU.subtract)
                        tt(s5a(15), s5a(11), A_RE, ALU.mult)
                        tt(s5a(16), s5a(12), A_IM, ALU.mult)
                        tt(s5a(15), s5a(15), s5a(16), ALU.add)
                        tt(s5a(16), s5a(12), A_RE, ALU.mult)
                        tt(s5a(17), s5a(11), A_IM, ALU.mult)
                        tt(s5a(16), s5a(16), s5a(17), ALU.subtract)
                    elif st.kind == "s5_params3":
                        pool.wait_ge(sp_dve.sem, 1)
                        tt(s5a(15), s5a(15), s5a(18), ALU.mult)
                        tt(s5a(16), s5a(16), s5a(18), ALU.mult)
                        pool.wait_ge(s5_in, 48)
                        tt(S5BB[:, 0], S5B[:, 0], wide(15), ALU.mult)
                        tt(S5BB[:, 1], S5B[:, 1], wide(15), ALU.mult)
                        tt(S5BT[:, 0], S5B[:, 1], wide(16), ALU.mult)
                        tt(S5BT[:, 1], S5B[:, 0], wide(16), ALU.mult)
                        tt(S5BB[:, 0], S5BB[:, 0], S5BT[:, 0], ALU.subtract)
                        tt(S5BB[:, 1], S5BB[:, 1], S5BT[:, 1], ALU.add)
                        ts(S5C[:, 2], S5C[:, 1], -1.0, None, ALU.mult)
                    elif st.kind == "s5_rot":
                        pool.wait_ge(ro.sem, ro.after(2, 4 * st.p + 3))
                        a = [S5T[:, 4 * (st.p % 3) + k, :] for k in range(4)]
                        pool.tensor_tensor(a[0], a[0], a[1], ALU.add).then_inc(ro_sum.sem, 1)
                        pool.tensor_tensor(a[2], a[3], a[2], ALU.subtract).then_inc(ro_sum.sem, 1)
                    elif st.kind == "s5_scan":
                        pool.wait_ge(sn.sem, sn.after(2, 2 * st.p + 1))
                        a = [S5T[:, 4 * (st.p % 3) + k, :] for k in range(4)]
                        r = [S5T[:, 12 + 2 * (st.p % 2) + k, :] for k in range(2)]
                        c, s = (S5T[:, 16 + 2 * (st.p % 3) + k, :] for k in range(2))
                        pool.tensor_tensor(a[0], r[0], c, ALU.mult).then_inc(sn_q.sem, 1)
                        pool.tensor_tensor(a[1], r[1], s, ALU.mult).then_inc(sn_q.sem, 1)
                    elif st.kind == "s5_gelu0":
                        f = [FF[:, 4 * (st.m % 2) + k, :] for k in range(4)]
                        pool.wait_ge(ge_a.sem, ge_a.after(2, 2 * st.m))
                        pool.tensor_scalar(f[1], f[1], 0.044715, 1.0, ALU.mult, ALU.add).then_inc(ge_p.sem, 1)
                        pool.wait_ge(ge_p.sem, ge_p.after(2, 3 * st.m))
                        pool.tensor_tensor(f[1], f[1], f[0], ALU.mult).then_inc(ge_p.sem, 1)
                        pool.wait_ge(ge_a.sem, ge_a.after(2, 2 * st.m + 1))
                        pool.tensor_tensor(f[3], f[0], f[2], ALU.mult).then_inc(ge_p.sem, 1)
                    elif st.kind == "evac_cup":
                        u = (FF[:, 7, :], TMP[:, 2, :])[st.m % 2]
                        pool.wait_ge(bank_free.sem, bank_free.after(2, st.j))
                        pool.wait_ge(cge.sem, cge.after(2, st.cu))
                        pool.tensor_tensor(u, u, FF[:, 5 + st.m % 2, :], ALU.mult).then_inc(ct.sem, 1)
                        pool.wait_ge(chh.sem, chh.after(2, st.cu))
                        pool.tensor_tensor(CHL[:, st.m, :], u, f32(CHH[:, st.m, :]), ALU.subtract).then_inc(chl.sem, 1)

            with pool.Fori(0, LAYERS) as l:
                layer_inputs(l)
                for st in LAYER.steps:
                    step(l, st)
            second_block()

        def pv_place(h):
            if h < HEADS:
                a = h // QT * HD
                return QH, QL, slice(a, a + HD), h % QT
            m = h - HEADS
            return YBH, YBL, slice(m % 2 * HD, m % 2 * HD + HD), m // 2

        def small_input(st):
            k = st.i if st.kind == "evac_cq" else CQT + st.i
            return k, LP[:, G_CQ + k:G_CQ + k + 1]

        def rot_dest(st):
            if st.what == "q":
                return [(QH[:, st.i, :], QL[:, st.i, :])], slice(0, P)
            if st.what == "k":
                return [(KH[:], KL[:])], slice(0, P)
            if st.what == "mla":
                return [(MQH[0:QK, st.h % 2, :], MQL[0:QK, st.h % 2, :])], slice(0, QK)
            return [(MKH[HD:QK, k, :], MKL[HD:QK, k, :]) for k in range(2)], slice(HD, QK)

        @block.scalar
        def _(act):
            def cut_next(l, st, sizes):
                for n in range(len(st.kt)):
                    c = st.c + n + 1
                    if sizes[c]:
                        cut(l, c, sizes[c])

            def cut(l, c, size):
                act.wait_ge(raw_in[c % RAW], l * (CHUNKS_L // RAW * 16) + 16 * (c // RAW + 1))
                act.wait_ge(used.sem, used.room(l, c))
                act.activation(slot_words(WH, c % CUT, size), slot_words(RAWW, c % RAW, size), ACT.Copy
                               ).then_inc(hi.sem, 1)

            def square(l, s, src):
                act.wait_ge(summed.sem, summed.room(l, s))
                act.activation(TMP[0:src.shape[0], s % 2, :], src, ACT.Square).then_inc(sq.sem, 1)

            def factor(l, g, last_s, dst, scale, bias):
                act.wait_ge(summed.sem, summed.after(l, last_s))
                act.activation(dst, stat_bank(g)[:], ACT.Ln, bias=bias, scale=scale).then_inc(logged.sem, 1)
                act.wait_ge(logged.sem, logged.after(l, g))
                act.activation(dst, dst, ACT.Exp, scale=-0.5).then_inc(rstd.sem, 1)

            def gains(l, st, gain):
                for k in range(DT):
                    act.activation(UH[:, k, :], X[:, k, :], ACT.Copy, scale=gain[:, k:k + 1]).then_inc(uh.sem, 1)

            def norm(l, st, gain):
                for k in range(DT):
                    act.wait_ge(x_done.sem, x_done.room(l, DT * st.version + k))
                    act.activation(UH[:, k, :], X[:, k, :], ACT.Copy, scale=gain[:, k:k + 1]).then_inc(uh.sem, 1)

            def squares_of_x(l, st):
                for k in range(DT):
                    act.wait_ge(x_done.sem, x_done.room(l, DT * int(st.version) + k))
                    square(l, st.s + k, X[:, k, :])
                factor(l, st.g, st.s + DT - 1, RSTD[:], 1.0 / DM, EPS)

            def step(l, st):
                kind = st.kind
                if kind in ("mm", "mla_mm"):
                    cut_next(l, st, LAYER_WORDS)
                elif kind == "norm":
                    if st.gain == 0:
                        act.wait_ge(par_in, l * 16 + 16)
                    norm(l, st, LP[:, st.gain:st.gain + DT])
                elif kind == "stat":
                    squares_of_x(l, st)
                elif kind == "regain":
                    gains(l, st, LP[:, st.gain:st.gain + DT])
                elif kind in ("evac_q", "evac_k"):
                    act.wait_ge(bank_free.sem, bank_free.after(l, st.j))
                    square(l, st.s, TMP[:, 2 + st.x % 2, :])
                elif kind in ("evac_cq", "evac_ckv"):
                    k, gain = small_input(st)
                    act.wait_ge(bank_free.sem, bank_free.after(l, st.j))
                    act.activation(CH[:, k, :], TMP[:, 2 + st.x % 2, :], ACT.Copy, scale=gain).then_inc(c_h.sem, 1)
                    square(l, st.s, TMP[:, 2 + st.x % 2, :])
                elif kind == "rc_cq":
                    factor(l, st.g, st.s, RCQ[:], 1.0 / Q_RANK, EPS)
                elif kind == "rc_ckv":
                    factor(l, st.g, st.s, RKV[:], 1.0 / KV_RANK, EPS)
                elif kind == "rope":
                    if st.what == "q":
                        factor(l, st.g, st.s, FF[:, 4 + st.rot % 2, :], 1.0, HD * EPS)
                    elif st.what == "k":
                        factor(l, st.g, st.s, FF[:, 4 + st.rot % 2, :], 1.0 / HD, EPS)
                    act.wait_ge(*rotation_ready(l, st))
                    act.activation(RH[0:st.rows, :], FF[0:st.rows, 6 + st.rot % 2, :], ACT.Copy).then_inc(rh.sem, 1)
                    dests, rows = rot_dest(st)
                    act.wait_ge(rdone.sem, rdone.after(l, st.rot))
                    for n, (h, _) in enumerate(dests):
                        ins = act.activation(h, FF[rows, 6 + st.rot % 2, :], ACT.Copy)
                    ins.then_inc(rot_h.sem, 1)
                elif kind == "gqa_v":
                    act.wait_ge(turn.sem, turn.after(l, st.b))
                    act.activation(VH[:].rearrange("p k n -> p (k n)"), TURN[:], ACT.Copy).then_inc(v_h.sem, 1)
                elif kind == "mla_v":
                    act.wait_ge(bank_free.sem, bank_free.after(l, st.j + 1))
                    act.activation(MKH[0:HD, st.h % 2, :], KVF[0:HD, st.h % 2, :], ACT.Copy).then_inc(mk_h.sem, 1)
                    act.wait_ge(turn.sem, turn.after(l, st.b))
                    a = st.h % 2 * HD
                    act.activation(MVH[:, st.h % 2, :, a:a + HD], TURN[:].rearrange("p (k n) -> p k n", k=KT)[:, :, HD:P],
                                   ACT.Copy).then_inc(v_h.sem, 1)
                elif kind == "S":
                    act.wait_ge(row_max.sem, row_max.after(l, st.u))
                    act.wait_ge(probs_t.sem, probs_t.room(l, st.u))
                    r = st.u % 4
                    act.activation(TMP[:, r, :], BANK[2 + st.u % 2][:], ACT.Exp, bias=STAT[:, 0, r:r + 1],
                                   accum_out=STAT[:, 1, r:r + 1]).then_inc(expd.sem, 1)
                elif kind == "T":
                    act.wait_ge(probs_t.sem, probs_t.after(l, st.u))
                    act.activation(PHH[:, st.h % 2, :, st.t * P:(st.t + 1) * P],
                                   BANK[4 + st.u % 2][:].rearrange("p (k q) -> p k q", k=KT), ACT.Copy
                                   ).then_inc(probs_h.sem, 1)
                elif kind == "PV":
                    h, _, rows, k = pv_place(st.h)
                    act.wait_ge(turn.sem, turn.after(l, st.b))
                    act.activation(h[rows, k, :], TURN[rows, :], ACT.Copy).then_inc(y_h.sem, 1)
                elif kind in ("evac_ga", "evac_gb"):
                    b = kind == "evac_gb"
                    t = FF[:, 2 * b + st.m % 2, :]
                    act.wait_ge(bank_free.sem, bank_free.after(l, st.j))
                    bias = G_BIAS + DT * b + st.m
                    act.activation(t, t, ACT.Sigmoid, bias=LP[:, bias:bias + 1]).then_inc(gate.sem, 1)
                elif kind == "merge":
                    act.wait_ge(merged.sem, merged.after(l, st.mg))
                    act.activation(MH[:, st.m, :], FF[:, 4 + st.m % 2, :], ACT.Copy).then_inc(merged_h.sem, 1)
                elif kind == "evac_ff" and st.group is not None:
                    act.wait_ge(bank_free.sem, bank_free.after(l, st.j))
                    square(l, st.s, FF[:, st.m, :])
                elif kind == "post":
                    factor(l, st.g, st.last_s, TMP[:, 2, :], 1.0 / DM, EPS)
                elif kind == "evac_up":
                    act.wait_ge(bank_free.sem, bank_free.after(l, st.j))
                    act.activation(HH[:, st.m, :], TMP[:, 2 + st.m % 2, :], ACT.Square).then_inc(hid_h.sem, 1)

            def second(st):
                kind = st.kind
                copy = ACT.Copy
                if kind == "mm":
                    cut_next(2, st, SECOND_WORDS)
                elif kind in ("norm", "regain"):
                    g = S_GAIN[st.gain]
                    if st.last_use is not None:
                        act.wait_ge(used.sem, used.after(2, st.last_use))
                    (norm if kind == "norm" else gains)(2, st, SP_[:, g:g + DT])
                elif kind == "stat":
                    squares_of_x(2, st)
                elif kind == "s5_params0":
                    act.activation(s5a(0), SP_[:, S_A + 2 * PAIRS:S_A + 3 * PAIRS], ACT.Exp).then_inc(sp_act.sem, 1)
                elif kind == "s5_params1":
                    act.wait_ge(sp_pool.sem, 2)
                    act.activation(s5a(7), s5a(1), ACT.Exp).then_inc(sp_act.sem, 1)
                elif kind == "s5_params2":
                    act.wait_ge(sp_pool.sem, 12)
                    act.activation(s5a(8), s5a(2), ACT.Sin).then_inc(sp_act.sem, 1)
                    act.activation(s5a(9), s5a(2), ACT.Abs).then_inc(sp_act.sem, 1)
                    act.activation(S5AR[:], s5a(5), copy).then_inc(sp_act.sem, 1)
                    act.wait_ge(sp_act.sem, 5)
                    act.activation(s5a(10), s5a(9), ACT.Sin, bias=math.pi / 2, scale=-1.0).then_inc(sp_act.sem, 1)
                elif kind == "s5_params4":
                    for k in range(4):
                        act.wait_ge(sp_pe.sem, k + 1)
                        act.activation(BBT[:, k // 2, 4 * (k % 2):4 * (k % 2) + 4, :].rearrange("p t n -> p (t n)"),
                                       BANK[2 + k][:], copy).then_inc(sp_act.sem, 1)
                elif kind == "s5_table":
                    g, ag = S5T[:, 22 + st.p % 2, :], S5T[:, 24 + st.p % 2, :]
                    c, s = (S5T[:, 16 + 2 * (st.p % 3) + k, :] for k in range(2))
                    act.wait_ge(tb.sem, tb.after(2, 5 * st.p + 4))
                    if st.p >= 3:
                        act.wait_ge(sn_q.sem, sn_q.after(2, 2 * (st.p - 3) + 1))
                        act.wait_ge(ge_q.sem, ge_q.after(2, 2 * (st.p - 3) + 1))
                    act.activation(ag, g, ACT.Abs).then_inc(tba.sem, 1)
                    act.activation(s, g, ACT.Sin, scale=2.0 * math.pi).then_inc(tba.sem, 1)
                    act.wait_ge(tba.sem, tba.after(2, 3 * st.p))
                    act.activation(c, ag, ACT.Sin, bias=math.pi / 2, scale=-2.0 * math.pi).then_inc(tba.sem, 1)
                elif kind == "s5_gelu0":
                    f = [FF[:, 4 * (st.m % 2) + k, :] for k in range(4)]
                    act.wait_ge(ys.sem, ys.after(2, st.m))
                    act.activation(f[1], f[0], ACT.Square).then_inc(ge_a.sem, 1)
                    act.wait_ge(ge_p.sem, ge_p.after(2, 3 * st.m + 1))
                    act.activation(f[2], f[1], ACT.Sigmoid, scale=2.0 * math.sqrt(2.0 / math.pi)).then_inc(ge_a.sem, 1)
                elif kind == "s5_gelu1":
                    act.wait_ge(ge_p.sem, ge_p.after(2, 3 * st.m + 2))
                    act.activation(UH[:, st.m, :], FF[:, 4 * (st.m % 2) + 3, :], copy).then_inc(ge_h.sem, 1)
                elif kind == "evac_glu_gate":
                    t = FF[:, st.m % 2, :]
                    act.wait_ge(bank_free.sem, bank_free.after(2, st.j))
                    act.activation(t, t, ACT.Sigmoid).then_inc(gge.sem, 1)
                elif kind == "evac_gate":
                    act.wait_ge(cgx.sem, cgx.after(2, 3 * st.cg + 2))
                    if st.cg >= 2:
                        act.wait_ge(ct.sem, ct.after(2, st.cg - 2))
                    act.activation(FF[:, 5 + st.m % 2, :], FF[:, 3 + st.m % 2, :], ACT.Silu).then_inc(cge.sem, 1)
                elif kind == "evac_cup":
                    act.wait_ge(ct.sem, ct.after(2, st.cu))
                    act.activation(CHH[:, st.m, :], (FF[:, 7, :], TMP[:, 2, :])[st.m % 2], copy).then_inc(chh.sem, 1)
                elif kind == "evac_k2":
                    act.wait_ge(bank_free.sem, bank_free.after(2, st.j))
                    act.activation(K2H[:, st.m, :], TMP[:, 2 + st.kv % 2, :], copy).then_inc(kv_h.sem, 1)
                elif kind == "v2_turn":
                    act.wait_ge(v2_pe.sem, v2_pe.after(2, st.v2))
                    act.activation(V2H[:, :, st.m * P:(st.m + 1) * P], BANK[2 + st.m % 2][:].rearrange("p (k n) -> p k n", k=KT),
                                   copy).then_inc(v2_h.sem, 1)
                elif kind == "evac_q2":
                    act.wait_ge(bank_free.sem, bank_free.after(2, st.j))
                    act.activation(Q2H[:, st.m, :], TMP[:, 2 + st.m % 2, :], copy).then_inc(q2_h.sem, 1)
                elif kind == "sb_scores":
                    act.wait_ge(z.sem, z.after(2, st.h))
                    for k, n in enumerate((SEQ, SEQ, SEQ // 2)):
                        act.activation(SBZ[:, SEQ * k:SEQ * k + n], BANK[3 * (st.h % 2) + k][:, 0:n], ACT.Abs).then_inc(za.sem, 1)
                    act.wait_ge(za.sem, za.after(2, 3 * st.h + 2))
                    act.activation(SBZ[:], SBZ[:], ACT.Exp, scale=-1.0).then_inc(ze.sem, 1)
                    act.wait_ge(ze.sem, ze.after(2, st.h))
                    act.activation(SBZ[:], SBZ[:], ACT.Ln, bias=1.0).then_inc(zl.sem, 1)
                    act.wait_ge(zs.sem, zs.after(2, st.h))
                    if st.h:
                        act.wait_ge(w.sem, w.after(2, st.h - 1))
                    act.activation(SPH[:], SBS[:], copy).then_inc(z_h.sem, 1)
                elif kind == "sb_weights":
                    act.wait_ge(w.sem, w.after(2, st.h))
                    if st.h:
                        act.wait_ge(w_l.sem, w_l.after(2, st.h - 1))
                    for k, n in enumerate((SEQ, SEQ, SEQ // 2)):
                        ins = act.activation(SBW[:, SEQ * k:SEQ * k + n], BANK[3 * (st.h % 2) + k][:, 0:n], ACT.Exp)
                    ins.then_inc(we.sem, 1)
                    act.wait_ge(we.sem, we.after(2, st.h))
                    if st.h:
                        act.wait_ge(o.sem, o.after(2, st.h - 1))
                    act.activation(WTH[:], SBW[:], copy).then_inc(w_h.sem, 1)
                elif kind == "sb_out":
                    rows = slice(st.h % 2 * HD, st.h % 2 * HD + HD)
                    act.wait_ge(o.sem, o.after(2, st.h))
                    act.activation(Q2H[rows, st.h // 2, :], BANK[6 + st.h % 2][rows, :], copy).then_inc(o_h.sem, 1)
                elif kind == "final":
                    squares_of_x(2, st)

            act.wait_ge(mat_in, 64)
            act.activation(MATR[:].rearrange("p k n -> p (k n)"), FF[:, 0, 0:4 * P], ACT.Copy).then_inc(mats_cut, 1)
            act.sem_inc(expd.sem, 2)
            cut(0, 0, SLOT)
            with act.Fori(0, LAYERS) as l:
                for st in LAYER.steps:
                    step(l, st)
            for st in SECOND.steps:
                second(st)

        @block.vector
        def _(dve):
            def cut_next(l, st, sizes):
                for n in range(len(st.kt)):
                    c = st.c + n + 1
                    if sizes[c]:
                        cut(l, c, sizes[c])

            def cut(l, c, size):
                dve.wait_ge(hi.sem, hi.after(l, c))
                dve.tensor_tensor(slot_words(WL, c % CUT, size), slot_words(RAWW, c % RAW, size),
                                  f32(slot_words(WH, c % CUT, size)), ALU.subtract).then_inc(lo.sem, 1)

            def rest(dst, src, h):
                return dve.tensor_tensor(dst, src, f32(h), ALU.subtract)

            def gained_rest(l, st, gain):
                for k in range(DT):
                    dve.wait_ge(uh.sem, uh.after(l, st.n + k))
                    dve.scalar_tensor_tensor(UL[:, k, :], X[:, k, :], gain[:, k:k + 1], f32(UH[:, k, :]),
                                             ALU.mult, ALU.subtract).then_inc(ul.sem, 1)

            def from_bank(l, st):
                dve.wait_ge(used.sem, used.after(l, st.done))
                return BANK[st.j % 2]

            def times_rstd(l, st, dst, rows=P):
                b = from_bank(l, st)
                return dve.tensor_tensor(dst, b[0:rows, :], RSTD[0:rows, :], ALU.mult).then_inc(bank_free.sem, 1)

            def step(l, st):
                kind = st.kind
                if kind in ("mm", "mla_mm"):
                    cut_next(l, st, LAYER_WORDS)
                elif kind in ("norm", "regain"):
                    gained_rest(l, st, LP[:, st.gain:st.gain + DT])
                elif kind == "stat":
                    dve.wait_ge(rstd.sem, rstd.after(l, st.g))
                elif kind in ("evac_q", "evac_k", "evac_v"):
                    times_rstd(l, st, TMP[:, 2 + st.x % 2, :])
                elif kind in ("evac_cq", "evac_ckv"):
                    t = TMP[:, 2 + st.x % 2, :]
                    times_rstd(l, st, t)
                    k, gain = small_input(st)
                    dve.wait_ge(c_h.sem, c_h.after(l, st.cn))
                    dve.wait_ge(bank_free.sem, bank_free.after(l, st.j))
                    dve.scalar_tensor_tensor(CL[:, k, :], t, gain, f32(CH[:, k, :]), ALU.mult, ALU.subtract
                                             ).then_inc(c_l.sem, 1)
                elif kind == "evac_kr":
                    b = from_bank(l, st)
                    dve.tensor_tensor(FF[0:QK, 6 + st.rot % 2, :], b[0:QK, :], RSTD[0:QK, :], ALU.mult
                                      ).then_inc(bank_free.sem, 1)
                elif kind == "mla_evac":
                    dve.wait_ge(used.sem, used.after(l, st.done))
                    if st.h == 0:
                        dve.wait_ge(rstd.sem, rstd.after(l, RC_LAST))
                    dve.scalar_tensor_tensor(FF[0:QK, 6 + st.rot % 2, :], BANK[st.j % 2][0:QK, :], QK ** -0.5, RCQ[0:QK, :],
                                             ALU.mult, ALU.mult).then_inc(bank_free.sem, 1)
                    dve.tensor_tensor(KVF[:, st.h % 2, :], BANK[(st.j + 1) % 2][:], RKV[:], ALU.mult
                                      ).then_inc(bank_free.sem, 1)
                elif kind == "rope":
                    r, rows = st.rot, slice(0, st.rows)
                    src, a = FF[rows, 6 + r % 2, :], FF[rows, 4 + r % 2, :]
                    if st.what in "qk":
                        gain = G_Q if st.what == "q" else G_K
                        dve.wait_ge(rstd.sem, rstd.after(l, st.g))
                        dve.scalar_tensor_tensor(src, TMP[:, 2 + st.x % 2, :], LP[:, gain:gain + 1], a, ALU.mult, ALU.mult
                                                 ).then_inc(turned_in.sem, 1)
                    dve.wait_ge(rh.sem, rh.after(l, r))
                    rest(RL[rows, :], src, RH[rows, :]).then_inc(rl.sem, 1)
                    dve.wait_ge(turn.sem, turn.after(l, st.b))
                    if r == 0:
                        dve.wait_ge(tab_in, l * 16 + 16)
                    sin = FF[rows, 1 if st.what in "qk" else 3, :]
                    b = FF[rows, r % 2, :] if st.what == "mla" else TMP[rows, 2 + st.x % 2, :]
                    dve.tensor_tensor(b, TURN[rows, :], sin, ALU.mult).then_inc(turn_free.sem, 1)
                    dve.wait_ge(rcos.sem, rcos.after(l, r))
                    dve.wait_ge(turn_free.sem, turn_free.after(l, st.b))
                    dve.tensor_tensor(src, a, b, ALU.add).then_inc(rdone.sem, 1)
                    dve.wait_ge(rdone.sem, rdone.after(l, r))
                    dve.wait_ge(rot_h.sem, rot_h.after(l, r))
                    dests, rows = rot_dest(st)
                    for h, lo_ in dests:
                        ins = rest(lo_, FF[rows, 6 + r % 2, :], h)
                    ins.then_inc(rot_l.sem, 1)
                elif kind == "gqa_v":
                    dve.wait_ge(v_h.sem, v_h.after(l, st.vh))
                    rest(VL[:].rearrange("p k n -> p (k n)"), TURN[:], VH[:].rearrange("p k n -> p (k n)")
                         ).then_inc(turn_free.sem, 1)
                elif kind == "mla_v":
                    dve.wait_ge(mk_h.sem, mk_h.after(l, st.mk))
                    rest(MKL[0:HD, st.h % 2, :], KVF[0:HD, st.h % 2, :], MKH[0:HD, st.h % 2, :]).then_inc(mk_l.sem, 1)
                    dve.wait_ge(v_h.sem, v_h.after(l, st.vh))
                    a = st.h % 2 * HD
                    rest(MVL[:, st.h % 2, :, a:a + HD], TURN[:].rearrange("p (k n) -> p k n", k=KT)[:, :, HD:P],
                         MVH[:, st.h % 2, :, a:a + HD]).then_inc(turn_free.sem, 1)
                elif kind == "S":
                    r = st.u % 4
                    dve.wait_ge(scores.sem, scores.after(l, st.u))
                    dve.tensor_reduce(STAT[:, 0, r:r + 1], BANK[2 + st.u % 2][:], AX_X, ALU.max, negate=True
                                      ).then_inc(row_max.sem, 1)
                elif kind == "N":
                    r = st.u % 4
                    dve.wait_ge(expd.sem, expd.after(l, st.u))
                    dve.reciprocal(STAT[:, 2, r:r + 1], STAT[:, 1, r:r + 1]).then_inc(recip.sem, 1)
                elif kind == "T":
                    dve.wait_ge(probs_h.sem, probs_h.after(l, st.u))
                    at_ = (slice(None), st.h % 2, slice(None), slice(st.t * P, (st.t + 1) * P))
                    rest(PHL[at_], BANK[4 + st.u % 2][:].rearrange("p (k q) -> p k q", k=KT), PHH[at_]
                         ).then_inc(probs_l.sem, 1)
                elif kind == "PV":
                    h, lo_, rows, k = pv_place(st.h)
                    dve.wait_ge(y_h.sem, y_h.after(l, st.pv))
                    rest(lo_[rows, k, :], TURN[rows, :], h[rows, k, :]).then_inc(turn_free.sem, 1)
                elif kind in ("evac_ga", "evac_gb"):
                    b = from_bank(l, st)
                    dve.tensor_tensor(FF[:, 2 * (kind == "evac_gb") + st.m % 2, :], b[:], RSTD[:], ALU.mult
                                      ).then_inc(bank_free.sem, 1)
                elif kind in ("evac_br_a", "evac_br_b"):
                    b, n = from_bank(l, st), kind == "evac_br_b"
                    g = FF[:, 2 * n + st.m % 2, :]
                    dve.wait_ge(gate.sem, gate.after(l, 2 * st.m + n))
                    dve.tensor_tensor(FF[:, 4 + 2 * n + st.m % 2, :], b[:], g, ALU.mult).then_inc(bank_free.sem, 1)
                elif kind == "merge":
                    dve.wait_ge(merged_h.sem, merged_h.after(l, st.mg))
                    rest(ML[:, st.m, :], FF[:, 4 + st.m % 2, :], MH[:, st.m, :]).then_inc(merged_l.sem, 1)
                elif kind == "evac_ff":
                    b = from_bank(l, st)
                    if st.add:
                        dve.tensor_tensor(FF[:, st.m, :], b[:], FF[:, st.m, :], ALU.add).then_inc(bank_free.sem, 1)
                    else:
                        dve.tensor_copy(FF[:, st.m, :], b[:]).then_inc(bank_free.sem, 1)
                elif kind == "post":
                    dve.wait_ge(rstd.sem, rstd.after(l, st.g))
                    for k in range(DT):
                        dve.tensor_tensor(FF[:, k, :], FF[:, k, :], TMP[:, 2, :], ALU.mult).then_inc(scaled.sem, 1)
                    for k in range(DT):
                        dve.wait_ge(scaled.sem, scaled.after(l, st.sc + k))
                        dve.scalar_tensor_tensor(X[:, k, :], FF[:, k, :], LP[:, st.gain + k:st.gain + k + 1], X[:, k, :],
                                                 ALU.mult, ALU.add).then_inc(x_done.sem, 1)
                elif kind == "evac_up":
                    b = from_bank(l, st)
                    t = TMP[:, 2 + st.m % 2, :]
                    if st.up >= 2:
                        dve.wait_ge(hid_f.sem, hid_f.after(l, st.up - 2))
                        dve.wait_ge(hid_h.sem, hid_h.after(l, st.up - 2))
                    dve.scalar_tensor_tensor(t, b[:], 0.0, RSTD[:], ALU.max, ALU.mult).then_inc(bank_free.sem, 1)

            def second(st):
                kind = st.kind
                if kind == "mm":
                    cut_next(2, st, SECOND_WORDS)
                elif kind in ("norm", "regain"):
                    g = S_GAIN[st.gain]
                    gained_rest(2, st, SP_[:, g:g + DT])
                elif kind == "stat":
                    dve.wait_ge(rstd.sem, rstd.after(2, st.g))
                elif kind == "evac_u":
                    times_rstd(2, st, S5U[:, st.m, :])
                elif kind == "s5_params2":
                    dve.wait_ge(sp_pool.sem, 18)
                    dve.reciprocal(s5a(18), s5a(13)).then_inc(sp_dve.sem, 1)
                elif kind == "s5_table":
                    t, g = TMP[:, 2, :], S5T[:, 22 + st.p % 2, :]
                    k, kh, kl = (a[:, st.p:st.p + 1] for a in (s5a(5), f32(S5AR[:]), s5a(6)))
                    if st.p == 0:
                        dve.wait_ge(s5_in, 48)
                        dve.wait_ge(sp_pool.sem, 34)
                        dve.wait_ge(sp_act.sem, 10)
                    if st.p >= 2:
                        dve.wait_ge(tba.sem, tba.after(2, 3 * (st.p - 2) + 2))
                    m = S5T[:, 24 + st.p % 2, :]
                    dve.tensor_scalar(m, t, k, MAGIC, ALU.mult, ALU.add).then_inc(tb.sem, 1)
                    dve.wait_ge(tb.sem, tb.after(2, 5 * st.p))
                    dve.tensor_scalar(m, m, MAGIC, None, ALU.subtract).then_inc(tb.sem, 1)
                    dve.wait_ge(tb.sem, tb.after(2, 5 * st.p + 1))
                    dve.scalar_tensor_tensor(g, t, kh, m, ALU.mult, ALU.subtract).then_inc(tb.sem, 1)
                    dve.wait_ge(tb.sem, tb.after(2, 5 * st.p + 2))
                    dve.scalar_tensor_tensor(g, t, kl, g, ALU.mult, ALU.add).then_inc(tb.sem, 1)
                    dve.wait_ge(tb.sem, tb.after(2, 5 * st.p + 3))
                    dve.tensor_scalar(g, g, 0.5, -0.5, ALU.min, ALU.max).then_inc(tb.sem, 1)
                elif kind == "s5_rot":
                    a = [S5T[:, 4 * (st.p % 3) + k, :] for k in range(4)]
                    c, s = (S5T[:, 16 + 2 * (st.p % 3) + k, :] for k in range(2))
                    re, im = (BANK[2 + 2 * (st.p % 2) + k][:] for k in range(2))
                    dve.wait_ge(tba.sem, tba.after(2, 3 * st.p + 2))
                    dve.wait_ge(ro_pe.sem, ro_pe.after(2, st.p))
                    if st.p >= 3:
                        dve.wait_ge(so.sem, so.after(2, st.p - 3))
                    for k, (b, v) in enumerate(((re, c), (im, s), (im, c), (re, s))):
                        dve.tensor_tensor(a[k], b, v, ALU.mult).then_inc(ro.sem, 1)
                elif kind == "s5_scan":
                    a = [S5T[:, 4 * (st.p % 3) + k, :] for k in range(4)]
                    r = [S5T[:, 12 + 2 * (st.p % 2) + k, :] for k in range(2)]
                    c, s = (S5T[:, 16 + 2 * (st.p % 3) + k, :] for k in range(2))
                    mag = s5a(7)[:, st.p:st.p + 1].to_broadcast([P, SEQ])
                    if st.p >= 2:
                        dve.wait_ge(sn_q.sem, sn_q.after(2, 2 * (st.p - 2) + 1))
                    for k in range(2):
                        dve.wait_ge(ro_sum.sem, ro_sum.after(2, 2 * st.p + k))
                        dve.tensor_tensor_scan(r[k], mag, a[2 * k], 0.0, ALU.mult, ALU.add).then_inc(sn.sem, 1)
                    dve.wait_ge(sn.sem, sn.after(2, 2 * st.p + 1))
                    dve.tensor_tensor(a[2], r[0], s, ALU.mult).then_inc(ge_q.sem, 1)
                    dve.tensor_tensor(a[3], r[1], c, ALU.mult).then_inc(ge_q.sem, 1)
                elif kind == "s5_gelu0":
                    dve.wait_ge(so.sem, so.after(2, 4 * st.m + 3))
                    dve.scalar_tensor_tensor(FF[:, 4 * (st.m % 2), :], S5U[:, st.m, :], SP_[:, S_D + st.m:S_D + st.m + 1],
                                             BANK[6 + st.m % 2][:], ALU.mult, ALU.add).then_inc(ys.sem, 1)
                elif kind == "s5_gelu2":
                    dve.wait_ge(ge_h.sem, ge_h.after(2, st.m))
                    rest(UL[:, st.m, :], FF[:, 4 * (st.m % 2) + 3, :], UH[:, st.m, :]).then_inc(ge_l.sem, 1)
                elif kind == "evac_glu_gate":
                    b = from_bank(2, st)
                    dve.tensor_copy(FF[:, st.m % 2, :], b[:]).then_inc(bank_free.sem, 1)
                elif kind == "evac_glu":
                    b, t = from_bank(2, st), FF[:, st.m % 2, :]
                    dve.wait_ge(gge.sem, gge.after(2, st.m))
                    dve.tensor_tensor(t, b[:], t, ALU.mult).then_inc(bank_free.sem, 1)
                    dve.wait_ge(bank_free.sem, bank_free.after(2, st.j))
                    dve.tensor_tensor(X[:, st.m, :], X[:, st.m, :], t, ALU.add).then_inc(x_done.sem, 1)
                elif kind == "evac_gate":
                    g, t = GATE[:, st.m % 2, :], FF[:, 3 + st.m % 2, :]
                    w_ = [SP_[:, S_CONV + (st.layer * C_TILES + st.m) * 4 + k:][:, 0:1] for k in range(4)]
                    if st.m < 2:
                        dve.memset(g[:, 0:2], 0.0)
                    times_rstd(2, st, g[:, 2:2 + SEQ])
                    dve.wait_ge(bank_free.sem, bank_free.after(2, st.j))
                    if st.cg >= 2:
                        dve.wait_ge(cge.sem, cge.after(2, st.cg - 2))
                    dve.tensor_scalar(t, g[:, 2:2 + SEQ], w_[2], w_[3], ALU.mult, ALU.add).then_inc(cgx.sem, 1)
                    dve.wait_ge(cgx.sem, cgx.after(2, 3 * st.cg))
                    dve.scalar_tensor_tensor(t, g[:, 1:1 + SEQ], w_[1], t, ALU.mult, ALU.add).then_inc(cgx.sem, 1)
                    dve.wait_ge(cgx.sem, cgx.after(2, 3 * st.cg + 1))
                    dve.scalar_tensor_tensor(t, g[:, 0:SEQ], w_[0], t, ALU.mult, ALU.add).then_inc(cgx.sem, 1)
                elif kind == "evac_cup":
                    u = (FF[:, 7, :], TMP[:, 2, :])[st.m % 2]
                    if st.cu >= 2:
                        dve.wait_ge(chl.sem, chl.after(2, st.cu - 2))
                    times_rstd(2, st, u)
                elif kind == "evac_res":
                    b = from_bank(2, st)
                    dve.tensor_tensor(X[:, st.m, :], b[:], X[:, st.m, :], ALU.add).then_inc(x_done.sem, 1)
                    dve.wait_ge(x_done.sem, x_done.after(2, st.x))
                    dve.sem_inc(bank_free.sem, 1)
                elif kind in ("evac_k2", "evac_v2"):
                    if 2 <= st.kv < DT + 2:
                        dve.wait_ge(kv_l.sem, kv_l.after(2, st.kv - 2))
                    elif st.kv >= DT + 2:
                        dve.wait_ge(v2_pe.sem, v2_pe.after(2, st.kv - 2 - DT))
                    times_rstd(2, st, TMP[:, 2 + st.kv % 2, :])
                    if kind == "evac_k2":
                        dve.wait_ge(kv_h.sem, kv_h.after(2, st.m))
                        rest(K2L[:, st.m, :], TMP[:, 2 + st.kv % 2, :], K2H[:, st.m, :]).then_inc(kv_l.sem, 1)
                elif kind == "v2_turn":
                    dst = (slice(None), slice(None), slice(st.m * P, (st.m + 1) * P))
                    dve.wait_ge(v2_h.sem, v2_h.after(2, st.v2))
                    rest(V2L[dst], BANK[2 + st.m % 2][:].rearrange("p (k n) -> p k n", k=KT), V2H[dst]).then_inc(v2_l.sem, 1)
                elif kind == "evac_q2":
                    b, t = from_bank(2, st), TMP[:, 2 + st.m % 2, :]
                    if st.q2 >= 2:
                        dve.wait_ge(q2_l.sem, q2_l.after(2, st.q2 - 2))
                    else:
                        dve.wait_ge(v2_pe.sem, v2_pe.after(2, DT - 2 + st.q2))
                    dve.scalar_tensor_tensor(t, b[:], HD ** -0.5, RSTD[:], ALU.mult, ALU.mult).then_inc(bank_free.sem, 1)
                    dve.wait_ge(q2_h.sem, q2_h.after(2, st.q2))
                    rest(Q2L[:, st.m, :], t, Q2H[:, st.m, :]).then_inc(q2_l.sem, 1)
                elif kind == "sb_scores":
                    pieces = [(slice(SEQ * k, SEQ * k + n), BANK[3 * (st.h % 2) + k][:, 0:n])
                              for k, n in enumerate((SEQ, SEQ, SEQ // 2))]
                    dve.wait_ge(zl.sem, zl.after(2, st.h))
                    if st.h:
                        dve.wait_ge(z_l.sem, z_l.after(2, st.h - 1))
                    for k, (cols, b) in enumerate(pieces):
                        ins = dve.scalar_tensor_tensor(SBS[:, cols], b, 0.0, SBZ[:, cols], ALU.max, ALU.add)
                    ins.then_inc(zs.sem, 1)
                    dve.wait_ge(z_h.sem, z_h.after(2, st.h))
                    rest(SPL[:], SBS[:], SPH[:]).then_inc(z_l.sem, 1)
                elif kind == "sb_weights":
                    dve.wait_ge(w_h.sem, w_h.after(2, st.h))
                    rest(WTL[:], SBW[:], WTH[:]).then_inc(w_l.sem, 1)
                elif kind == "sb_out":
                    rows = slice(st.h % 2 * HD, st.h % 2 * HD + HD)
                    dve.wait_ge(o_h.sem, o_h.after(2, st.h))
                    rest(Q2L[rows, st.h // 2, :], BANK[6 + st.h % 2][rows, :], Q2H[rows, st.h // 2, :]).then_inc(o_l.sem, 1)
                elif kind == "final":
                    g = S_GAIN["final", 0]
                    dve.wait_ge(rstd.sem, rstd.after(2, st.g))
                    for k in range(DT):
                        dve.scalar_tensor_tensor(FF[:, k, :], X[:, k, :], SP_[:, g + k:g + k + 1], RSTD[:], ALU.mult, ALU.mult
                                                 ).then_inc(outs.sem, 1)

            dve.sem_inc(lo.sem, RAW)
            dve.sem_inc(bank_free.sem, 2)
            dve.sem_inc(turn_free.sem, 1)
            dve.sem_inc(probs_l.sem, 2)
            dve.wait_ge(x_in, 16 * DT)
            dve.sem_inc(x_done.sem, DT)
            cut(0, 0, SLOT)
            with dve.Fori(0, LAYERS) as l:
                for st in LAYER.steps:
                    step(l, st)
            for st in SECOND.steps:
                second(st)

        @block.tensor
        def _(pe):
            def product(out_, w, x_, start, stop, **how):
                nc.tensor.matmul(out_, w[0], x_[0], start=start, stop=False, **how)
                nc.tensor.matmul(out_, w[0], x_[1], start=False, stop=False, **how)
                return nc.tensor.matmul(out_, w[1], x_[0], start=False, stop=stop, **how)

            inputs = {"u": (UH, UL), "merged": (MH, ML), "ya": (QH, QL), "yb": (YBH, YBL), "hidden": (HH, HL),
                      "s5": (UH, UL), "conv": (CHH, CHL), "y2": (Q2H, Q2L)}

            def linear_job(l, st, ready):
                xh, xl = inputs[st.rhs]
                pe.wait_ge(bank_free.sem, bank_free.room(l, st.j))
                n = len(st.kt)
                k0 = 0
                for i, kt in enumerate(st.kt):
                    c = st.c + i
                    pe.wait_ge(lo.sem, lo.after(l, c))
                    for k in range(kt):
                        if st.first:
                            pe.wait_ge(*ready(k0 + k))
                        cols = slice(k * st.cols, (k + 1) * st.cols)
                        ins = product(BANK[st.j % 2][0:st.cols, :], (WH[:, c % CUT, cols], WL[:, c % CUT, cols]),
                                      (xh[:, k0 + k, :], xl[:, k0 + k, :]), k0 + k == 0, i == n - 1 and k == kt - 1)
                    ins.then_inc(used.sem, 1)
                    k0 += kt

            def small_job(l, j, c, at_, kt, cols, k0):
                pe.wait_ge(bank_free.sem, bank_free.room(l, j))
                for k in range(kt):
                    w_ = slice(at_ + k * cols, at_ + (k + 1) * cols)
                    ins = product(BANK[j % 2][0:cols, :], (WH[:, c % CUT, w_], WL[:, c % CUT, w_]),
                                  (CH[:, k0 + k, :], CL[:, k0 + k, :]), k == 0, k == kt - 1)
                return ins

            def add_square(l, s, g, ones, first, last):
                if first and g >= 2:
                    pe.wait_ge(logged.sem, logged.after(l, g - 2))
                pe.wait_ge(sq.sem, sq.after(l, s))
                nc.tensor.matmul(stat_bank(g)[:], ones, TMP[:, s % 2, :], start=first, stop=last).then_inc(summed.sem, 1)

            state = {}

            def step(l, st):
                kind = st.kind
                if kind in ("norm", "regain"):
                    state["n"] = st.n
                elif kind == "mm":
                    n = state["n"]
                    ready = {"u": lambda k: (ul.sem, ul.after(l, n + k)),
                             "merged": lambda k: (merged_l.sem, merged_l.after(l, k)),
                             "ya": lambda k: (turn_free.sem, turn_free.after(l, LAST_PV.b)),
                             "yb": lambda k: (turn_free.sem, turn_free.after(l, LAST_PV.b)),
                             "hidden": lambda k: (hid_l.sem, hid_l.after(l, state["up"] - HALF + 1 + k))}[st.rhs]
                    linear_job(l, st, ready)
                elif kind == "evac_up":
                    state["up"] = st.up
                elif kind == "stat":
                    for k in range(DT):
                        add_square(l, st.s + k, st.g, ONES, k == 0, k == DT - 1)
                elif kind in ("evac_q", "evac_k"):
                    add_square(l, st.s, st.group, ONES_HEAD, True, True)
                elif kind in ("evac_cq", "evac_ckv"):
                    add_square(l, st.s, st.group, ONES, st.i == 0, st.i == (CQT if kind == "evac_cq" else CKT) - 1)
                elif kind == "evac_ff" and st.group is not None:
                    add_square(l, st.s, st.group, ONES, st.m == 0, st.m == DT - 1)
                elif kind == "rope":
                    rot = ROT_A if st.what in "qk" else ROT_B
                    rows = slice(0, st.rows)
                    pe.wait_ge(rl.sem, rl.after(l, st.rot))
                    pe.wait_ge(turn_free.sem, turn_free.room(l, st.b))
                    nc.tensor.matmul(TURN[rows, :], rot[rows, rows], RH[rows, :], start=True, stop=False)
                    nc.tensor.matmul(TURN[rows, :], rot[rows, rows], RL[rows, :], start=False, stop=True
                                     ).then_inc(turn.sem, 1)
                elif kind == "gqa_v":
                    pe.wait_ge(bank_free.sem, bank_free.after(l, st.j))
                    pe.wait_ge(turn_free.sem, turn_free.room(l, st.b))
                    for k in range(KT):
                        ins = nc.tensor.transpose(TURN[:, k * P:(k + 1) * P], TMP[:, 2 + st.x % 2, k * P:(k + 1) * P], IDENT)
                    ins.then_inc(turn.sem, 1)
                elif kind == "mla_mm":
                    pe.wait_ge(lo.sem, lo.after(l, st.c))
                    if st.h == 0:
                        pe.wait_ge(c_l.sem, c_l.after(l, CQT + CKT - 1))
                    small_job(l, st.j, st.c, 0, CQT, QK, 0)
                    small_job(l, st.j + 1, st.c, CQT * QK, CKT, P, CQT).then_inc(used.sem, 1)
                elif kind == "mla_v":
                    pe.wait_ge(bank_free.sem, bank_free.after(l, st.j + 1))
                    pe.wait_ge(turn_free.sem, turn_free.room(l, st.b))
                    for k in range(KT):
                        ins = nc.tensor.transpose(TURN[:, k * P:(k + 1) * P], KVF[:, st.h % 2, k * P:(k + 1) * P], IDENT)
                    ins.then_inc(turn.sem, 1)
                elif kind == "S":
                    q = slice(st.t * P, (st.t + 1) * P)
                    if st.u == 0:
                        pe.wait_ge(rot_l.sem, rot_l.after(l, QT))
                        pe.wait_ge(logged.sem, logged.after(l, RC_LAST))
                    if st.h >= HEADS and st.t == 0:
                        pe.wait_ge(rot_l.sem, rot_l.after(l, QT + 2 + st.h - HEADS))
                        pe.wait_ge(mk_l.sem, mk_l.after(l, st.h - HEADS))
                    pe.wait_ge(expd.sem, expd.room(l, st.u))
                    if st.h < HEADS:
                        rows, i = slice(st.h // QT * HD, st.h // QT * HD + HD), st.h % QT
                        qs = QH[rows, i, q], QL[rows, i, q]
                        ks = KH[rows, :], KL[rows, :]
                    else:
                        i = st.h % 2
                        qs = MQH[0:QK, i, q], MQL[0:QK, i, q]
                        ks = MKH[0:QK, i, :], MKL[0:QK, i, :]
                    product(BANK[2 + st.u % 2][:], qs, ks, True, True).then_inc(scores.sem, 1)
                elif kind == "T":
                    pe.wait_ge(normed.sem, normed.after(l, st.u))
                    pe.wait_ge(probs_l.sem, probs_l.room(l, st.u))
                    for k in range(KT):
                        ins = nc.tensor.transpose(BANK[4 + st.u % 2][:, k * P:(k + 1) * P],
                                                  TMP[:, st.u % 4, k * P:(k + 1) * P], IDENT)
                    ins.then_inc(probs_t.sem, 1)
                elif kind == "PV":
                    pe.wait_ge(probs_l.sem, probs_l.after(l, KT * st.h + KT - 1))
                    pe.wait_ge(turn_free.sem, turn_free.room(l, st.b))
                    if st.h == HEADS:
                        pe.wait_ge(mv_zero, l + 1)
                    for k in range(KT):
                        v = (VH[:, k, :], VL[:, k, :]) if st.h < HEADS else (MVH[:, st.h % 2, k, :], MVL[:, st.h % 2, k, :])
                        ins = product(TURN[:], v, (PHH[:, st.h % 2, k, :], PHL[:, st.h % 2, k, :]), k == 0, k == KT - 1)
                    ins.then_inc(turn.sem, 1)

            def second_pe(st):
                kind = st.kind
                if kind in ("norm", "regain"):
                    state["n"] = st.n
                elif kind == "mm":
                    n = state["n"]
                    ready = {"u": lambda k: (ul.sem, ul.after(2, n + k)),
                             "s5": lambda k: (ge_l.sem, ge_l.after(2, k)),
                             "conv": lambda k: (chl.sem, chl.after(2, state["cu"] - C_TILES + 1 + k)),
                             "y2": lambda k: (o_l.sem, o_l.after(2, 2 * k + 1))}[st.rhs]
                    linear_job(2, st, ready)
                    state["j"] = st.j
                elif kind == "evac_cup":
                    state["cu"] = st.cu
                elif kind in ("stat", "final"):
                    for k in range(DT):
                        add_square(2, st.s + k, st.g, ONES, k == 0, k == DT - 1)
                elif kind == "s5_params3":
                    pe.wait_ge(sp_pool.sem, 34)
                    for k in range(4):
                        for t in range(4):
                            j = 4 * (4 * (k % 2) + t)
                            ins = nc.tensor.transpose(BANK[2 + k][:, t * P:(t + 1) * P],
                                                      S5BB[:, k // 2, j:j + 4, :].rearrange("p j h -> p (j h)"), IDENT)
                        ins.then_inc(sp_pe.sem, 1)
                elif kind == "s5_table":
                    rows = slice(32 * (st.p % 4), 32 * (st.p % 4) + 32)
                    if st.p == 0:
                        pe.wait_ge(sp_act.sem, 10)
                        pe.wait_ge(bank_free.sem, bank_free.after(2, DT - 1))
                    if st.p >= 2:
                        pe.wait_ge(ro.sem, ro.after(2, 4 * (st.p - 2) + 3))
                    for k in range(2):
                        ins = nc.tensor.matmul(BANK[2 + 2 * (st.p % 2) + k][:], BBT[rows, k, st.p // 4, :], S5U[rows, st.p // 4, :],
                                               start=True, stop=True)
                    ins.then_inc(ro_pe.sem, 1)
                elif kind == "s5_out":
                    rows = slice(32 * (st.p % 4), 32 * (st.p % 4) + 32)
                    t = st.p // 4
                    a = [S5T[:, 4 * (st.p % 3) + k, :] for k in range(4)]
                    if st.p % 4 == 0 and t >= 2:
                        pe.wait_ge(ys.sem, ys.after(2, t - 2))
                    pe.wait_ge(sn_q.sem, sn_q.after(2, 2 * st.p + 1))
                    pe.wait_ge(ge_q.sem, ge_q.after(2, 2 * st.p + 1))
                    for n, (k, part) in enumerate(((0, 0), (1, 0), (2, 2), (3, 1))):
                        ins = nc.tensor.matmul(BANK[6 + t % 2][rows, :], S5C[:, part, st.p, :], a[k],
                                               start=n == 0, stop=n == 3)
                    ins.then_inc(so.sem, 1)
                elif kind == "v2_turn":
                    pe.wait_ge(bank_free.sem, bank_free.after(2, st.j))
                    if st.m >= 2:
                        pe.wait_ge(v2_l.sem, v2_l.after(2, st.m - 2))
                    for k in range(KT):
                        ins = nc.tensor.transpose(BANK[2 + st.m % 2][:, k * P:(k + 1) * P],
                                                  TMP[:, 2 + st.kv % 2, k * P:(k + 1) * P], IDENT)
                    ins.then_inc(v2_pe.sem, 1)
                elif kind == "sb_scores":
                    rows = slice(st.h % 2 * HD, st.h % 2 * HD + HD)
                    i = st.h // 2
                    if st.h == 0:
                        pe.wait_ge(bank_free.sem, bank_free.after(2, state["j"]))
                        pe.wait_ge(v2_l.sem, v2_l.after(2, DT - 1))
                    pe.wait_ge(q2_l.sem, q2_l.after(2, i))
                    if st.h >= 2:
                        pe.wait_ge(we.sem, we.after(2, st.h - 2))
                    for k in (0, 1, 3, 2):
                        b, c = divmod(COL[k], SEQ)
                        product(BANK[3 * (st.h % 2) + b][:, c:c + WIDE[k]],
                                (K2H[rows, i, k * P:(k + 1) * P], K2L[rows, i, k * P:(k + 1) * P]),
                                (Q2H[rows, i, k * P:], Q2L[rows, i, k * P:]), k != 3, False, skip_group_check=True)
                        ins = nc.tensor.matmul(BANK[3 * (st.h % 2) + b][:, c:c + P], IDENT, MASK[:], start=False, stop=False,
                                               skip_group_check=True)
                    ins.then_inc(z.sem, 1)
                elif kind == "sb_weights":
                    pe.wait_ge(z_l.sem, z_l.after(2, st.h))
                    for k in range(KT):
                        b, c = divmod(COL[k], SEQ)
                        for k2 in range(k, KT):
                            mat = NEG_TRI if k2 == k else NEG_ONES
                            d = c + (k2 - k) * P
                            for part in (SPH, SPL):
                                ins = nc.tensor.matmul(BANK[3 * (st.h % 2) + b][:, d:d + WIDE[k2]], mat,
                                                       part[:, COL[k2]:COL[k2] + WIDE[k2]], start=False, stop=False,
                                                       skip_group_check=True)
                    ins.then_inc(w.sem, 1)
                elif kind == "sb_out":
                    pe.wait_ge(w_l.sem, w_l.after(2, st.h))
                    if st.h >= 2:
                        pe.wait_ge(o_l.sem, o_l.after(2, st.h - 2))
                    i = st.h // 2
                    for k in range(KT):
                        cols = slice(COL[k], COL[k] + WIDE[k])
                        ins = product(BANK[6 + st.h % 2][:, k * P:], (V2H[:, k, i * P:(i + 1) * P], V2L[:, k, i * P:(i + 1) * P]),
                                      (WTH[:, cols], WTL[:, cols]), k == 0, k == KT - 1, skip_group_check=True)
                    ins.then_inc(o.sem, 1)
            pe.wait_ge(mat_in, 64)
            pe.wait_ge(mats_cut, 1)
            pe.sem_inc(used.sem, CUT)
            pe.sem_inc(summed.sem, 2)
            pe.sem_inc(probs_t.sem, 4)
            with pe.Fori(0, LAYERS) as l:
                for st in LAYER.steps:
                    step(l, st)
            for st in SECOND.steps:
                second_pe(st)


def packed(w, k0, kt, c0, cols, rows=None):
    part = w[k0 * P:(k0 + kt) * P] if rows is None else w[rows]
    return part[:, c0:c0 + cols].reshape(kt, P, cols).transpose(1, 0, 2).reshape(P, kt * cols)


def weight_stream(w):
    chunks = []

    def whole(matrix, c0, n, cols=P):
        for m in range(n):
            chunks.append(packed(matrix, 0, matrix.shape[0] // P, c0 + m * cols, cols))

    paired = np.concatenate([np.arange(h * HD, h * HD + HD) for i in range(QT) for h in (i, QT + i)])
    for l in range(LAYERS):
        w_in = w["w_in"][l]
        q_pairs = w_in[:, paired]
        whole(q_pairs, 0, QT)
        kv0 = HEADS * HD
        low0 = kv0 + 2 * KV_HEADS * HD
        rope0 = low0 + Q_RANK + KV_RANK
        gate0 = rope0 + ROPE
        whole(w_in, kv0, 2)
        whole(w_in, low0, CQT + CKT)
        whole(w_in, rope0 - HD, 1, QK)
        for h in range(HEADS):
            chunks.append(np.concatenate([packed(w["w_q_up"][l], 0, CQT, h * QK, QK),
                                          packed(w["w_kv_up"][l], 0, CKT, h * P, P)], axis=1))
        for m in range(DT):
            whole(w_in, gate0 + m * P, 1)
            whole(w_in, gate0 + DM + m * P, 1)
            chunks.append(packed(w["w_branch_a"][l], 0, QT, m * P, P, rows=paired))
            chunks.append(packed(w["w_branch_b"][l], 0, QT, m * P, P))
        whole(w["w_o"][l], 0, DT)
        for half in range(2):
            whole(w["w_ffn_up"][l], half * HALF * P, HALF)
            for m in range(DT):
                for k in range(2):
                    chunks.append(packed(w["w_ffn_down"][l], half * HALF + k * DT, DT, m * P, P))

    def conv_ffn(layer):
        up, down = w["ffn_w_up_2"][layer], w["ffn_w_down_2"][layer]
        for m in range(C_TILES):
            whole(up, m * P, 1)
            whole(up, (C_TILES + m) * P, 1)
        for m in range(DT):
            for k0 in range(0, C_TILES, DT):
                chunks.append(packed(down, k0, min(DT, C_TILES - k0), m * P, P))

    whole(w["ssm_w_in_2"][0], 0, DT)
    for m in range(DT):
        whole(w["ssm_w_glu_2"][0], DM + m * P, 1)
        whole(w["ssm_w_glu_2"][0], m * P, 1)
    conv_ffn(0)
    whole(w["kv_w_2"], 0, 2 * DT)
    whole(w["attn_w_q_2"][0], 0, DT)
    whole(w["attn_w_o_2"][0], 0, DT)
    conv_ffn(1)
    stream = np.zeros((CHUNKS, P, SLOT), np.float32)
    assert len(chunks) == CHUNKS
    for c, chunk in enumerate(chunks):
        stream[c, :, :chunk.shape[1]] = chunk
    return stream


def by_tile(v):
    return v.reshape(-1, P).T


def layer_parameters(w):
    rows = []
    for l in range(LAYERS):
        cols = [by_tile(w[k][l]) for k in ("pre_mix_g", "post_mix_g", "pre_ffn_g", "post_ffn_g", "b_gate")]
        cols += [np.tile(w[k][l], 2)[:, None] for k in ("q_norm_g", "k_norm_g")]
        cols += [by_tile(w[k][l]) for k in ("q_a_norm_g", "kv_a_norm_g")]
        rows.append(np.concatenate(cols, axis=1))
    return np.stack(rows)


def by_pair(v):
    return v.reshape(PAIRS, 2 * STATE).T


def second_parameters(w):
    cols = [by_tile(w["norm_mix_2"][0]), by_tile(w["norm_mix_2"][1]), by_tile(w["norm_ffn_2"][0]),
            by_tile(w["norm_ffn_2"][1]), by_tile(w["norm_kv_2"]), by_tile(w["norm_final_2"]),
            by_tile(w["ssm_d_2"][0].reshape(-1))]
    for layer in range(LAYERS):
        taps = [by_tile(w["ffn_conv_w_2"][layer, k, 0]) for k in range(3)] + [by_tile(w["ffn_conv_b_2"][layer])]
        cols.append(np.stack(taps, axis=2).reshape(P, C_TILES * 4))
    cols += [by_pair(w["ssm_a_re_2"][0]), by_pair(w["ssm_a_im_2"][0]),
             by_pair(np.repeat(w["ssm_log_dt_2"][0][:, None], STATE, axis=1))]
    return np.concatenate(cols, axis=1)


def pair_blocks(v):
    wide = np.zeros((2, STATE, PAIRS, 2, GH), np.float32)
    for g in range(2):
        wide[g, :, :, g, :] = v[g::2].transpose(1, 0, 2)
    return wide.reshape(P, PAIRS * 2 * GH)


def rotation(dim, at_):
    m = np.zeros((P, P), np.float32)
    quarter = dim // 4
    for a in at_:
        for half in (a, a + dim // 2):
            for k in range(quarter):
                m[half + quarter + k, half + k] = -1.0
                m[half + k, half + quarter + k] = 1.0
    return m


def angles(dim):
    token = np.arange(SEQ)
    row, col = (token // GRID_W).astype(np.float32), (token % GRID_W).astype(np.float32)
    half = dim // 2
    inv = np.float32(ROPE_THETA) ** (-np.arange(0, half, 2, dtype=np.float32) / np.float32(half))
    ar, ac = row[:, None] * inv[None], col[:, None] * inv[None]
    a = np.concatenate([ar, ar, ac, ac], axis=1).T
    return np.cos(a).astype(np.float32), np.sin(a).astype(np.float32)


def constants():
    eye, ones = np.eye(P, dtype=np.float32), np.ones((P, P), np.float32)
    ones_head = np.kron(np.eye(2, dtype=np.float32), np.ones((HD, HD), np.float32))
    mats = [eye, ones, ones_head, rotation(HD, (0, HD)), rotation(ROPE, (HD,)), -np.tril(ones), -ones,
            HIDDEN * np.tril(ones)]
    cos_a, sin_a = angles(HD)
    tables = np.zeros((4, P, SEQ), np.float32)
    tables[0], tables[1] = np.tile(cos_a, (2, 1)), np.tile(sin_a, (2, 1))
    tables[2] = 1.0
    tables[2, HD:QK], tables[3, HD:QK] = angles(ROPE)
    steps = np.tile(np.arange(SEQ, dtype=np.float32), (P, 1))
    return np.concatenate(mats, axis=1), tables, steps


def kernel(**inputs):
    import concourse.bacc as _bacc
    from concourse.bass_utils import run_bass_kernel_spmd as _run

    w = {name: np.asarray(a) for name, a in inputs.items()}
    mats, tables, steps = constants()
    arrays = {
        "weights": weight_stream(w),
        "x": np.ascontiguousarray(w["x"][0].T).reshape(DT, P, SEQ),
        "layer_params": layer_parameters(w),
        "second_params": second_parameters(w),
        "mats": mats,
        "tables": tables,
        "steps_t": steps,
        "s5_b": np.stack([pair_blocks(w["ssm_b_re_2"][0]), pair_blocks(w["ssm_b_im_2"][0])]),
        "s5_c": np.stack([pair_blocks(w[k][0].transpose(0, 2, 1)) for k in ("ssm_c_re_2", "ssm_c_im_2")]),
    }
    arrays = {name: np.ascontiguousarray(a, dtype=np.float32) for name, a in arrays.items()}
    nc = _bacc.Bacc("TRN2", target_bir_lowering=False, num_devices=1)
    args = {name: nc.dram_tensor(name, a.shape, F32, kind="ExternalInput").ap() for name, a in arrays.items()}
    out = nc.dram_tensor("out", (DT, P, SEQ), F32, kind="ExternalOutput").ap()
    build(nc, out=out, **args)
    r = _run(nc, [arrays], core_ids=[0])
    return np.ascontiguousarray(r.results[0]["out"].reshape(DM, SEQ).T)[None]
```

```python
import math
from contextlib import ExitStack

import numpy as np

import concourse.bass as bass
from concourse import mybir

F32 = mybir.dt.float32
F32R = mybir.dt.float32r
ALU = mybir.AluOpType
ACT = mybir.ActivationFunctionType
AX_X = mybir.AxisListType.X

P = 128
SEQ = 512
DM = 1024
DT = DM // P
LAYERS = 2
EPS = 1e-6
KT = SEQ // P
GRID_W = 64
ROPE_THETA = 10000.0

HEADS = 8
HD = 64
KV_HEADS = 2
QT = HEADS * HD // P
ROPE = 32
QK = HD + ROPE
Q_RANK, KV_RANK = 384, 256
CQT, CKT = Q_RANK // P, KV_RANK // P
FF_TILES = 4096 // P
HALF = FF_TILES // 2
SLOT = 8 * P

C_TILES = 2816 // P
COARSE, FINE = 16, 32
GROUPS, STATE, GH = 64, 64, 16
PAIRS = GROUPS // 2
H2 = 16
HIDDEN = -2.0 ** 100
LOG_EXP = "natural_log_exp_and_others"
MAGIC = 1.5 * 2.0 ** 23
INV2PI = 1.0 / (2.0 * math.pi)
PI_A, PI_B = 6.28125, 0.0019350051879882812
PI_C = 2.0 * math.pi - PI_A - PI_B
CHUNKS_L = 124
CHUNKS = 2 * CHUNKS_L + 192

RAW = 4
CUT = 2


RC_LAST, POST_MIX, POST_FFN = 3 + QT, 4 + QT, 6 + QT


ADDED = 4
NORM = f"n:{DT} f a:{ADDED} s:{DT - 1 - ADDED}"


class Signal:

    def __init__(self, sem, per_layer, slots=0):
        self.sem, self.per_layer, self.slots = sem, per_layer, slots

    def after(self, l, k):
        return l * self.per_layer + (k + 1 + self.slots)

    def room(self, l, k):
        return l * self.per_layer + (k + 1)


class Step:

    def __init__(self, kind, a=None, add=None, b=None, c=None, cg=None, cn=None, cols=None, cu=None, done=None, eu=None,
                 f=None, ff=None, first=None, g=None, gain=None, ge=None, gg=None, group=None, h=None, i=None,
                 j=None, keys=None, kt=None, kv=None, last_a=None, last_f=None, last_s=None, last_use=None,
                 layer=None, m=None, mg=None, mk=None, mt=None, n=None, o=None, p=None, pv=None, q2=None, qk=None,
                 rhs=None, ro=None, rot=None, rows=None, s=None, sc=None, sn=None, so=None, stat=None, sums=None,
                 t=None, tb=None, turn_before=None, u=None, up=None, v2=None, version=None, vh=None, what=None,
                 x=None, z=None):
        self.kind, self.a, self.add, self.b, self.c, self.cg, self.cn, self.cols = kind, a, add, b, c, cg, cn, cols
        self.cu, self.done, self.eu, self.f, self.ff, self.first, self.g, self.gain = cu, done, eu, f, ff, first, g, gain
        self.ge, self.gg, self.group, self.h, self.i, self.j, self.keys, self.kt = ge, gg, group, h, i, j, keys, kt
        self.kv, self.last_a, self.last_f, self.last_s, self.last_use, self.layer, self.m, self.mg = kv, last_a, last_f, last_s, last_use, layer, m, mg
        self.mk, self.mt, self.n, self.o, self.p, self.pv, self.q2, self.qk = mk, mt, n, o, p, pv, q2, qk
        self.rhs, self.ro, self.rot, self.rows, self.s, self.sc, self.sn, self.so = rhs, ro, rot, rows, s, sc, sn, so
        self.stat, self.sums, self.t, self.tb, self.turn_before, self.u, self.up, self.v2 = stat, sums, t, tb, turn_before, u, up, v2
        self.version, self.vh, self.what, self.x, self.z = version, vh, what, x, z


class Plan:

    def __init__(self):
        self.steps, self.total = [], {}

    def add(self, kind, take="", **info):
        at = {}
        for item in take.split():
            name, n = (item.split(":") + ["1"])[:2]
            at[name] = self.total.get(name, 0)
            self.total[name] = at[name] + int(n)
        step = Step(kind, **at, **info)
        self.steps.append(step)
        return step


def linear(plan, jobs, after, lag=1):
    mm = []
    for x in range(len(jobs) + lag):
        if x < len(jobs):
            mm.append(plan.add("mm", f"c:{len(jobs[x]['kt'])} j", first=x == 0, **jobs[x]))
        if x == 0 and after.get("stat"):
            norm = after["stat"]
            plan.add("stat", "g", f=norm.f, a=norm.a, s=norm.s, version=norm.version)
        if x >= lag:
            after["evac"](x - lag, mm[x - lag])


def done_of(mm):
    return mm.c + len(mm.kt) - 1


def attention_steps(plan):
    n = 2 * HEADS * KT
    mm = ev = None
    value_j = {}
    for x in range(n + 8):
        h, phase = divmod(x - KT - 4, KT)
        if 0 <= h < 2 * HEADS and phase == 3:
            plan.add("PV_out", h=h, pv=h)
        m, phase = divmod(x + 2 - (HEADS - 1) * KT, KT)
        if 1 <= m <= HEADS and phase == 1:
            plan.add("turn_out", **rotation)
        if x < n:
            plan.add("S", "u", h=x // KT, t=x % KT)
        if 1 <= x <= n:
            plan.add("N", u=x - 1)
        h, phase = divmod(x - KT - 4, KT)
        if 0 <= h < 2 * HEADS and phase < 3:
            plan.add("PV", "pv" if phase == 2 else "", h=h, keys=((0, 1), (2,), (3,))[phase])
        if 3 <= x <= n + 2:
            plan.add("T", u=x - 3, h=(x - 3) // KT, t=(x - 3) % KT)
        if 4 <= x <= n + 3:
            plan.add("L", u=x - 4, h=(x - 4) // KT, t=(x - 4) % KT)
        m, phase = divmod(x + 2 - (HEADS - 1) * KT, KT)
        if 1 <= m <= HEADS and phase == 0:
            plan.add("turn", "b", **rotation)
        if 0 <= m < HEADS and phase == 0:
            mm = plan.add("mla_mm", "c j:2", h=m, kt=[None])
        if 2 <= m <= HEADS + 1 and phase == 1:
            plan.add("mla_v", "b vh", h=m - 2, j=value_j[m - 2])
        if 0 <= m < HEADS and phase == 1:
            ev = plan.add("mla_evac", "rot mk", h=m, j=mm.j, done=mm.c)
            value_j[m] = mm.j
            rotation = dict(what="mla", h=m, rot=ev.rot, j=ev.j, rows=QK)
        if 0 <= m < HEADS and phase == 2:
            plan.add("turn_in", **rotation)
            plan.add("mla_k", h=m, mk=ev.mk, j=ev.j)

def plan_layer():
    plan = Plan()
    norm = plan.add("norm", NORM, gain=0, version=0)
    items = [("q", i) for i in range(QT)] + [("k", 0), ("v", 0)] + [("cq", i) for i in range(CQT)]
    items += [("ckv", i) for i in range(CKT)] + [("kr", 0)]
    ev = {}

    def first_products(x, mm):
        what, i = items[x]
        take = {"q": "s rot", "k": "s rot", "v": "", "cq": "s cn", "ckv": "s cn", "kr": "rot"}[what]
        group = {"q": 1 + i, "k": 1 + QT, "cq": 2 + QT, "ckv": 3 + QT}.get(what)
        ev[x] = plan.add("evac_" + what, take, i=i, x=x, j=mm.j, done=mm.c, group=group)
        if x >= 2:
            rotate("turn", x - 2)
        if x >= 1:
            finish(x - 1)
        if x >= 2:
            rotate("turn_out", x - 2)

    def rotate(kind, x):
        what, i = items[x]
        if what in ("q", "k", "kr"):
            take = "b" if kind == "turn" else "g qk" if kind == "turn_in" and what != "kr" else ""
            st = plan.add(kind, take, what=what, i=i, x=x, rot=ev[x].rot, s=ev[x].s, j=ev[x].j, h=0,
                          rows=QK if what == "kr" else P)

    def finish(x):
        what, i = items[x]
        rotate("turn_in", x)
        if what == "v":
            plan.add("gqa_v", "b vh", x=x, j=ev[x].j)
        elif (what, i) in (("cq", CQT - 1), ("ckv", CKT - 1)):
            plan.add("rc_" + what, "g", s=ev[x].s)

    jobs = [dict(kt=[DT], cols=QK if what == "kr" else P, rhs="u") for what, _ in items]
    linear(plan, jobs, dict(stat=norm, evac=first_products))
    finish(len(items) - 1)
    rotate("turn", len(items) - 1)
    rotate("turn_out", len(items) - 1)
    attention_steps(plan)
    plan.add("regain", "n:8", gain=0)

    def gates_and_branches(x, mm):
        what, m = ("ga", "gb", "br_a", "br_b")[x % 4], x // 4
        plan.add("evac_" + what, {"ga": "ge", "gb": "ge", "br_b": "mt"}.get(what, ""), m=m, j=mm.j,
                 done=mm.c)
        if what == "gb" and m:
            plan.add("merge", "mg", m=m - 1)

    jobs = []
    for m in range(DT):
        jobs += [dict(kt=[DT], cols=P, rhs="u"), dict(kt=[DT], cols=P, rhs="u"),
                 dict(kt=[QT], cols=P, rhs="ya"), dict(kt=[QT], cols=P, rhs="yb")]
    linear(plan, jobs, dict(evac=gates_and_branches))
    plan.add("merge", "mg", m=DT - 1)

    def into_ff(add, group=None):
        def evac(x, mm):
            take = "" if group is None else "f" if x == 0 else "a" if x < DT - 1 else "s"
            plan.add("evac_ff", "ff " + take, m=x, j=mm.j, done=done_of(mm), add=add, group=group)
        return evac

    tile = dict(cols=P, kt=[DT])
    linear(plan, [dict(tile, rhs="merged")] * DT, dict(evac=into_ff(False, POST_MIX)))
    plan.add("post", "g x:8 sc:8", gain=8)
    norm = plan.add("norm", NORM, gain=16, version=1)
    for half in range(2):
        linear(plan, [dict(tile, rhs="u")] * HALF,
               dict(stat=None if half else norm,
                    evac=lambda x, mm: plan.add("evac_up", "up", m=x, j=mm.j, done=mm.c)))
        linear(plan, [dict(cols=P, kt=[DT, DT], rhs="hidden")] * DT, dict(evac=into_ff(half == 1, POST_FFN if half else None)))
    plan.add("post", "g x:8 sc:8", gain=24)
    return plan


def conv_ffn_steps(plan, layer, version):
    norm = plan.add("norm", NORM, gain=("ffn", layer), version=version)

    def hidden(x, mm):
        if x % 2 == 0:
            plan.add("evac_gate", "cg", m=x // 2, j=mm.j, done=mm.c, layer=layer)
        else:
            plan.add("evac_cup", "cu", m=x // 2, j=mm.j, done=mm.c)

    linear(plan, [dict(kt=[DT], cols=P, rhs="u")] * (2 * C_TILES), dict(stat=norm, evac=hidden))
    linear(plan, [dict(kt=[8, 8, 6], cols=P, rhs="conv")] * DT,
           dict(evac=lambda x, mm: plan.add("evac_res", "x", m=x, j=mm.j, done=done_of(mm))))


def plan_second():
    plan = Plan()
    tile = dict(kt=[DT], cols=P)
    norm = plan.add("norm", NORM, gain=("mix", 0), version=0)

    def ssm_input(x, mm):
        plan.add("evac_u", "eu", m=x, j=mm.j, done=mm.c)
        if x < 5:
            plan.add(f"s5_params{x}")
        if x == 3:
            plan.add("s5_grid")

    linear(plan, [dict(tile, rhs="u")] * DT, dict(stat=norm, evac=ssm_input))
    for x in range(PAIRS + 6):
        if x < PAIRS:
            plan.add("s5_table", "tb", p=x)
        if 1 <= x <= PAIRS:
            plan.add("s5_rot", "ro", p=x - 1)
        if 2 <= x <= PAIRS + 1:
            plan.add("s5_scan", "sn", p=x - 2)
        if 3 <= x <= PAIRS + 2:
            plan.add("s5_out", "so", p=x - 3)
        if x >= 7 and (x - 3) % 4 == 0:
            plan.add("s5_gelu0", "", m=(x - 7) // 4)
        if x >= 8 and (x - 4) % 4 == 0:
            plan.add("s5_gelu1", "", m=(x - 8) // 4)
        if x >= 9 and (x - 5) % 4 == 0:
            plan.add("s5_gelu2", "", m=(x - 9) // 4)

    def glu(x, mm):
        if x % 2 == 0:
            plan.add("evac_glu_gate", "gg", m=x // 2, j=mm.j, done=mm.c)
        else:
            plan.add("evac_glu", "x", m=x // 2, j=mm.j, done=mm.c)

    linear(plan, [dict(tile, rhs="s5")] * (2 * DT), dict(evac=glu))
    conv_ffn_steps(plan, 0, 1)
    norm = plan.add("norm", NORM, gain=("kv", 0), version=2)

    turns = {}

    def keys_and_values(x, mm):
        plan.add("evac_k2" if x < DT else "evac_v2", "kv", m=x % DT, j=mm.j, done=mm.c)
        turns[x] = mm.j
        if x > DT:
            plan.add("v2_turn", "v2", m=x - 1 - DT, kv=x - 1, j=turns[x - 1])

    linear(plan, [dict(tile, rhs="u")] * (2 * DT), dict(stat=norm, evac=keys_and_values))
    plan.add("v2_turn", "v2", m=DT - 1, kv=2 * DT - 1, j=turns[2 * DT - 1])
    plan.add("regain", "n:8", gain=("mix", 1))
    linear(plan, [dict(tile, rhs="u")] * DT,
           dict(evac=lambda x, mm: plan.add("evac_q2", "q2", m=x, j=mm.j, done=mm.c)))
    for x in range(H2 + 4):
        if x < H2:
            plan.add("sb_scores", "z", h=x)
        if x >= 4:
            plan.add("sb_out_cut", h=x - 4)
        if 2 <= x <= H2 + 1:
            plan.add("sb_weights_lo", h=x - 2)
        if x < H2:
            plan.add("sb_sum", h=x)
        if 1 <= x <= H2:
            plan.add("sb_weights", "sums", h=x - 1)
        if x < H2:
            plan.add("sb_cut", h=x)
        if 1 <= x <= H2:
            plan.add("sb_weights_hi", h=x - 1)
        if 3 <= x <= H2 + 2:
            plan.add("sb_out", "o", h=x - 3)
    linear(plan, [dict(tile, rhs="y2")] * DT,
           dict(evac=lambda x, mm: plan.add("evac_res", "x", m=x, j=mm.j, done=mm.c)))
    conv_ffn_steps(plan, 1, 3)
    plan.add("final", "f a:4 s:3 g", version=4)
    return plan


LAYER, SECOND = plan_layer(), plan_second()
for st in LAYER.steps:
    if st.kind == "evac_ff" and st.f is not None:
        last_f = st.f
    if st.kind == "evac_ff" and st.a is not None:
        st.last_f, last_a = last_f, st.a
    if st.kind == "evac_ff" and st.s is not None:
        st.last_a, last_s = last_a, st.s
    if st.kind == "post":
        st.last_s = last_s
last_use = None
for st in SECOND.steps:
    if st.kind in ("norm", "regain"):
        st.last_use = last_use
    elif st.kind == "mm" and st.rhs in ("u", "s5"):
        last_use = done_of(st)
turns = {st.rot: st.b for st in LAYER.steps if st.kind == "turn"}
for st in LAYER.steps:
    if st.kind == "turn_in" and st.rot:
        st.turn_before = turns[st.rot - 1]
assert LAYER.total["c"] == CHUNKS_L and LAYER.total["c"] + CHUNKS_L + SECOND.total["c"] == CHUNKS


def words(step):
    if step.kind == "mla_mm":
        return [CQT * QK + CKT * P]
    return [k * step.cols for k in step.kt]


LAYER_WORDS = [w for s in LAYER.steps if s.kind in ("mm", "mla_mm") for w in words(s)] + [SLOT]
SECOND_WORDS = [w for s in SECOND.steps if s.kind == "mm" for w in words(s)] + [0]

COL = [0, SEQ, 2 * SEQ, SEQ + 3 * P]
WIDE = [SEQ - P * k for k in range(KT)]

G_BIAS = 32
G_Q, G_K, G_CQ, G_CKV = 48, 49, 50, 53
N_LAYER_PARAMS = 55
S_GAIN = {("mix", 0): 0, ("mix", 1): 8, ("ffn", 0): 16, ("ffn", 1): 24, ("kv", 0): 32, ("final", 0): 40}
S_D, S_CONV, S_A = 48, 56, 56 + 2 * C_TILES * 4
N_SECOND_PARAMS = S_A + 3 * PAIRS
MATS = ("ident", "ones", "ones_head", "rot_a", "rot_b", "neg_tri", "neg_ones", "mask")


def build(nc, weights, x, layer_params, second_params, mats, tables, steps_t, s5_b, s5_c, out):
    ctx = ExitStack()
    with ctx:
        KB = 1024
        start = 16640
        fence = ctx.enter_context(nc.sbuf_tensor("fence", [P, 53120], F32))

        def at(name, kb, shape, dt=F32):
            return nc.alloc_sbuf_tensor_at(name, shape, dt, offset=start + int(kb * KB))

        X = at("X", 0, [P, DT, SEQ])
        RSTD = at("RSTD", 16, [P, SEQ])
        RAWW = at("RAWW", 18, [P, RAW, SLOT])
        WH = at("WH", 34, [P, CUT, SLOT], F32R)
        WL = at("WL", 42, [P, CUT, SLOT], F32R)
        UH = at("UH", 50, [P, DT, SEQ], F32R)
        UL = at("UL", 66, [P, DT, SEQ], F32R)
        PHH = at("PHH", 50, [P, 2, KT, SEQ], F32R)
        PHL = at("PHL", 66, [P, 2, KT, SEQ], F32R)
        FF = at("FF", 82, [P, DT, SEQ])
        TMP = at("TMP", 98, [P, 4, SEQ])
        A0 = 106
        QH = at("QH", A0, [P, QT, SEQ], F32R)
        QL = at("QL", A0 + 8, [P, QT, SEQ], F32R)
        KH = at("KH", A0 + 16, [P, SEQ], F32R)
        KL = at("KL", A0 + 18, [P, SEQ], F32R)
        VH = at("VH", A0 + 20, [P, KT, P], F32R)
        VL = at("VL", A0 + 22, [P, KT, P], F32R)
        CH = at("CH", A0 + 24, [P, CQT + CKT, SEQ], F32R)
        CL = at("CL", A0 + 34, [P, CQT + CKT, SEQ], F32R)
        MQH = at("MQH", A0 + 44, [P, 2, SEQ], F32R)
        MQL = at("MQL", A0 + 48, [P, 2, SEQ], F32R)
        MKH = at("MKH", A0 + 52, [P, 2, SEQ], F32R)
        MKL = at("MKL", A0 + 56, [P, 2, SEQ], F32R)
        MVH = at("MVH", A0 + 60, [P, 2, KT, P], F32R)
        MVL = at("MVL", A0 + 64, [P, 2, KT, P], F32R)
        YBH = at("YBH", A0 + 68, [P, QT, SEQ], F32R)
        YBL = at("YBL", A0 + 76, [P, QT, SEQ], F32R)
        RH = at("RH", A0 + 84, [P, SEQ], F32R)
        RL = at("RL", A0 + 86, [P, SEQ], F32R)
        RKV = at("RKV", A0 + 88, [P, SEQ])
        RCQ = at("RCQ", A0 + 90, [P, SEQ])
        SQUARES = at("SQUARES", A0 + 88, [P, SEQ])
        KVF = at("KVF", A0 + 92, [P, 2, SEQ])
        MH = at("MH", A0 + 24, [P, DT, SEQ], F32R)
        ML = at("ML", A0 + 40, [P, DT, SEQ], F32R)
        HH = at("HH", A0, [P, HALF, SEQ], F32R)
        HL = at("HL", A0 + 32, [P, HALF, SEQ], F32R)
        CHH = at("CHH", A0, [P, C_TILES, SEQ], F32R)
        CHL = at("CHL", A0 + 44, [P, C_TILES, SEQ], F32R)
        GATE = at("GATE", 82, [P, 2, 520])
        S5U = at("S5U", A0, [P, DT, SEQ])
        BBT = at("BBT", A0 + 16, [P, 2, DT, P])
        S5C = at("S5C", A0 + 24, [P, 3, PAIRS, 32])
        S5A = at("S5A", A0 + 36, [P, 24, PAIRS])
        S5AR = at("S5AR", A0 + 39, [P, PAIRS], F32R)
        S5N = at("S5N", A0 + 40, [P, COARSE + FINE])
        GRID = at("GRID", 100, [P, PAIRS, COARSE + FINE])
        GRIDA = at("GRIDA", A0 + 68, [P, PAIRS, COARSE + FINE])
        GRIDB = at("GRIDB", A0 + 74, [P, PAIRS, COARSE + FINE])
        S5B = at("S5B", A0 + 44, [P, 2, PAIRS, 32])
        S5BB = at("S5BB", A0 + 52, [P, 2, PAIRS, 32])
        S5BT = at("S5BT", A0 + 60, [P, 2, PAIRS, 32])
        S5T = at("S5T", A0 + 44, [P, 26, SEQ])
        K2H = at("K2H", A0, [P, DT, SEQ], F32R)
        K2L = at("K2L", A0 + 16, [P, DT, SEQ], F32R)
        V2H = at("V2H", A0 + 32, [P, KT, DM], F32R)
        V2L = at("V2L", A0 + 48, [P, KT, DM], F32R)
        Q2H = at("Q2H", A0 + 64, [P, DT, SEQ], F32R)
        Q2L = at("Q2L", A0 + 80, [P, DT, SEQ], F32R)
        TRI = SEQ * (KT + 1) * KT // 2 // KT
        SPH = at("SPH", 50, [P, TRI], F32R)
        SBS = at("SBS", 87, [P, TRI])
        SPL = at("SPL", 87, [P, TRI], F32R)
        SBZ = at("SBZ", 82, [P, TRI])
        SBP = at("SBP", 70, [P, TRI])
        WTH = [at(f"WTH{k}", kb, [P, TRI], F32R) for k, kb in enumerate((55, 60, 98))]
        SBW = [at(f"SBW{k}", kb, [P, TRI]) for k, kb in enumerate((65, 75, 92))]
        WTL = [at(f"WTL{k}", kb, [P, TRI], F32R) for k, kb in enumerate((65, 75, 92))]
        MAT = at("MAT", 202, [P, 3, P])
        MATR = at("MATR", 203.5, [P, 4, P], F32R)
        LP = at("LP", 205.5, [P, N_LAYER_PARAMS])
        MASK = at("MASK", 207.1875, [P, P])
        STAT = at("STAT", 205.8125, [P, 3, 4])
        SP_ = at("SP_", 205.875, [P, N_SECOND_PARAMS])
        IDENT, ONES, ONES_HEAD = (MAT[:, k, :] for k in range(3))
        ROT_A, ROT_B, NEG_TRI, NEG_ONES = (MATR[:, k, :] for k in range(4))

        BANK = [ctx.enter_context(nc.psum_tensor(f"bank{k}", [P, SEQ], F32)) for k in range(8)]
        OUTB, TURN = BANK[6], BANK[7]

        def stat_bank(g):
            return BANK[6 if g % 2 == 0 else 3]

        def signal(name, kind, slots=0):
            return Signal(ctx.enter_context(nc.semaphore(name)), LAYER.total.get(kind, 0), slots)

        raw_in = [ctx.enter_context(nc.semaphore(f"raw_in{k}")) for k in range(RAW)]
        hi = signal("hi", "c")
        lo = signal("lo", "c", RAW)
        used = signal("used", "c", CUT)
        bank_free = signal("bank_free", "j", 2)
        x_in, par_in, mat_in, tab_in, s5_in, y_out = (ctx.enter_context(nc.semaphore(k)) for k in (
            "x_in", "par_in", "mat_in", "tab_in", "s5_in", "y_out"))
        mats_cut = ctx.enter_context(nc.semaphore("mats_cut"))
        mv_zero = ctx.enter_context(nc.semaphore("mv_zero"))
        x_done = signal("x_done", "x", DT)
        uh, ul = signal("uh", "n"), signal("ul", "n")
        sq = signal("sq", "s")
        summed = signal("summed", "s", 2)
        first_sq, sq_in = signal("first_sq", "f"), signal("sq_in", "a")
        added = signal("added", "a", 2)
        logged, rstd = signal("logged", "g"), signal("rstd", "g")
        scaled = signal("scaled", "sc")
        turned_in = signal("turned_in", "qk")
        rh, rl, rcos, rdone = signal("rh", "rot"), signal("rl", "rot"), signal("rcos", "rot"), signal("rdone", "rot")
        rot_h, rot_l = signal("rot_h", "rot"), signal("rot_l", "rot")
        turn, turn_free = signal("turn", "b"), signal("turn_free", "b", 1)
        v_h, c_h, c_l = signal("v_h", "vh"), signal("c_h", "cn"), signal("c_l", "cn")
        mk_h, mk_l = signal("mk_h", "mk"), signal("mk_l", "mk")
        scores, row_max = signal("scores", "u"), signal("row_max", "u")
        expd, recip = signal("expd", "u", 2), signal("recip", "u")
        normed, probs_t = signal("normed", "u"), signal("probs_t", "u", 4)
        probs_h, probs_l = signal("probs_h", "u"), signal("probs_l", "u", 2)
        pv, y_h, y_l = signal("pv", "pv"), signal("y_h", "pv"), signal("y_l", "pv")
        gate = signal("gate", "ge")
        merged, merged_h, merged_l = (signal(k, "mt") for k in ("merged", "merged_h", "merged_l"))
        hid_h, hid_f, hid_l = (signal(k, "up") for k in ("hid_h", "hid_f", "hid_l"))
        cgx, cge = signal("cgx", ""), signal("cge", "")
        ct, chh, chl = (signal(k, "") for k in ("ct", "chh", "chl"))
        eu, grid, ts = signal("eu", ""), signal("grid", ""), signal("ts", "")
        sp_pool, sp_act, sp_dve, sp_pe = (signal(k, "") for k in ("sp_pool", "sp_act", "sp_dve", "sp_pe"))
        tb, tba, ro_pe, ro, ro_sum, sn, sn_q, so, ys = (signal(k, "") for k in (
            "tb", "tba", "ro_pe", "ro", "ro_sum", "sn", "sn_q", "so", "ys"))
        ge_q, ge_l, v2_l = (signal(k, "") for k in ("ge_q", "ge_l", "v2_l"))
        ge_a, ge_p, ge_h = (signal(k, "") for k in ("ge_a", "ge_p", "ge_h"))
        gge = signal("gge", "")
        kv_x, kv_h, kv_l, v2_pe, v2_h = (signal(k, "") for k in ("kv_x", "kv_h", "kv_l", "v2_pe", "v2_h"))
        q2_x, q2_h, q2_l = (signal(k, "") for k in ("q2_x", "q2_h", "q2_l"))
        z, zp, za, ze, zl, zs, z_h, z_l = (signal(k, "") for k in ("z", "zp", "za", "ze", "zl", "zs", "z_h", "z_l"))
        w, we, w_h, w_l = (signal(k, "") for k in ("w", "we", "w_h", "w_l"))
        o, o_h, o_l = (signal(k, "") for k in ("o", "o_h", "o_l"))
        outs = signal("outs", "")

        def rotation_ready(l, st):
            if st.what in "qk":
                return turned_in.sem, turned_in.after(l, st.qk)
            return bank_free.sem, bank_free.after(l, st.j)

        def sine(st):
            return FF[:, st.rot % 2, :] if st.what == "mla" else KVF[:, st.rot % 2, :]

        def total_of(st):
            return FF[:, 3, :] if st.version == 3 else SQUARES[:]

        def f32(ap):
            return ap.bitcast(F32)

        def slot_words(ap, slot, n):
            return ap[:, slot, 0:n]

        def s5a(k):
            return S5A[:, k, :]

        block = ctx.enter_context(nc.Block())

        @block.sync
        def _(sp):
            sp.dma_start(MAT[:], mats[:, 0:3 * P].rearrange("p (k n) -> p k n", k=3)).then_inc(mat_in, 16)
            sp.dma_start(FF[:, 0, 0:4 * P], mats[:, 3 * P:7 * P]).then_inc(mat_in, 16)
            sp.dma_start(MASK[:], mats[:, 7 * P:8 * P]).then_inc(mat_in, 16)
            sp.dma_start(SP_[:], second_params).then_inc(mat_in, 16)
            for k in range(DT):
                sp.dma_start(X[:, k, :], x[k]).then_inc(x_in, 16)
            with sp.Fori(0, CHUNKS // RAW) as it:
                for k in range(RAW):
                    sp.wait_ge(lo.sem, it * RAW + (k + 1))
                    sp.dma_start(RAWW[:, k, :], weights[bass.ds(it * RAW + k, 1)].rearrange("a p n -> (a p) n")
                                 ).then_inc(raw_in[k], 16)
            for k in range(DT):
                sp.wait_ge(outs.sem, k + 1)
                sp.dma_start(out[k], FF[:, k, :]).then_inc(y_out, 16)
            sp.wait_ge(y_out, 16 * DT)

        @block.gpsimd
        def _(pool):
            def layer_inputs(l):
                pool.wait_ge(x_done.sem, x_done.room(l, DT - 1))
                pool.wait_ge(mats_cut, 1)
                pool.dma_start(LP[:, 0:N_LAYER_PARAMS], layer_params[bass.ds(l, 1)].rearrange("a p n -> (a p) n")
                               ).then_inc(par_in, 16)
                pool.dma_start(FF[:, 0:4, :], tables.rearrange("k p n -> p k n")).then_inc(tab_in, 16)
                for k in range(2):
                    for v in (MVH, MVL):
                        ins = pool.memset(f32(v[:, k, :, HD - k * HD:P - k * HD]), 0.0)
                ins.then_inc(mv_zero, 1)

            def add_squares(l, total, st, n):
                pool.wait_ge(first_sq.sem, first_sq.after(l, st.f))
                for k in range(st.a, st.a + n):
                    add_squared(l, total, k, k > st.a)

            def add_squared(l, total, k, again):
                if again:
                    pool.wait_ge(added.sem, added.after(l, k - 1))
                pool.wait_ge(sq_in.sem, sq_in.after(l, k))
                pool.tensor_tensor(total, total, TMP[:, 2 + k % 2, :], ALU.add).then_inc(added.sem, 1)

            def step(l, st):
                if st.kind == "stat":
                    add_squares(l, SQUARES[:], st, ADDED)
                elif st.kind == "evac_ff" and st.a is not None:
                    if st.m == 1:
                        pool.wait_ge(first_sq.sem, first_sq.after(l, st.last_f))
                    add_squared(l, SQUARES[:], st.a, st.m > 1)
                elif st.kind == "turn_in":
                    pool.wait_ge(*rotation_ready(l, st))
                    if st.rot == 0:
                        pool.wait_ge(tab_in, l * 16 + 16)
                    cos = 0 if st.what in "qk" else 2
                    pool.tensor_tensor(FF[0:st.rows, 4 + st.rot % 2, :], FF[0:st.rows, 6 + st.rot % 2, :],
                                       FF[0:st.rows, cos, :], ALU.mult).then_inc(rcos.sem, 1)
                elif st.kind == "turn":
                    rows = slice(0, st.rows)
                    pool.wait_ge(rcos.sem, rcos.after(l, st.rot))
                    pool.wait_ge(turn_free.sem, turn_free.after(l, st.b))
                    pool.tensor_tensor(FF[rows, 6 + st.rot % 2, :], FF[rows, 4 + st.rot % 2, :], sine(st)[rows, :], ALU.add
                                       ).then_inc(rdone.sem, 1)
                elif st.kind == "mla_k":
                    pool.wait_ge(mk_h.sem, mk_h.after(l, st.mk))
                    pool.tensor_tensor(MKL[0:HD, st.h % 2, :], KVF[0:HD, st.h % 2, :], f32(MKH[0:HD, st.h % 2, :]), ALU.subtract
                                       ).then_inc(mk_l.sem, 1)
                elif st.kind == "N":
                    pool.wait_ge(recip.sem, recip.after(l, st.u))
                    pool.tensor_tensor(TMP[:, st.u % 4, :], TMP[:, st.u % 4, :],
                                       STAT[:, 2, st.u % 4:st.u % 4 + 1].to_broadcast([P, SEQ]), ALU.mult
                                       ).then_inc(normed.sem, 1)
                elif st.kind == "evac_br_b":
                    pool.wait_ge(bank_free.sem, bank_free.after(l, st.j))
                    pool.tensor_tensor(FF[:, 4 + st.m % 2, :], FF[:, 4 + st.m % 2, :], FF[:, 6 + st.m % 2, :],
                                       ALU.add).then_inc(merged.sem, 1)
                elif st.kind == "evac_up":
                    pool.wait_ge(bank_free.sem, bank_free.after(l, st.j))
                    pool.tensor_tensor(TMP[:, st.m % 2, :], TMP[:, 2 + st.m % 2, :], TMP[:, 2 + st.m % 2, :],
                                       ALU.mult).then_inc(hid_f.sem, 1)
                    pool.wait_ge(hid_f.sem, hid_f.after(l, st.up))
                    pool.wait_ge(hid_h.sem, hid_h.after(l, st.up))
                    pool.tensor_tensor(HL[:, st.m, :], TMP[:, st.m % 2, :], f32(HH[:, st.m, :]),
                                       ALU.subtract).then_inc(hid_l.sem, 1)

            def second_block():
                (A_RE, A_IM, LDT) = (SP_[:, S_A + k * PAIRS:S_A + (k + 1) * PAIRS] for k in range(3))
                n = [0]

                def chain(ins):
                    ins.then_inc(sp_pool.sem, 1)
                    n[0] += 1
                    pool.wait_ge(sp_pool.sem, n[0])

                def tt(out_, a, b, op):
                    chain(pool.tensor_tensor(out_, a, b, op))

                def ts(out_, a, s1, s2, op0, op1=None):
                    if op1 is None:
                        chain(pool.tensor_scalar(out_, a, s1, None, op0))
                    else:
                        chain(pool.tensor_scalar(out_, a, s1, s2, op0, op1))

                def wide(k):
                    return s5a(k).unsqueeze(2).to_broadcast([P, PAIRS, 32])

                for st in SECOND.steps:
                    if st.kind in ("stat", "final"):
                        add_squares(2, total_of(st), st, ADDED)
                    elif st.kind == "s5_params0":
                        pool.wait_ge(x_done.sem, x_done.room(2, DT - 1))
                        pool.dma_start(S5B[:], s5_b.rearrange("k p (j h) -> p k j h", h=32)).then_inc(s5_in, 16)
                        pool.dma_start(S5C[:, 0:2], s5_c.rearrange("k p (j h) -> p k j h", h=32)).then_inc(s5_in, 16)
                        pool.dma_start(S5N[:], steps_t).then_inc(s5_in, 16)
                        pool.wait_ge(sp_act.sem, 1)
                        tt(s5a(1), A_RE, s5a(0), ALU.mult)
                        tt(s5a(2), A_IM, s5a(0), ALU.mult)
                    elif st.kind == "s5_params1":
                        ts(s5a(3), s5a(2), INV2PI, MAGIC, ALU.mult, ALU.add)
                        ts(s5a(3), s5a(3), MAGIC, None, ALU.subtract)
                        for part in (PI_A, PI_B, PI_C):
                            ts(s5a(4), s5a(3), part, None, ALU.mult)
                            tt(s5a(2), s5a(2), s5a(4), ALU.subtract)
                        ts(s5a(2), s5a(2), 3.1415925, -3.1415925, ALU.min, ALU.max)
                        ts(s5a(5), s5a(2), INV2PI, None, ALU.mult)
                    elif st.kind == "s5_params2":
                        pool.wait_ge(sp_act.sem, 6)
                        tt(s5a(6), s5a(5), f32(S5AR[:]), ALU.subtract)
                        tt(s5a(11), s5a(7), s5a(10), ALU.mult)
                        tt(s5a(12), s5a(7), s5a(8), ALU.mult)
                        tt(s5a(13), A_RE, A_RE, ALU.mult)
                        tt(s5a(14), A_IM, A_IM, ALU.mult)
                        tt(s5a(13), s5a(13), s5a(14), ALU.add)
                        ts(s5a(11), s5a(11), 1.0, None, ALU.subtract)
                        tt(s5a(15), s5a(11), A_RE, ALU.mult)
                        tt(s5a(16), s5a(12), A_IM, ALU.mult)
                        tt(s5a(15), s5a(15), s5a(16), ALU.add)
                        tt(s5a(16), s5a(12), A_RE, ALU.mult)
                        tt(s5a(17), s5a(11), A_IM, ALU.mult)
                        tt(s5a(16), s5a(16), s5a(17), ALU.subtract)
                    elif st.kind == "s5_params3":
                        pool.wait_ge(sp_dve.sem, 1)
                        tt(s5a(15), s5a(15), s5a(18), ALU.mult)
                        tt(s5a(16), s5a(16), s5a(18), ALU.mult)
                        pool.wait_ge(s5_in, 48)
                        tt(S5BB[:, 0], S5B[:, 0], wide(15), ALU.mult)
                        tt(S5BB[:, 1], S5B[:, 1], wide(15), ALU.mult)
                        tt(S5BT[:, 0], S5B[:, 1], wide(16), ALU.mult)
                        tt(S5BT[:, 1], S5B[:, 0], wide(16), ALU.mult)
                        tt(S5BB[:, 0], S5BB[:, 0], S5BT[:, 0], ALU.subtract)
                        tt(S5BB[:, 1], S5BB[:, 1], S5BT[:, 1], ALU.add)
                        ts(S5C[:, 2], S5C[:, 1], -1.0, None, ALU.mult)
                    elif st.kind == "s5_rot":
                        pool.wait_ge(ro.sem, ro.after(2, 4 * st.p + 3))
                        a = [S5T[:, 4 * (st.p % 3) + k, :] for k in range(4)]
                        pool.tensor_tensor(a[0], a[0], a[1], ALU.add).then_inc(ro_sum.sem, 1)
                        pool.tensor_tensor(a[2], a[3], a[2], ALU.subtract).then_inc(ro_sum.sem, 1)
                    elif st.kind == "s5_scan":
                        pool.wait_ge(sn.sem, sn.after(2, 2 * st.p + 1))
                        a = [S5T[:, 4 * (st.p % 3) + k, :] for k in range(4)]
                        r = [S5T[:, 12 + 2 * (st.p % 2) + k, :] for k in range(2)]
                        c, s = (S5T[:, 16 + 2 * (st.p % 3) + k, :] for k in range(2))
                        pool.tensor_tensor(a[0], r[0], c, ALU.mult).then_inc(sn_q.sem, 1)
                        pool.tensor_tensor(a[1], r[1], s, ALU.mult).then_inc(sn_q.sem, 1)
                    elif st.kind == "s5_gelu0":
                        f = [FF[:, 4 * (st.m % 2) + k, :] for k in range(4)]
                        pool.wait_ge(ge_a.sem, ge_a.after(2, 2 * st.m))
                        pool.tensor_scalar(f[1], f[1], 0.044715, 1.0, ALU.mult, ALU.add).then_inc(ge_p.sem, 1)
                        pool.wait_ge(ge_p.sem, ge_p.after(2, 3 * st.m))
                        pool.tensor_tensor(f[1], f[1], f[0], ALU.mult).then_inc(ge_p.sem, 1)
                        pool.wait_ge(ge_a.sem, ge_a.after(2, 2 * st.m + 1))
                        pool.tensor_tensor(f[3], f[0], f[2], ALU.mult).then_inc(ge_p.sem, 1)
                    elif st.kind == "evac_cup":
                        u = (FF[:, 7, :], TMP[:, 2, :])[st.m % 2]
                        pool.wait_ge(bank_free.sem, bank_free.after(2, st.j))
                        pool.wait_ge(cge.sem, cge.after(2, st.cu))
                        pool.tensor_tensor(u, u, FF[:, 5 + st.m % 2, :], ALU.mult).then_inc(ct.sem, 1)
                        pool.wait_ge(chh.sem, chh.after(2, st.cu))
                        pool.tensor_tensor(CHL[:, st.m, :], u, f32(CHH[:, st.m, :]), ALU.subtract).then_inc(chl.sem, 1)

            pool.sem_inc(added.sem, 2)
            with pool.Fori(0, LAYERS) as l:
                layer_inputs(l)
                for st in LAYER.steps:
                    step(l, st)
            second_block()

        def pv_place(h):
            if h < HEADS:
                a = h // QT * HD
                return QH, QL, slice(a, a + HD), h % QT
            m = h - HEADS
            return YBH, YBL, slice(m % 2 * HD, m % 2 * HD + HD), m // 2

        def small_input(st):
            k = st.i if st.kind == "evac_cq" else CQT + st.i
            return k, LP[:, G_CQ + k:G_CQ + k + 1]

        def rot_dest(st):
            if st.what == "q":
                return [(QH[:, st.i, :], QL[:, st.i, :])], slice(0, P)
            if st.what == "k":
                return [(KH[:], KL[:])], slice(0, P)
            if st.what == "mla":
                return [(MQH[0:QK, st.h % 2, :], MQL[0:QK, st.h % 2, :])], slice(0, QK)
            return [(MKH[HD:QK, k, :], MKL[HD:QK, k, :]) for k in range(2)], slice(HD, QK)

        @block.scalar
        def _(act):
            def cut_next(l, st, sizes):
                for n in range(len(st.kt)):
                    c = st.c + n + 1
                    if sizes[c]:
                        cut(l, c, sizes[c])

            def cut(l, c, size):
                act.wait_ge(raw_in[c % RAW], l * (CHUNKS_L // RAW * 16) + 16 * (c // RAW + 1))
                act.wait_ge(used.sem, used.room(l, c))
                act.activation(slot_words(WH, c % CUT, size), slot_words(RAWW, c % RAW, size), ACT.Copy
                               ).then_inc(hi.sem, 1)

            def square(l, s, src):
                act.wait_ge(summed.sem, summed.room(l, s))
                act.activation(TMP[0:src.shape[0], s % 2, :], src, ACT.Square).then_inc(sq.sem, 1)

            def factor(l, g, last_s, dst, scale, bias):
                act.wait_ge(summed.sem, summed.after(l, last_s))
                act.activation(dst, stat_bank(g)[:], ACT.Ln, bias=bias, scale=scale).then_inc(logged.sem, 1)
                act.wait_ge(logged.sem, logged.after(l, g))
                act.activation(dst, dst, ACT.Exp, scale=-0.5).then_inc(rstd.sem, 1)

            def gains(l, st, gain):
                for k in range(DT):
                    act.activation(UH[:, k, :], X[:, k, :], ACT.Copy, scale=gain[:, k:k + 1]).then_inc(uh.sem, 1)

            def square_for_pool(l, a, src):
                act.wait_ge(added.sem, added.room(l, a))
                act.activation(TMP[:, 2 + a % 2, :], src, ACT.Square).then_inc(sq_in.sem, 1)

            def norm(l, st, gain, total):
                for k in range(DT):
                    act.wait_ge(x_done.sem, x_done.room(l, DT * st.version + k))
                    if gain is not None:
                        act.activation(UH[:, k, :], X[:, k, :], ACT.Copy, scale=gain[:, k:k + 1]).then_inc(uh.sem, 1)
                    if k == 0:
                        act.activation(total, X[:, k, :], ACT.Square).then_inc(first_sq.sem, 1)
                    elif k <= ADDED:
                        square_for_pool(l, st.a + k - 1, X[:, k, :])
                    else:
                        square(l, st.s + k - ADDED - 1, X[:, k, :])

            def stat(l, st):
                factor(l, st.g, st.s + DT - 2 - ADDED, RSTD[:], 1.0 / DM, EPS)

            def step(l, st):
                kind = st.kind
                if kind in ("mm", "mla_mm"):
                    cut_next(l, st, LAYER_WORDS)
                elif kind == "norm":
                    if st.gain == 0:
                        act.wait_ge(par_in, l * 16 + 16)
                    norm(l, st, LP[:, st.gain:st.gain + DT], SQUARES[:])
                elif kind == "stat":
                    stat(l, st)
                elif kind == "regain":
                    gains(l, st, LP[:, st.gain:st.gain + DT])
                elif kind in ("evac_q", "evac_k"):
                    act.wait_ge(bank_free.sem, bank_free.after(l, st.j))
                    square(l, st.s, TMP[:, 2 + st.x % 2, :])
                elif kind in ("evac_cq", "evac_ckv"):
                    k, gain = small_input(st)
                    act.wait_ge(bank_free.sem, bank_free.after(l, st.j))
                    act.activation(CH[:, k, :], TMP[:, 2 + st.x % 2, :], ACT.Copy, scale=gain).then_inc(c_h.sem, 1)
                    square(l, st.s, TMP[:, 2 + st.x % 2, :])
                elif kind == "rc_cq":
                    factor(l, st.g, st.s, RCQ[:], 1.0 / Q_RANK, EPS)
                elif kind == "rc_ckv":
                    factor(l, st.g, st.s, RKV[:], 1.0 / KV_RANK, EPS)
                elif kind == "turn_in":
                    if st.what == "q":
                        factor(l, st.g, st.s, FF[:, 4 + st.rot % 2, :], 1.0, HD * EPS)
                    elif st.what == "k":
                        factor(l, st.g, st.s, FF[:, 4 + st.rot % 2, :], 1.0 / HD, EPS)
                    act.wait_ge(*rotation_ready(l, st))
                    if st.rot:
                        act.wait_ge(turn.sem, turn.after(l, st.turn_before))
                    act.activation(RH[0:st.rows, :], FF[0:st.rows, 6 + st.rot % 2, :], ACT.Copy).then_inc(rh.sem, 1)
                elif kind == "turn_out":
                    dests, rows = rot_dest(st)
                    act.wait_ge(rdone.sem, rdone.after(l, st.rot))
                    for n, (h, _) in enumerate(dests):
                        ins = act.activation(h, FF[rows, 6 + st.rot % 2, :], ACT.Copy)
                    ins.then_inc(rot_h.sem, 1)
                elif kind == "gqa_v":
                    act.wait_ge(turn.sem, turn.after(l, st.b))
                    act.activation(VH[:].rearrange("p k n -> p (k n)"), TURN[:], ACT.Copy).then_inc(v_h.sem, 1)
                elif kind == "mla_k":
                    act.wait_ge(bank_free.sem, bank_free.after(l, st.j + 1))
                    act.activation(MKH[0:HD, st.h % 2, :], KVF[0:HD, st.h % 2, :], ACT.Copy).then_inc(mk_h.sem, 1)
                elif kind == "mla_v":
                    act.wait_ge(turn.sem, turn.after(l, st.b))
                    a = st.h % 2 * HD
                    act.activation(MVH[:, st.h % 2, :, a:a + HD], TURN[:].rearrange("p (k n) -> p k n", k=KT)[:, :, HD:P],
                                   ACT.Copy).then_inc(v_h.sem, 1)
                elif kind == "S":
                    act.wait_ge(row_max.sem, row_max.after(l, st.u))
                    act.wait_ge(probs_t.sem, probs_t.room(l, st.u))
                    r = st.u % 4
                    act.activation(TMP[:, r, :], BANK[2 + st.u % 2][:], ACT.Exp, bias=STAT[:, 0, r:r + 1],
                                   accum_out=STAT[:, 1, r:r + 1]).then_inc(expd.sem, 1)
                elif kind == "T":
                    act.wait_ge(probs_t.sem, probs_t.after(l, st.u))
                    act.activation(PHH[:, st.h % 2, :, st.t * P:(st.t + 1) * P],
                                   BANK[4 + st.u % 2][:].rearrange("p (k q) -> p k q", k=KT), ACT.Copy
                                   ).then_inc(probs_h.sem, 1)
                elif kind == "PV_out":
                    h, _, rows, k = pv_place(st.h)
                    act.wait_ge(pv.sem, pv.after(l, st.pv))
                    act.activation(h[rows, k, :], OUTB[rows, :], ACT.Copy).then_inc(y_h.sem, 1)
                elif kind in ("evac_ga", "evac_gb"):
                    b = kind == "evac_gb"
                    t = FF[:, 2 * b + st.m % 2, :]
                    act.wait_ge(bank_free.sem, bank_free.after(l, st.j))
                    bias = G_BIAS + DT * b + st.m
                    act.activation(t, t, ACT.Sigmoid, bias=LP[:, bias:bias + 1]).then_inc(gate.sem, 1)
                elif kind == "merge":
                    act.wait_ge(merged.sem, merged.after(l, st.mg))
                    act.activation(MH[:, st.m, :], FF[:, 4 + st.m % 2, :], ACT.Copy).then_inc(merged_h.sem, 1)
                    if st.m == DT - 1:
                        act.preload_act_table_set(LOG_EXP)
                elif kind == "evac_ff" and st.group is not None:
                    act.wait_ge(bank_free.sem, bank_free.after(l, st.j))
                    if st.m == 0:
                        act.activation(SQUARES[:], FF[:, st.m, :], ACT.Square).then_inc(first_sq.sem, 1)
                    elif st.a is not None:
                        square_for_pool(l, st.a, FF[:, st.m, :])
                    else:
                        square(l, st.s, FF[:, st.m, :])
                elif kind == "post":
                    factor(l, st.g, st.last_s, RCQ[:], 1.0 / DM, EPS)
                elif kind == "evac_up":
                    act.wait_ge(bank_free.sem, bank_free.after(l, st.j))
                    act.activation(HH[:, st.m, :], TMP[:, 2 + st.m % 2, :], ACT.Square).then_inc(hid_h.sem, 1)

            def second(st):
                kind = st.kind
                copy = ACT.Copy
                if kind == "mm":
                    cut_next(2, st, SECOND_WORDS)
                elif kind in ("norm", "regain"):
                    g = S_GAIN[st.gain]
                    if st.last_use is not None:
                        act.wait_ge(used.sem, used.after(2, st.last_use))
                    if kind == "norm":
                        act.preload_act_table_set(LOG_EXP)
                        norm(2, st, SP_[:, g:g + DT], total_of(st))
                    else:
                        gains(2, st, SP_[:, g:g + DT])
                elif kind == "stat":
                    stat(2, st)
                elif kind == "s5_params0":
                    act.activation(s5a(0), SP_[:, S_A + 2 * PAIRS:S_A + 3 * PAIRS], ACT.Exp).then_inc(sp_act.sem, 1)
                elif kind == "s5_params1":
                    act.wait_ge(sp_pool.sem, 2)
                    act.activation(s5a(7), s5a(1), ACT.Exp).then_inc(sp_act.sem, 1)
                elif kind == "s5_params2":
                    act.wait_ge(sp_pool.sem, 12)
                    act.activation(s5a(8), s5a(2), ACT.Sin).then_inc(sp_act.sem, 1)
                    act.activation(s5a(9), s5a(2), ACT.Abs).then_inc(sp_act.sem, 1)
                    act.activation(S5AR[:], s5a(5), copy).then_inc(sp_act.sem, 1)
                    act.wait_ge(sp_act.sem, 5)
                    act.activation(s5a(10), s5a(9), ACT.Sin, bias=math.pi / 2, scale=-1.0).then_inc(sp_act.sem, 1)
                elif kind == "s5_params4":
                    for k in range(4):
                        act.wait_ge(sp_pe.sem, k + 1)
                        act.activation(BBT[:, k // 2, 4 * (k % 2):4 * (k % 2) + 4, :].rearrange("p t n -> p (t n)"),
                                       BANK[2 + k][:], copy).then_inc(sp_act.sem, 1)
                elif kind == "s5_table":
                    g, half = S5T[:, 22 + st.p % 2, :], S5T[:, 24 + st.p % 2, :]
                    c = S5T[:, 16 + 2 * (st.p % 3), :]
                    act.wait_ge(tb.sem, tb.after(2, st.p))
                    if st.p >= 2:
                        act.wait_ge(ts.sem, ts.after(2, st.p - 2))
                    act.activation(half, g, ACT.Sin, scale=math.pi).then_inc(tba.sem, 1)
                    act.wait_ge(tba.sem, tba.after(2, 5 * st.p))
                    act.activation(g, g, ACT.Abs).then_inc(tba.sem, 1)
                    if st.p >= 3:
                        act.wait_ge(sn_q.sem, sn_q.after(2, 2 * (st.p - 3) + 1))
                        act.wait_ge(ge_q.sem, ge_q.after(2, 2 * (st.p - 3) + 1))
                    act.activation(c, half, ACT.Square).then_inc(tba.sem, 1)
                    act.wait_ge(tba.sem, tba.after(2, 5 * st.p + 1))
                    act.activation(g, g, ACT.Sin, bias=math.pi / 2, scale=-math.pi).then_inc(tba.sem, 1)
                    act.wait_ge(tba.sem, tba.after(2, 5 * st.p + 2))
                    act.activation(c, c, copy, bias=1.0, scale=-2.0).then_inc(tba.sem, 1)
                elif kind == "s5_gelu0":
                    f = [FF[:, 4 * (st.m % 2) + k, :] for k in range(4)]
                    act.wait_ge(ys.sem, ys.after(2, st.m))
                    act.activation(f[1], f[0], ACT.Square).then_inc(ge_a.sem, 1)
                    act.wait_ge(ge_p.sem, ge_p.after(2, 3 * st.m + 1))
                    act.activation(f[2], f[1], ACT.Sigmoid, scale=2.0 * math.sqrt(2.0 / math.pi)).then_inc(ge_a.sem, 1)
                elif kind == "s5_gelu1":
                    act.wait_ge(ge_p.sem, ge_p.after(2, 3 * st.m + 2))
                    act.activation(UH[:, st.m, :], FF[:, 4 * (st.m % 2) + 3, :], copy).then_inc(ge_h.sem, 1)
                elif kind == "evac_glu_gate":
                    t = FF[:, st.m % 2, :]
                    act.wait_ge(bank_free.sem, bank_free.after(2, st.j))
                    act.activation(t, t, ACT.Sigmoid).then_inc(gge.sem, 1)
                elif kind == "evac_gate":
                    act.wait_ge(cgx.sem, cgx.after(2, 3 * st.cg + 2))
                    if st.cg >= 2:
                        act.wait_ge(ct.sem, ct.after(2, st.cg - 2))
                    act.activation(FF[:, 5 + st.m % 2, :], FF[:, 3 + st.m % 2, :], ACT.Silu).then_inc(cge.sem, 1)
                elif kind == "evac_cup":
                    act.wait_ge(ct.sem, ct.after(2, st.cu))
                    act.activation(CHH[:, st.m, :], (FF[:, 7, :], TMP[:, 2, :])[st.m % 2], copy).then_inc(chh.sem, 1)
                elif kind == "evac_k2":
                    act.wait_ge(bank_free.sem, bank_free.after(2, st.j))
                    act.activation(K2H[:, st.m, :], TMP[:, 2 + st.kv % 2, :], copy).then_inc(kv_h.sem, 1)
                elif kind == "v2_turn":
                    act.wait_ge(v2_pe.sem, v2_pe.after(2, st.v2))
                    act.activation(V2H[:, :, st.m * P:(st.m + 1) * P], BANK[2 + st.m % 2][:].rearrange("p (k n) -> p k n", k=KT),
                                   copy).then_inc(v2_h.sem, 1)
                elif kind == "evac_q2":
                    act.wait_ge(bank_free.sem, bank_free.after(2, st.j))
                    act.activation(Q2H[:, st.m, :], TMP[:, 2 + st.m % 2, :], copy).then_inc(q2_h.sem, 1)
                elif kind == "sb_scores":
                    act.wait_ge(za.sem, za.after(2, 3 * st.h))
                    act.activation(SBZ[:, 0:SEQ], SBZ[:, 0:SEQ], ACT.Exp).then_inc(ze.sem, 1)
                elif kind == "sb_sum":
                    act.wait_ge(za.sem, za.after(2, 3 * st.h + 2))
                    act.activation(SBZ[:, SEQ:], SBZ[:, SEQ:], ACT.Exp).then_inc(ze.sem, 1)
                    act.wait_ge(ze.sem, ze.after(2, 2 * st.h + 1))
                    act.activation(SBZ[:], SBZ[:], ACT.Ln, bias=1.0).then_inc(zl.sem, 1)
                elif kind == "sb_cut":
                    act.wait_ge(zs.sem, zs.after(2, st.h))
                    if st.h:
                        act.wait_ge(w.sem, w.after(2, st.h - 1))
                    act.activation(SPH[:], SBS[:], copy).then_inc(z_h.sem, 1)
                elif kind == "sb_weights":
                    act.wait_ge(w.sem, w.after(2, st.h))
                    if st.h >= 3:
                        act.wait_ge(o.sem, o.after(2, st.h - 3))
                    for k, n in enumerate((SEQ, SEQ, SEQ // 2)):
                        ins = act.activation(SBW[st.h % 3][:, SEQ * k:SEQ * k + n], BANK[3 * (st.h % 2) + k][:, 0:n], ACT.Exp)
                    ins.then_inc(we.sem, 1)
                elif kind == "sb_weights_hi":
                    act.wait_ge(we.sem, we.after(2, st.h))
                    act.activation(WTH[st.h % 3][:], SBW[st.h % 3][:], copy).then_inc(w_h.sem, 1)
                elif kind == "sb_out_cut":
                    rows = slice(st.h % 2 * HD, st.h % 2 * HD + HD)
                    act.wait_ge(o.sem, o.after(2, st.h))
                    act.activation(Q2H[rows, st.h // 2, :], BANK[6 + st.h % 2][rows, :], copy).then_inc(o_h.sem, 1)
                elif kind == "final":
                    act.preload_act_table_set(LOG_EXP)
                    norm(2, st, None, total_of(st))
                    stat(2, st)

            act.preload_act_table_set(LOG_EXP)
            act.wait_ge(mat_in, 64)
            act.activation(MATR[:].rearrange("p k n -> p (k n)"), FF[:, 0, 0:4 * P], ACT.Copy).then_inc(mats_cut, 1)
            act.sem_inc(expd.sem, 2)
            cut(0, 0, SLOT)
            with act.Fori(0, LAYERS) as l:
                for st in LAYER.steps:
                    step(l, st)
            for st in SECOND.steps:
                second(st)

        @block.vector
        def _(dve):
            def cut_next(l, st, sizes):
                for n in range(len(st.kt)):
                    c = st.c + n + 1
                    if sizes[c]:
                        cut(l, c, sizes[c])

            def cut(l, c, size):
                dve.wait_ge(hi.sem, hi.after(l, c))
                dve.tensor_tensor(slot_words(WL, c % CUT, size), slot_words(RAWW, c % RAW, size),
                                  f32(slot_words(WH, c % CUT, size)), ALU.subtract).then_inc(lo.sem, 1)

            def rest(dst, src, h):
                return dve.tensor_tensor(dst, src, f32(h), ALU.subtract)

            def gained_rest(l, st, gain):
                for k in range(DT):
                    dve.wait_ge(uh.sem, uh.after(l, st.n + k))
                    dve.scalar_tensor_tensor(UL[:, k, :], X[:, k, :], gain[:, k:k + 1], f32(UH[:, k, :]),
                                             ALU.mult, ALU.subtract).then_inc(ul.sem, 1)

            def from_bank(l, st):
                dve.wait_ge(used.sem, used.after(l, st.done))
                return BANK[st.j % 2]

            def times_rstd(l, st, dst, rows=P):
                b = from_bank(l, st)
                return dve.tensor_tensor(dst, b[0:rows, :], RSTD[0:rows, :], ALU.mult).then_inc(bank_free.sem, 1)

            def step(l, st):
                kind = st.kind
                if kind in ("mm", "mla_mm"):
                    cut_next(l, st, LAYER_WORDS)
                elif kind in ("norm", "regain"):
                    gained_rest(l, st, LP[:, st.gain:st.gain + DT])
                elif kind == "stat":
                    dve.wait_ge(rstd.sem, rstd.after(l, st.g))
                elif kind in ("evac_q", "evac_k", "evac_v"):
                    times_rstd(l, st, TMP[:, 2 + st.x % 2, :])
                elif kind in ("evac_cq", "evac_ckv"):
                    t = TMP[:, 2 + st.x % 2, :]
                    times_rstd(l, st, t)
                    k, gain = small_input(st)
                    dve.wait_ge(c_h.sem, c_h.after(l, st.cn))
                    dve.wait_ge(bank_free.sem, bank_free.after(l, st.j))
                    dve.scalar_tensor_tensor(CL[:, k, :], t, gain, f32(CH[:, k, :]), ALU.mult, ALU.subtract
                                             ).then_inc(c_l.sem, 1)
                elif kind == "evac_kr":
                    b = from_bank(l, st)
                    dve.wait_ge(rot_l.sem, rot_l.after(l, st.rot - 2))
                    dve.tensor_tensor(FF[0:QK, 6 + st.rot % 2, :], b[0:QK, :], RSTD[0:QK, :], ALU.mult
                                      ).then_inc(bank_free.sem, 1)
                elif kind == "mla_evac":
                    dve.wait_ge(used.sem, used.after(l, st.done))
                    if st.h == 0:
                        dve.wait_ge(rstd.sem, rstd.after(l, RC_LAST))
                    dve.wait_ge(rot_l.sem, rot_l.after(l, st.rot - 2))
                    dve.scalar_tensor_tensor(FF[0:QK, 6 + st.rot % 2, :], BANK[st.j % 2][0:QK, :], QK ** -0.5, RCQ[0:QK, :],
                                             ALU.mult, ALU.mult).then_inc(bank_free.sem, 1)
                    dve.tensor_tensor(KVF[:, st.h % 2, :], BANK[(st.j + 1) % 2][:], RKV[:], ALU.mult
                                      ).then_inc(bank_free.sem, 1)
                elif kind == "turn_in":
                    rows = slice(0, st.rows)
                    src, a = FF[rows, 6 + st.rot % 2, :], FF[rows, 4 + st.rot % 2, :]
                    if st.what in "qk":
                        gain = G_Q if st.what == "q" else G_K
                        dve.wait_ge(rstd.sem, rstd.after(l, st.g))
                        if st.rot >= 2:
                            dve.wait_ge(rot_l.sem, rot_l.after(l, st.rot - 2))
                        dve.scalar_tensor_tensor(src, TMP[:, 2 + st.x % 2, :], LP[:, gain:gain + 1], a, ALU.mult, ALU.mult
                                                 ).then_inc(turned_in.sem, 1)
                    dve.wait_ge(rh.sem, rh.after(l, st.rot))
                    rest(RL[rows, :], src, RH[rows, :]).then_inc(rl.sem, 1)
                elif kind == "turn":
                    rows = slice(0, st.rows)
                    b = sine(st)[rows, :]
                    dve.wait_ge(turn.sem, turn.after(l, st.b))
                    if st.rot == 0:
                        dve.wait_ge(tab_in, l * 16 + 16)
                    sin = FF[rows, 1 if st.what in "qk" else 3, :]
                    dve.tensor_tensor(b, TURN[rows, :], sin, ALU.mult).then_inc(turn_free.sem, 1)
                elif kind == "turn_out":
                    dests, rows = rot_dest(st)
                    dve.wait_ge(rdone.sem, rdone.after(l, st.rot))
                    dve.wait_ge(rot_h.sem, rot_h.after(l, st.rot))
                    for h, lo_ in dests:
                        ins = rest(lo_, FF[rows, 6 + st.rot % 2, :], h)
                    ins.then_inc(rot_l.sem, 1)
                elif kind == "gqa_v":
                    dve.wait_ge(v_h.sem, v_h.after(l, st.vh))
                    rest(VL[:].rearrange("p k n -> p (k n)"), TURN[:], VH[:].rearrange("p k n -> p (k n)")
                         ).then_inc(turn_free.sem, 1)
                elif kind == "mla_v":
                    dve.wait_ge(v_h.sem, v_h.after(l, st.vh))
                    a = st.h % 2 * HD
                    rest(MVL[:, st.h % 2, :, a:a + HD], TURN[:].rearrange("p (k n) -> p k n", k=KT)[:, :, HD:P],
                         MVH[:, st.h % 2, :, a:a + HD]).then_inc(turn_free.sem, 1)
                elif kind == "S":
                    r = st.u % 4
                    dve.wait_ge(scores.sem, scores.after(l, st.u))
                    dve.tensor_reduce(STAT[:, 0, r:r + 1], BANK[2 + st.u % 2][:], AX_X, ALU.max, negate=True
                                      ).then_inc(row_max.sem, 1)
                elif kind == "N":
                    r = st.u % 4
                    dve.wait_ge(expd.sem, expd.after(l, st.u))
                    dve.reciprocal(STAT[:, 2, r:r + 1], STAT[:, 1, r:r + 1]).then_inc(recip.sem, 1)
                elif kind == "L":
                    dve.wait_ge(probs_h.sem, probs_h.after(l, st.u))
                    at_ = (slice(None), st.h % 2, slice(None), slice(st.t * P, (st.t + 1) * P))
                    rest(PHL[at_], BANK[4 + st.u % 2][:].rearrange("p (k q) -> p k q", k=KT), PHH[at_]
                         ).then_inc(probs_l.sem, 1)
                elif kind == "PV_out":
                    h, lo_, rows, k = pv_place(st.h)
                    dve.wait_ge(y_h.sem, y_h.after(l, st.pv))
                    rest(lo_[rows, k, :], OUTB[rows, :], h[rows, k, :]).then_inc(y_l.sem, 1)
                elif kind in ("evac_ga", "evac_gb"):
                    b = from_bank(l, st)
                    dve.tensor_tensor(FF[:, 2 * (kind == "evac_gb") + st.m % 2, :], b[:], RSTD[:], ALU.mult
                                      ).then_inc(bank_free.sem, 1)
                elif kind in ("evac_br_a", "evac_br_b"):
                    b, n = from_bank(l, st), kind == "evac_br_b"
                    g = FF[:, 2 * n + st.m % 2, :]
                    dve.wait_ge(gate.sem, gate.after(l, 2 * st.m + n))
                    dve.tensor_tensor(FF[:, 4 + 2 * n + st.m % 2, :], b[:], g, ALU.mult).then_inc(bank_free.sem, 1)
                elif kind == "merge":
                    dve.wait_ge(merged_h.sem, merged_h.after(l, st.mg))
                    rest(ML[:, st.m, :], FF[:, 4 + st.m % 2, :], MH[:, st.m, :]).then_inc(merged_l.sem, 1)
                elif kind == "evac_ff":
                    b = from_bank(l, st)
                    if st.add:
                        dve.tensor_tensor(FF[:, st.m, :], b[:], FF[:, st.m, :], ALU.add).then_inc(bank_free.sem, 1)
                    else:
                        dve.tensor_copy(FF[:, st.m, :], b[:]).then_inc(bank_free.sem, 1)
                elif kind == "post":
                    dve.wait_ge(rstd.sem, rstd.after(l, st.g))
                    for k in range(DT):
                        dve.tensor_tensor(FF[:, k, :], FF[:, k, :], RCQ[:], ALU.mult).then_inc(scaled.sem, 1)
                    for k in range(DT):
                        dve.wait_ge(scaled.sem, scaled.after(l, st.sc + k))
                        dve.scalar_tensor_tensor(X[:, k, :], FF[:, k, :], LP[:, st.gain + k:st.gain + k + 1], X[:, k, :],
                                                 ALU.mult, ALU.add).then_inc(x_done.sem, 1)
                elif kind == "evac_up":
                    b = from_bank(l, st)
                    t = TMP[:, 2 + st.m % 2, :]
                    if st.up >= 2:
                        dve.wait_ge(hid_f.sem, hid_f.after(l, st.up - 2))
                        dve.wait_ge(hid_h.sem, hid_h.after(l, st.up - 2))
                    dve.scalar_tensor_tensor(t, b[:], 0.0, RSTD[:], ALU.max, ALU.mult).then_inc(bank_free.sem, 1)

            def second(st):
                kind = st.kind
                if kind == "mm":
                    cut_next(2, st, SECOND_WORDS)
                elif kind in ("norm", "regain"):
                    g = S_GAIN[st.gain]
                    gained_rest(2, st, SP_[:, g:g + DT])
                elif kind == "stat":
                    dve.wait_ge(rstd.sem, rstd.after(2, st.g))
                elif kind == "evac_u":
                    times_rstd(2, st, S5U[:, st.m, :])
                elif kind == "s5_params2":
                    dve.wait_ge(sp_pool.sem, 18)
                    dve.reciprocal(s5a(18), s5a(13)).then_inc(sp_dve.sem, 1)
                elif kind == "s5_grid":
                    number = S5N[:].unsqueeze(1).to_broadcast([P, PAIRS, COARSE + FINE])
                    k, kh, kl = (a.unsqueeze(2).to_broadcast([P, PAIRS, COARSE + FINE]) for a in (s5a(5), f32(S5AR[:]), s5a(6)))
                    dve.wait_ge(s5_in, 48)
                    dve.wait_ge(sp_pool.sem, 13)
                    dve.tensor_tensor(GRIDA[:], number, k, ALU.mult).then_inc(grid.sem, 1)
                    dve.tensor_tensor(GRID[:], number, kh, ALU.mult).then_inc(grid.sem, 1)
                    dve.tensor_tensor(GRIDB[:], number, kl, ALU.mult).then_inc(grid.sem, 1)
                    dve.wait_ge(grid.sem, 1)
                    dve.tensor_scalar(GRIDA[:], GRIDA[:], MAGIC, None, ALU.add).then_inc(grid.sem, 1)
                    dve.wait_ge(grid.sem, 4)
                    dve.tensor_scalar(GRIDA[:], GRIDA[:], MAGIC, None, ALU.subtract).then_inc(grid.sem, 1)
                    dve.wait_ge(grid.sem, 5)
                    dve.tensor_tensor(GRID[:], GRID[:], GRIDA[:], ALU.subtract).then_inc(grid.sem, 1)
                    dve.wait_ge(grid.sem, 6)
                    dve.tensor_tensor(GRID[:], GRID[:], GRIDB[:], ALU.add).then_inc(grid.sem, 1)
                    dve.wait_ge(grid.sem, 7)
                    dve.tensor_scalar(GRID[:], GRID[:], 0.5, -0.5, ALU.min, ALU.max).then_inc(grid.sem, 1)
                    dve.wait_ge(grid.sem, 8)
                elif kind == "s5_table":
                    if st.p >= 2:
                        dve.wait_ge(ts.sem, ts.after(2, st.p - 2))
                    dve.tensor_tensor(S5T[:, 22 + st.p % 2, :].rearrange("p (a b) -> p a b", a=COARSE),
                                      GRID[:, st.p, 0:COARSE].unsqueeze(2).to_broadcast([P, COARSE, FINE]),
                                      GRID[:, st.p, COARSE:].unsqueeze(1).to_broadcast([P, COARSE, FINE]), ALU.add
                                      ).then_inc(tb.sem, 1)
                elif kind == "s5_rot":
                    a = [S5T[:, 4 * (st.p % 3) + k, :] for k in range(4)]
                    c, s = (S5T[:, 16 + 2 * (st.p % 3) + k, :] for k in range(2))
                    re, im = (BANK[2 + 2 * (st.p % 2) + k][:] for k in range(2))
                    dve.wait_ge(tba.sem, tba.after(2, 5 * st.p + 4))
                    if st.p >= 3:
                        dve.wait_ge(sn_q.sem, sn_q.after(2, 2 * (st.p - 3) + 1))
                        dve.wait_ge(ge_q.sem, ge_q.after(2, 2 * (st.p - 3) + 1))
                    dve.scalar_tensor_tensor(s, S5T[:, 24 + st.p % 2, :], 2.0, S5T[:, 22 + st.p % 2, :], ALU.mult, ALU.mult
                                             ).then_inc(ts.sem, 1)
                    dve.wait_ge(ts.sem, ts.after(2, st.p))
                    dve.wait_ge(ro_pe.sem, ro_pe.after(2, st.p))
                    if st.p >= 3:
                        dve.wait_ge(so.sem, so.after(2, st.p - 3))
                    for k, (b, v) in enumerate(((re, c), (im, s), (im, c), (re, s))):
                        dve.tensor_tensor(a[k], b, v, ALU.mult).then_inc(ro.sem, 1)
                elif kind == "s5_scan":
                    a = [S5T[:, 4 * (st.p % 3) + k, :] for k in range(4)]
                    r = [S5T[:, 12 + 2 * (st.p % 2) + k, :] for k in range(2)]
                    c, s = (S5T[:, 16 + 2 * (st.p % 3) + k, :] for k in range(2))
                    mag = s5a(7)[:, st.p:st.p + 1].to_broadcast([P, SEQ])
                    if st.p >= 2:
                        dve.wait_ge(sn_q.sem, sn_q.after(2, 2 * (st.p - 2) + 1))
                    for k in range(2):
                        dve.wait_ge(ro_sum.sem, ro_sum.after(2, 2 * st.p + k))
                        dve.tensor_tensor_scan(r[k], mag, a[2 * k], 0.0, ALU.mult, ALU.add).then_inc(sn.sem, 1)
                    dve.wait_ge(sn.sem, sn.after(2, 2 * st.p + 1))
                    dve.tensor_tensor(a[2], r[0], s, ALU.mult).then_inc(ge_q.sem, 1)
                    dve.tensor_tensor(a[3], r[1], c, ALU.mult).then_inc(ge_q.sem, 1)
                elif kind == "s5_gelu0":
                    dve.wait_ge(so.sem, so.after(2, 4 * st.m + 3))
                    dve.scalar_tensor_tensor(FF[:, 4 * (st.m % 2), :], S5U[:, st.m, :], SP_[:, S_D + st.m:S_D + st.m + 1],
                                             BANK[6 + st.m % 2][:], ALU.mult, ALU.add).then_inc(ys.sem, 1)
                elif kind == "s5_gelu2":
                    dve.wait_ge(ge_h.sem, ge_h.after(2, st.m))
                    rest(UL[:, st.m, :], FF[:, 4 * (st.m % 2) + 3, :], UH[:, st.m, :]).then_inc(ge_l.sem, 1)
                elif kind == "evac_glu_gate":
                    b = from_bank(2, st)
                    dve.tensor_copy(FF[:, st.m % 2, :], b[:]).then_inc(bank_free.sem, 1)
                elif kind == "evac_glu":
                    b, t = from_bank(2, st), FF[:, st.m % 2, :]
                    dve.wait_ge(gge.sem, gge.after(2, st.m))
                    dve.tensor_tensor(t, b[:], t, ALU.mult).then_inc(bank_free.sem, 1)
                    dve.wait_ge(bank_free.sem, bank_free.after(2, st.j))
                    dve.tensor_tensor(X[:, st.m, :], X[:, st.m, :], t, ALU.add).then_inc(x_done.sem, 1)
                elif kind == "evac_gate":
                    g, t = GATE[:, st.m % 2, :], FF[:, 3 + st.m % 2, :]
                    w_ = [SP_[:, S_CONV + (st.layer * C_TILES + st.m) * 4 + k:][:, 0:1] for k in range(4)]
                    if st.m < 2:
                        dve.memset(g[:, 0:2], 0.0)
                    times_rstd(2, st, g[:, 2:2 + SEQ])
                    dve.wait_ge(bank_free.sem, bank_free.after(2, st.j))
                    if st.cg >= 2:
                        dve.wait_ge(cge.sem, cge.after(2, st.cg - 2))
                    dve.tensor_scalar(t, g[:, 2:2 + SEQ], w_[2], w_[3], ALU.mult, ALU.add).then_inc(cgx.sem, 1)
                    dve.wait_ge(cgx.sem, cgx.after(2, 3 * st.cg))
                    dve.scalar_tensor_tensor(t, g[:, 1:1 + SEQ], w_[1], t, ALU.mult, ALU.add).then_inc(cgx.sem, 1)
                    dve.wait_ge(cgx.sem, cgx.after(2, 3 * st.cg + 1))
                    dve.scalar_tensor_tensor(t, g[:, 0:SEQ], w_[0], t, ALU.mult, ALU.add).then_inc(cgx.sem, 1)
                elif kind == "evac_cup":
                    u = (FF[:, 7, :], TMP[:, 2, :])[st.m % 2]
                    if st.cu >= 2:
                        dve.wait_ge(chl.sem, chl.after(2, st.cu - 2))
                    times_rstd(2, st, u)
                elif kind == "evac_res":
                    b = from_bank(2, st)
                    dve.tensor_tensor(X[:, st.m, :], b[:], X[:, st.m, :], ALU.add).then_inc(x_done.sem, 1)
                    dve.wait_ge(x_done.sem, x_done.after(2, st.x))
                    dve.sem_inc(bank_free.sem, 1)
                elif kind in ("evac_k2", "evac_v2"):
                    if 2 <= st.kv < DT + 2:
                        dve.wait_ge(kv_l.sem, kv_l.after(2, st.kv - 2))
                    elif st.kv >= DT + 2:
                        dve.wait_ge(v2_pe.sem, v2_pe.after(2, st.kv - 2 - DT))
                    times_rstd(2, st, TMP[:, 2 + st.kv % 2, :])
                    if kind == "evac_k2":
                        dve.wait_ge(kv_h.sem, kv_h.after(2, st.m))
                        rest(K2L[:, st.m, :], TMP[:, 2 + st.kv % 2, :], K2H[:, st.m, :]).then_inc(kv_l.sem, 1)
                elif kind == "v2_turn":
                    dst = (slice(None), slice(None), slice(st.m * P, (st.m + 1) * P))
                    dve.wait_ge(v2_h.sem, v2_h.after(2, st.v2))
                    rest(V2L[dst], BANK[2 + st.m % 2][:].rearrange("p (k n) -> p k n", k=KT), V2H[dst]).then_inc(v2_l.sem, 1)
                elif kind == "evac_q2":
                    b, t = from_bank(2, st), TMP[:, 2 + st.m % 2, :]
                    if st.q2 >= 2:
                        dve.wait_ge(q2_l.sem, q2_l.after(2, st.q2 - 2))
                    else:
                        dve.wait_ge(v2_pe.sem, v2_pe.after(2, DT - 2 + st.q2))
                    dve.scalar_tensor_tensor(t, b[:], HD ** -0.5, RSTD[:], ALU.mult, ALU.mult).then_inc(bank_free.sem, 1)
                    dve.wait_ge(q2_h.sem, q2_h.after(2, st.q2))
                    rest(Q2L[:, st.m, :], t, Q2H[:, st.m, :]).then_inc(q2_l.sem, 1)
                elif kind == "sb_scores":
                    dve.wait_ge(z.sem, z.after(2, st.h))
                    if st.h:
                        dve.wait_ge(zs.sem, zs.after(2, st.h - 1))
                    pieces = [(slice(SEQ * k, SEQ * k + n), BANK[3 * (st.h % 2) + k][:, 0:n])
                              for k, n in enumerate((SEQ, SEQ, SEQ // 2))]
                    for k, (cols, b) in enumerate(pieces):
                        dve.tensor_scalar(SBP[:, cols], b, 0.0, None, ALU.max).then_inc(zp.sem, 1)
                        dve.wait_ge(zp.sem, zp.after(2, 3 * st.h + k))
                        dve.scalar_tensor_tensor(SBZ[:, cols], SBP[:, cols], -2.0, b, ALU.mult, ALU.add).then_inc(za.sem, 1)
                elif kind == "sb_sum":
                    dve.wait_ge(zl.sem, zl.after(2, st.h))
                    if st.h:
                        dve.wait_ge(w.sem, w.after(2, st.h - 1))
                    dve.tensor_tensor(SBS[:], SBP[:], SBZ[:], ALU.add).then_inc(zs.sem, 1)
                elif kind == "sb_cut":
                    dve.wait_ge(z_h.sem, z_h.after(2, st.h))
                    rest(SPL[:], SBS[:], SPH[:]).then_inc(z_l.sem, 1)
                elif kind == "sb_weights_lo":
                    dve.wait_ge(w_h.sem, w_h.after(2, st.h))
                    rest(WTL[st.h % 3][:], SBW[st.h % 3][:], WTH[st.h % 3][:]).then_inc(w_l.sem, 1)
                elif kind == "sb_out_cut":
                    rows = slice(st.h % 2 * HD, st.h % 2 * HD + HD)
                    dve.wait_ge(o_h.sem, o_h.after(2, st.h))
                    rest(Q2L[rows, st.h // 2, :], BANK[6 + st.h % 2][rows, :], Q2H[rows, st.h // 2, :]).then_inc(o_l.sem, 1)
                elif kind == "final":
                    g = S_GAIN["final", 0]
                    dve.wait_ge(rstd.sem, rstd.after(2, st.g))
                    for k in range(DT):
                        dve.scalar_tensor_tensor(FF[:, k, :], X[:, k, :], SP_[:, g + k:g + k + 1], RSTD[:], ALU.mult, ALU.mult
                                                 ).then_inc(outs.sem, 1)

            dve.sem_inc(lo.sem, RAW)
            dve.sem_inc(bank_free.sem, 2)
            dve.sem_inc(turn_free.sem, 1)
            dve.sem_inc(probs_l.sem, 2)
            dve.wait_ge(x_in, 16 * DT)
            dve.sem_inc(x_done.sem, DT)
            cut(0, 0, SLOT)
            with dve.Fori(0, LAYERS) as l:
                for st in LAYER.steps:
                    step(l, st)
            for st in SECOND.steps:
                second(st)

        @block.tensor
        def _(pe):
            def product(out_, w, x_, start, stop, **how):
                nc.tensor.matmul(out_, w[0], x_[0], start=start, stop=False, **how)
                nc.tensor.matmul(out_, w[0], x_[1], start=False, stop=False, **how)
                return nc.tensor.matmul(out_, w[1], x_[0], start=False, stop=stop, **how)

            inputs = {"u": (UH, UL), "merged": (MH, ML), "ya": (QH, QL), "yb": (YBH, YBL), "hidden": (HH, HL),
                      "s5": (UH, UL), "conv": (CHH, CHL), "y2": (Q2H, Q2L)}

            def linear_job(l, st, ready):
                xh, xl = inputs[st.rhs]
                pe.wait_ge(bank_free.sem, bank_free.room(l, st.j))
                n = len(st.kt)
                k0 = 0
                for i, kt in enumerate(st.kt):
                    c = st.c + i
                    pe.wait_ge(lo.sem, lo.after(l, c))
                    for k in range(kt):
                        if st.first:
                            pe.wait_ge(*ready(k0 + k))
                        cols = slice(k * st.cols, (k + 1) * st.cols)
                        ins = product(BANK[st.j % 2][0:st.cols, :], (WH[:, c % CUT, cols], WL[:, c % CUT, cols]),
                                      (xh[:, k0 + k, :], xl[:, k0 + k, :]), k0 + k == 0, i == n - 1 and k == kt - 1)
                    ins.then_inc(used.sem, 1)
                    k0 += kt

            def small_job(l, j, c, at_, kt, cols, k0):
                pe.wait_ge(bank_free.sem, bank_free.room(l, j))
                for k in range(kt):
                    w_ = slice(at_ + k * cols, at_ + (k + 1) * cols)
                    ins = product(BANK[j % 2][0:cols, :], (WH[:, c % CUT, w_], WL[:, c % CUT, w_]),
                                  (CH[:, k0 + k, :], CL[:, k0 + k, :]), k == 0, k == kt - 1)
                return ins

            def add_square(l, s, g, ones, first, last):
                if first and g >= 2:
                    pe.wait_ge(logged.sem, logged.after(l, g - 2))
                pe.wait_ge(sq.sem, sq.after(l, s))
                nc.tensor.matmul(stat_bank(g)[:], ones, TMP[:, s % 2, :], start=first, stop=last).then_inc(summed.sem, 1)

            def add_total(l, a, g, total, first):
                if first and g >= 2:
                    pe.wait_ge(logged.sem, logged.after(l, g - 2))
                pe.wait_ge(added.sem, added.after(l, a))
                nc.tensor.matmul(stat_bank(g)[:], ONES, total, start=first, stop=False)

            def stat(l, st, total):
                n = DT - 1 - ADDED
                for k in range(n):
                    if k == n - 1:
                        add_total(l, st.a + ADDED - 1, st.g, total, False)
                    add_square(l, st.s + k, st.g, ONES, k == 0, k == n - 1)

            state = {}

            def step(l, st):
                kind = st.kind
                if kind in ("norm", "regain"):
                    state["n"] = st.n
                elif kind == "mm":
                    n = state["n"]
                    ready = {"u": lambda k: (ul.sem, ul.after(l, n + k)),
                             "merged": lambda k: (merged_l.sem, merged_l.after(l, k)),
                             "ya": lambda k: (y_l.sem, y_l.after(l, 2 * HEADS - 1)),
                             "yb": lambda k: (y_l.sem, y_l.after(l, 2 * HEADS - 1)),
                             "hidden": lambda k: (hid_l.sem, hid_l.after(l, state["up"] - HALF + 1 + k))}[st.rhs]
                    linear_job(l, st, ready)
                elif kind == "evac_up":
                    state["up"] = st.up
                elif kind == "stat":
                    stat(l, st, SQUARES[:])
                elif kind in ("evac_q", "evac_k"):
                    add_square(l, st.s, st.group, ONES_HEAD, True, True)
                elif kind in ("evac_cq", "evac_ckv"):
                    add_square(l, st.s, st.group, ONES, st.i == 0, st.i == (CQT if kind == "evac_cq" else CKT) - 1)
                elif kind == "evac_ff" and st.s is not None:
                    add_total(l, st.last_a, st.group, SQUARES[:], True)
                    add_square(l, st.s, st.group, ONES, False, True)
                elif kind == "turn":
                    rot = ROT_A if st.what in "qk" else ROT_B
                    rows = slice(0, st.rows)
                    pe.wait_ge(rl.sem, rl.after(l, st.rot))
                    pe.wait_ge(turn_free.sem, turn_free.room(l, st.b))
                    nc.tensor.matmul(TURN[rows, :], rot[rows, rows], RH[rows, :], start=True, stop=False)
                    nc.tensor.matmul(TURN[rows, :], rot[rows, rows], RL[rows, :], start=False, stop=True
                                     ).then_inc(turn.sem, 1)
                elif kind == "gqa_v":
                    pe.wait_ge(bank_free.sem, bank_free.after(l, st.j))
                    pe.wait_ge(turn_free.sem, turn_free.room(l, st.b))
                    for k in range(KT):
                        ins = nc.tensor.transpose(TURN[:, k * P:(k + 1) * P], TMP[:, 2 + st.x % 2, k * P:(k + 1) * P], IDENT)
                    ins.then_inc(turn.sem, 1)
                elif kind == "mla_mm":
                    pe.wait_ge(lo.sem, lo.after(l, st.c))
                    if st.h == 0:
                        pe.wait_ge(c_l.sem, c_l.after(l, CQT + CKT - 1))
                    small_job(l, st.j, st.c, 0, CQT, QK, 0)
                    small_job(l, st.j + 1, st.c, CQT * QK, CKT, P, CQT).then_inc(used.sem, 1)
                elif kind == "mla_v":
                    pe.wait_ge(bank_free.sem, bank_free.after(l, st.j + 1))
                    pe.wait_ge(turn_free.sem, turn_free.room(l, st.b))
                    for k in range(KT):
                        ins = nc.tensor.transpose(TURN[:, k * P:(k + 1) * P], KVF[:, st.h % 2, k * P:(k + 1) * P], IDENT)
                    ins.then_inc(turn.sem, 1)
                elif kind == "S":
                    q = slice(st.t * P, (st.t + 1) * P)
                    if st.u == 0:
                        pe.wait_ge(rot_l.sem, rot_l.after(l, QT))
                        pe.wait_ge(logged.sem, logged.after(l, RC_LAST))
                    if st.h >= HEADS and st.t == 0:
                        pe.wait_ge(rot_l.sem, rot_l.after(l, QT + 2 + st.h - HEADS))
                        pe.wait_ge(mk_l.sem, mk_l.after(l, st.h - HEADS))
                    pe.wait_ge(expd.sem, expd.room(l, st.u))
                    if st.h < HEADS:
                        rows, i = slice(st.h // QT * HD, st.h // QT * HD + HD), st.h % QT
                        qs = QH[rows, i, q], QL[rows, i, q]
                        ks = KH[rows, :], KL[rows, :]
                    else:
                        i = st.h % 2
                        qs = MQH[0:QK, i, q], MQL[0:QK, i, q]
                        ks = MKH[0:QK, i, :], MKL[0:QK, i, :]
                    product(BANK[2 + st.u % 2][:], qs, ks, True, True).then_inc(scores.sem, 1)
                elif kind == "T":
                    pe.wait_ge(normed.sem, normed.after(l, st.u))
                    pe.wait_ge(probs_l.sem, probs_l.room(l, st.u))
                    for k in range(KT):
                        ins = nc.tensor.transpose(BANK[4 + st.u % 2][:, k * P:(k + 1) * P],
                                                  TMP[:, st.u % 4, k * P:(k + 1) * P], IDENT)
                    ins.then_inc(probs_t.sem, 1)
                elif kind == "PV":
                    if st.keys[0] == 0:
                        pe.wait_ge(probs_l.sem, probs_l.after(l, KT * st.h + KT - 1))
                        if st.h:
                            pe.wait_ge(y_l.sem, y_l.after(l, st.h - 1))
                        if st.h == HEADS:
                            pe.wait_ge(mv_zero, l + 1)
                    for k in st.keys:
                        v = (VH[:, k, :], VL[:, k, :]) if st.h < HEADS else (MVH[:, st.h % 2, k, :], MVL[:, st.h % 2, k, :])
                        ins = product(OUTB[:], v, (PHH[:, st.h % 2, k, :], PHL[:, st.h % 2, k, :]), k == 0, k == KT - 1)
                    if k == KT - 1:
                        ins.then_inc(pv.sem, 1)

            def second_pe(st):
                kind = st.kind
                if kind in ("norm", "regain"):
                    state["n"] = st.n
                elif kind == "mm":
                    n = state["n"]
                    ready = {"u": lambda k: (ul.sem, ul.after(2, n + k)),
                             "s5": lambda k: (ge_l.sem, ge_l.after(2, k)),
                             "conv": lambda k: (chl.sem, chl.after(2, state["cu"] - C_TILES + 1 + k)),
                             "y2": lambda k: (o_l.sem, o_l.after(2, 2 * k + 1))}[st.rhs]
                    linear_job(2, st, ready)
                    state["j"] = st.j
                elif kind == "evac_cup":
                    state["cu"] = st.cu
                elif kind in ("stat", "final"):
                    stat(2, st, total_of(st))
                elif kind == "s5_params3":
                    pe.wait_ge(sp_pool.sem, 34)
                    for k in range(4):
                        for t in range(4):
                            j = 4 * (4 * (k % 2) + t)
                            ins = nc.tensor.transpose(BANK[2 + k][:, t * P:(t + 1) * P],
                                                      S5BB[:, k // 2, j:j + 4, :].rearrange("p j h -> p (j h)"), IDENT)
                        ins.then_inc(sp_pe.sem, 1)
                elif kind == "s5_table":
                    rows = slice(32 * (st.p % 4), 32 * (st.p % 4) + 32)
                    if st.p == 0:
                        pe.wait_ge(sp_act.sem, 10)
                        pe.wait_ge(bank_free.sem, bank_free.after(2, DT - 1))
                    if st.p >= 2:
                        pe.wait_ge(ro.sem, ro.after(2, 4 * (st.p - 2) + 3))
                    for k in range(2):
                        ins = nc.tensor.matmul(BANK[2 + 2 * (st.p % 2) + k][:], BBT[rows, k, st.p // 4, :], S5U[rows, st.p // 4, :],
                                               start=True, stop=True)
                    ins.then_inc(ro_pe.sem, 1)
                elif kind == "s5_out":
                    rows = slice(32 * (st.p % 4), 32 * (st.p % 4) + 32)
                    t = st.p // 4
                    a = [S5T[:, 4 * (st.p % 3) + k, :] for k in range(4)]
                    if st.p % 4 == 0 and t >= 2:
                        pe.wait_ge(ys.sem, ys.after(2, t - 2))
                    pe.wait_ge(sn_q.sem, sn_q.after(2, 2 * st.p + 1))
                    pe.wait_ge(ge_q.sem, ge_q.after(2, 2 * st.p + 1))
                    for n, (k, part) in enumerate(((0, 0), (1, 0), (2, 2), (3, 1))):
                        ins = nc.tensor.matmul(BANK[6 + t % 2][rows, :], S5C[:, part, st.p, :], a[k],
                                               start=n == 0, stop=n == 3)
                    ins.then_inc(so.sem, 1)
                elif kind == "v2_turn":
                    pe.wait_ge(bank_free.sem, bank_free.after(2, st.j))
                    if st.m >= 2:
                        pe.wait_ge(v2_l.sem, v2_l.after(2, st.m - 2))
                    for k in range(KT):
                        ins = nc.tensor.transpose(BANK[2 + st.m % 2][:, k * P:(k + 1) * P],
                                                  TMP[:, 2 + st.kv % 2, k * P:(k + 1) * P], IDENT)
                    ins.then_inc(v2_pe.sem, 1)
                elif kind == "sb_scores":
                    rows = slice(st.h % 2 * HD, st.h % 2 * HD + HD)
                    i = st.h // 2
                    if st.h == 0:
                        pe.wait_ge(bank_free.sem, bank_free.after(2, state["j"]))
                        pe.wait_ge(v2_l.sem, v2_l.after(2, DT - 1))
                    pe.wait_ge(q2_l.sem, q2_l.after(2, i))
                    if st.h >= 2:
                        pe.wait_ge(we.sem, we.after(2, st.h - 2))
                    for k in (0, 1, 3, 2):
                        b, c = divmod(COL[k], SEQ)
                        product(BANK[3 * (st.h % 2) + b][:, c:c + WIDE[k]],
                                (K2H[rows, i, k * P:(k + 1) * P], K2L[rows, i, k * P:(k + 1) * P]),
                                (Q2H[rows, i, k * P:], Q2L[rows, i, k * P:]), k != 3, False, skip_group_check=True)
                        ins = nc.tensor.matmul(BANK[3 * (st.h % 2) + b][:, c:c + P], IDENT, MASK[:], start=False, stop=False,
                                               skip_group_check=True)
                    ins.then_inc(z.sem, 1)
                elif kind == "sb_weights":
                    pe.wait_ge(z_l.sem, z_l.after(2, st.h))
                    for k in range(KT):
                        b, c = divmod(COL[k], SEQ)
                        for k2 in range(k, KT):
                            mat = NEG_TRI if k2 == k else NEG_ONES
                            d = c + (k2 - k) * P
                            for part in (SPH, SPL):
                                ins = nc.tensor.matmul(BANK[3 * (st.h % 2) + b][:, d:d + WIDE[k2]], mat,
                                                       part[:, COL[k2]:COL[k2] + WIDE[k2]], start=False, stop=False,
                                                       skip_group_check=True)
                    ins.then_inc(w.sem, 1)
                elif kind == "sb_out":
                    pe.wait_ge(w_l.sem, w_l.after(2, st.h))
                    if st.h >= 2:
                        pe.wait_ge(o_l.sem, o_l.after(2, st.h - 2))
                    i = st.h // 2
                    for k in range(KT):
                        cols = slice(COL[k], COL[k] + WIDE[k])
                        ins = product(BANK[6 + st.h % 2][:, k * P:], (V2H[:, k, i * P:(i + 1) * P], V2L[:, k, i * P:(i + 1) * P]),
                                      (WTH[st.h % 3][:, cols], WTL[st.h % 3][:, cols]), k == 0, k == KT - 1, skip_group_check=True)
                    ins.then_inc(o.sem, 1)
            pe.wait_ge(mat_in, 64)
            pe.wait_ge(mats_cut, 1)
            pe.sem_inc(used.sem, CUT)
            pe.sem_inc(summed.sem, 2)
            pe.sem_inc(probs_t.sem, 4)
            with pe.Fori(0, LAYERS) as l:
                for st in LAYER.steps:
                    step(l, st)
            for st in SECOND.steps:
                second_pe(st)


def packed(w, k0, kt, c0, cols, rows=None):
    part = w[k0 * P:(k0 + kt) * P] if rows is None else w[rows]
    return part[:, c0:c0 + cols].reshape(kt, P, cols).transpose(1, 0, 2).reshape(P, kt * cols)


def weight_stream(w):
    chunks = []

    def whole(matrix, c0, n, cols=P):
        for m in range(n):
            chunks.append(packed(matrix, 0, matrix.shape[0] // P, c0 + m * cols, cols))

    paired = np.concatenate([np.arange(h * HD, h * HD + HD) for i in range(QT) for h in (i, QT + i)])
    for l in range(LAYERS):
        w_in = w["w_in"][l]
        q_pairs = w_in[:, paired]
        whole(q_pairs, 0, QT)
        kv0 = HEADS * HD
        low0 = kv0 + 2 * KV_HEADS * HD
        rope0 = low0 + Q_RANK + KV_RANK
        gate0 = rope0 + ROPE
        whole(w_in, kv0, 2)
        whole(w_in, low0, CQT + CKT)
        whole(w_in, rope0 - HD, 1, QK)
        for h in range(HEADS):
            chunks.append(np.concatenate([packed(w["w_q_up"][l], 0, CQT, h * QK, QK),
                                          packed(w["w_kv_up"][l], 0, CKT, h * P, P)], axis=1))
        for m in range(DT):
            whole(w_in, gate0 + m * P, 1)
            whole(w_in, gate0 + DM + m * P, 1)
            chunks.append(packed(w["w_branch_a"][l], 0, QT, m * P, P, rows=paired))
            chunks.append(packed(w["w_branch_b"][l], 0, QT, m * P, P))
        whole(w["w_o"][l], 0, DT)
        for half in range(2):
            whole(w["w_ffn_up"][l], half * HALF * P, HALF)
            for m in range(DT):
                for k in range(2):
                    chunks.append(packed(w["w_ffn_down"][l], half * HALF + k * DT, DT, m * P, P))

    def conv_ffn(layer):
        up, down = w["ffn_w_up_2"][layer], w["ffn_w_down_2"][layer]
        for m in range(C_TILES):
            whole(up, m * P, 1)
            whole(up, (C_TILES + m) * P, 1)
        for m in range(DT):
            for k0 in range(0, C_TILES, DT):
                chunks.append(packed(down, k0, min(DT, C_TILES - k0), m * P, P))

    whole(w["ssm_w_in_2"][0], 0, DT)
    for m in range(DT):
        whole(w["ssm_w_glu_2"][0], DM + m * P, 1)
        whole(w["ssm_w_glu_2"][0], m * P, 1)
    conv_ffn(0)
    whole(w["kv_w_2"], 0, 2 * DT)
    whole(w["attn_w_q_2"][0], 0, DT)
    whole(w["attn_w_o_2"][0], 0, DT)
    conv_ffn(1)
    stream = np.zeros((CHUNKS, P, SLOT), np.float32)
    assert len(chunks) == CHUNKS
    for c, chunk in enumerate(chunks):
        stream[c, :, :chunk.shape[1]] = chunk
    return stream


def by_tile(v):
    return v.reshape(-1, P).T


def layer_parameters(w):
    rows = []
    for l in range(LAYERS):
        cols = [by_tile(w[k][l]) for k in ("pre_mix_g", "post_mix_g", "pre_ffn_g", "post_ffn_g", "b_gate")]
        cols += [np.tile(w[k][l], 2)[:, None] for k in ("q_norm_g", "k_norm_g")]
        cols += [by_tile(w[k][l]) for k in ("q_a_norm_g", "kv_a_norm_g")]
        rows.append(np.concatenate(cols, axis=1))
    return np.stack(rows)


def by_pair(v):
    return v.reshape(PAIRS, 2 * STATE).T


def second_parameters(w):
    cols = [by_tile(w["norm_mix_2"][0]), by_tile(w["norm_mix_2"][1]), by_tile(w["norm_ffn_2"][0]),
            by_tile(w["norm_ffn_2"][1]), by_tile(w["norm_kv_2"]), by_tile(w["norm_final_2"]),
            by_tile(w["ssm_d_2"][0].reshape(-1))]
    for layer in range(LAYERS):
        taps = [by_tile(w["ffn_conv_w_2"][layer, k, 0]) for k in range(3)] + [by_tile(w["ffn_conv_b_2"][layer])]
        cols.append(np.stack(taps, axis=2).reshape(P, C_TILES * 4))
    cols += [by_pair(w["ssm_a_re_2"][0]), by_pair(w["ssm_a_im_2"][0]),
             by_pair(np.repeat(w["ssm_log_dt_2"][0][:, None], STATE, axis=1))]
    return np.concatenate(cols, axis=1)


def pair_blocks(v):
    wide = np.zeros((2, STATE, PAIRS, 2, GH), np.float32)
    for g in range(2):
        wide[g, :, :, g, :] = v[g::2].transpose(1, 0, 2)
    return wide.reshape(P, PAIRS * 2 * GH)


def rotation(dim, at_):
    m = np.zeros((P, P), np.float32)
    quarter = dim // 4
    for a in at_:
        for half in (a, a + dim // 2):
            for k in range(quarter):
                m[half + quarter + k, half + k] = -1.0
                m[half + k, half + quarter + k] = 1.0
    return m


def angles(dim):
    token = np.arange(SEQ)
    row, col = (token // GRID_W).astype(np.float32), (token % GRID_W).astype(np.float32)
    half = dim // 2
    inv = np.float32(ROPE_THETA) ** (-np.arange(0, half, 2, dtype=np.float32) / np.float32(half))
    ar, ac = row[:, None] * inv[None], col[:, None] * inv[None]
    a = np.concatenate([ar, ar, ac, ac], axis=1).T
    return np.cos(a).astype(np.float32), np.sin(a).astype(np.float32)


def constants():
    eye, ones = np.eye(P, dtype=np.float32), np.ones((P, P), np.float32)
    ones_head = np.kron(np.eye(2, dtype=np.float32), np.ones((HD, HD), np.float32))
    mats = [eye, ones, ones_head, rotation(HD, (0, HD)), rotation(ROPE, (HD,)), -np.tril(ones), -ones,
            HIDDEN * np.tril(ones)]
    cos_a, sin_a = angles(HD)
    tables = np.zeros((4, P, SEQ), np.float32)
    tables[0], tables[1] = np.tile(cos_a, (2, 1)), np.tile(sin_a, (2, 1))
    tables[2] = 1.0
    tables[2, HD:QK], tables[3, HD:QK] = angles(ROPE)
    steps = np.tile(np.concatenate([FINE * np.arange(COARSE), np.arange(FINE)]).astype(np.float32), (P, 1))
    return np.concatenate(mats, axis=1), tables, steps


def kernel(**inputs):
    import concourse.bacc as _bacc
    from concourse.bass_utils import run_bass_kernel_spmd as _run

    w = {name: np.asarray(a) for name, a in inputs.items()}
    mats, tables, steps = constants()
    arrays = {
        "weights": weight_stream(w),
        "x": np.ascontiguousarray(w["x"][0].T).reshape(DT, P, SEQ),
        "layer_params": layer_parameters(w),
        "second_params": second_parameters(w),
        "mats": mats,
        "tables": tables,
        "steps_t": steps,
        "s5_b": np.stack([pair_blocks(w["ssm_b_re_2"][0]), pair_blocks(w["ssm_b_im_2"][0])]),
        "s5_c": np.stack([pair_blocks(w[k][0].transpose(0, 2, 1)) for k in ("ssm_c_re_2", "ssm_c_im_2")]),
    }
    arrays = {name: np.ascontiguousarray(a, dtype=np.float32) for name, a in arrays.items()}
    nc = _bacc.Bacc("TRN2", target_bir_lowering=False, num_devices=1)
    args = {name: nc.dram_tensor(name, a.shape, F32, kind="ExternalInput").ap() for name, a in arrays.items()}
    out = nc.dram_tensor("out", (DT, P, SEQ), F32, kind="ExternalOutput").ap()
    build(nc, out=out, **args)
    r = _run(nc, [arrays], core_ids=[0])
    return np.ascontiguousarray(r.results[0]["out"].reshape(DM, SEQ).T)[None]
```

```python
import math
from contextlib import ExitStack

import numpy as np

import concourse.bass as bass
from concourse import mybir

F32 = mybir.dt.float32
F32R = mybir.dt.float32r
ALU = mybir.AluOpType
ACT = mybir.ActivationFunctionType
AX_X = mybir.AxisListType.X

P = 128
SEQ = 512
DM = 1024
DT = DM // P
LAYERS = 2
EPS = 1e-6
KT = SEQ // P
GRID_W = 64
ROPE_THETA = 10000.0

HEADS = 8
HD = 64
KV_HEADS = 2
QT = HEADS * HD // P
ROPE = 32
QK = HD + ROPE
Q_RANK, KV_RANK = 384, 256
CQT, CKT = Q_RANK // P, KV_RANK // P
FF_TILES = 4096 // P
HALF = FF_TILES // 2
SLOT = 8 * P

C_TILES = 2816 // P
COARSE, FINE = 16, 32
GROUPS, STATE, GH = 64, 64, 16
PAIRS = GROUPS // 2
H2 = 16
HIDDEN = -2.0 ** 100
SIN_TANH = "silu_and_others"
LOG_EXP = "natural_log_exp_and_others"
MAGIC = 1.5 * 2.0 ** 23
INV2PI = 1.0 / (2.0 * math.pi)
PI_A, PI_B = 6.28125, 0.0019350051879882812
PI_C = 2.0 * math.pi - PI_A - PI_B
CHUNKS_L = 116
CHUNKS = 2 * CHUNKS_L + 192

RAW = 4
CUT = 2


RC_LAST, POST_MIX, POST_FFN = 3 + QT, 4 + QT, 6 + QT


ADDED = 4
SCALED = 5
POST = f"g x:{DT} sc:{SCALED} sp:{DT - SCALED}"
NORM = f"n:{DT} f a:{ADDED} s:{DT - 1 - ADDED}"


class Signal:

    def __init__(self, sem, per_layer, slots=0):
        self.sem, self.per_layer, self.slots = sem, per_layer, slots

    def after(self, l, k):
        return l * self.per_layer + (k + 1 + self.slots)

    def room(self, l, k):
        return l * self.per_layer + (k + 1)


class Step:

    def __init__(self, kind, a=None, add=None, at=None, b=None, c=None, cg=None, cn=None, cols=None, cu=None, done=None,
                 eu=None, f=None, ff=None, first=None, g=None, gain=None, ge=None, gg=None, group=None, h=None,
                 half=None, hf=None, i=None, j=None, keys=None, kt=None, kv=None, last_a=None, last_f=None,
                 last_s=None, last_use=None, layer=None, m=None, mg=None, mk=None, mt=None, n=None, o=None, p=None,
                 pv=None, q2=None, qk=None, rhs=None, ro=None, rot=None, rows=None, s=None, sc=None, sn=None,
                 so=None, sp=None, stat=None, sums=None, t=None, tb=None, turn_before=None, u=None, up=None,
                 v2=None, version=None, vh=None, what=None, x=None, z=None):
        self.kind, self.a, self.add, self.at, self.b, self.c, self.cg, self.cn = kind, a, add, at, b, c, cg, cn
        self.cols, self.cu, self.done, self.eu, self.f, self.ff, self.first, self.g = cols, cu, done, eu, f, ff, first, g
        self.gain, self.ge, self.gg, self.group, self.h, self.half, self.hf, self.i = gain, ge, gg, group, h, half, hf, i
        self.j, self.keys, self.kt, self.kv, self.last_a, self.last_f, self.last_s, self.last_use = j, keys, kt, kv, last_a, last_f, last_s, last_use
        self.layer, self.m, self.mg, self.mk, self.mt, self.n, self.o, self.p = layer, m, mg, mk, mt, n, o, p
        self.pv, self.q2, self.qk, self.rhs, self.ro, self.rot, self.rows, self.s = pv, q2, qk, rhs, ro, rot, rows, s
        self.sc, self.sn, self.so, self.sp, self.stat, self.sums, self.t, self.tb = sc, sn, so, sp, stat, sums, t, tb
        self.turn_before, self.u, self.up, self.v2, self.version, self.vh, self.what, self.x = turn_before, u, up, v2, version, vh, what, x
        self.z = z


class Plan:

    def __init__(self):
        self.steps, self.total = [], {}

    def add(self, kind, take="", **info):
        at = {}
        for item in take.split():
            name, n = (item.split(":") + ["1"])[:2]
            at[name] = self.total.get(name, 0)
            self.total[name] = at[name] + int(n)
        step = Step(kind, **at, **info)
        self.steps.append(step)
        return step


def linear(plan, jobs, after, lag=1):
    mm = []
    for x in range(len(jobs) + lag):
        if x < len(jobs):
            if jobs[x].get("at"):
                mm.append(plan.add("mm", "j", first=False, c=mm[-1].c, **jobs[x]))
            else:
                mm.append(plan.add("mm", f"c:{len(jobs[x]['kt'])} j", first=x == 0, **jobs[x]))
        if x == 0 and after.get("stat"):
            norm = after["stat"]
            plan.add("stat", "g", f=norm.f, a=norm.a, s=norm.s, version=norm.version)
        if x >= lag:
            after["evac"](x - lag, mm[x - lag])


def done_of(mm):
    return mm.c + len(mm.kt) - 1


def attention_steps(plan):
    n = 2 * HEADS * KT
    mm = ev = None
    value_j = {}
    for x in range(n + 8):
        h, phase = divmod(x - KT - 4, KT)
        if 0 <= h < 2 * HEADS and phase == 3:
            plan.add("att_out_hi", h=h, pv=h)
        m, phase = divmod(x + 2 - (HEADS - 1) * KT, KT)
        if 1 <= m <= HEADS and phase == 1:
            plan.add("turn_out", **rotation)
        if x < n:
            plan.add("att_scores", "u", h=x // KT, t=x % KT)
        if 1 <= x <= n:
            plan.add("att_normalise", u=x - 1)
        if 3 <= x <= n + 2:
            plan.add("att_transpose", u=x - 3, h=(x - 3) // KT, t=(x - 3) % KT)
        h, phase = divmod(x - KT - 4, KT)
        if 0 <= h < 2 * HEADS and phase < 3:
            plan.add("att_values", "pv" if phase == 2 else "", h=h, keys=((0, 1), (2,), (3,))[phase])
        if 4 <= x <= n + 3:
            plan.add("att_lo", u=x - 4, h=(x - 4) // KT, t=(x - 4) % KT)
        if 0 <= h < 2 * HEADS and phase == 3:
            plan.add("att_out_lo", h=h, pv=h)
        m, phase = divmod(x + 2 - (HEADS - 1) * KT, KT)
        if 1 <= m <= HEADS and phase == 0:
            plan.add("turn", "b", **rotation)
        if 0 <= m < HEADS and phase == 0:
            mm = plan.add("mla_mm", "c j:2", h=m, kt=[None])
        if 2 <= m <= HEADS + 1 and phase == 1:
            plan.add("mla_v", "b vh", h=m - 2, j=value_j[m - 2])
        if 0 <= m < HEADS and phase == 1:
            ev = plan.add("mla_evac", "rot mk", h=m, j=mm.j, done=mm.c)
            value_j[m] = mm.j
            rotation = dict(what="mla", h=m, rot=ev.rot, j=ev.j, rows=QK)
        if 0 <= m < HEADS and phase == 2:
            plan.add("turn_in", **rotation)
            plan.add("mla_k", h=m, mk=ev.mk, j=ev.j)
        if 0 <= m < HEADS and phase == 3:
            plan.add("turn_rest", **rotation)


def plan_layer():
    plan = Plan()
    norm = plan.add("norm", NORM, gain=0, version=0)
    items = [("q", i) for i in range(QT)] + [("k", 0), ("v", 0)] + [("cq", i) for i in range(CQT)]
    items += [("ckv", i) for i in range(CKT)] + [("kr", 0)]
    ev = {}

    def first_products(x, mm):
        what, i = items[x]
        take = {"q": "s rot", "k": "s rot", "v": "", "cq": "s cn", "ckv": "s cn", "kr": "rot"}[what]
        group = {"q": 1 + i, "k": 1 + QT, "cq": 2 + QT, "ckv": 3 + QT}.get(what)
        ev[x] = plan.add("evac_" + what, take, i=i, x=x, j=mm.j, done=mm.c, group=group)
        if x >= 2:
            rotate("turn", x - 2)
        if x >= 1:
            finish(x - 1)
        if x >= 2:
            rotate("turn_out", x - 2)

    def rotate(kind, x):
        what, i = items[x]
        if what in ("q", "k", "kr"):
            take = "b" if kind == "turn" else "g qk" if kind == "turn_in" and what != "kr" else ""
            st = plan.add(kind, take, what=what, i=i, x=x, rot=ev[x].rot, s=ev[x].s, j=ev[x].j, h=0,
                          rows=QK if what == "kr" else P)

    def finish(x):
        what, i = items[x]
        rotate("turn_in", x)
        rotate("turn_rest", x)
        if what == "v":
            plan.add("gqa_v", "b vh", x=x, j=ev[x].j)
        elif (what, i) in (("cq", CQT - 1), ("ckv", CKT - 1)):
            plan.add("rc_" + what, "g", s=ev[x].s)

    jobs = [dict(kt=[DT], cols=QK if what == "kr" else P, rhs="u") for what, _ in items]
    linear(plan, jobs, dict(stat=norm, evac=first_products))
    finish(len(items) - 1)
    rotate("turn", len(items) - 1)
    rotate("turn_out", len(items) - 1)
    attention_steps(plan)
    plan.add("regain", "n:8", gain=0)

    def gates_and_branches(x, mm):
        what, m = ("ga", "gb", "br_a", "br_b")[x % 4], x // 4
        plan.add("evac_" + what, {"ga": "ge", "gb": "ge", "br_a": "hf", "br_b": "mt"}.get(what, ""), m=m, j=mm.j,
                 done=mm.c)
        if what == "gb" and m:
            plan.add("merge", "mg", m=m - 1)

    jobs = []
    for m in range(DT):
        jobs += [dict(kt=[DT], cols=P, rhs="u"), dict(kt=[DT], cols=P, rhs="u"),
                 dict(kt=[QT], cols=P, rhs="ya", half=m), dict(kt=[QT], cols=P, rhs="yb", at=QT)]
    linear(plan, jobs, dict(evac=gates_and_branches))
    plan.add("merge", "mg", m=DT - 1)

    def into_ff(add, group=None):
        def evac(x, mm):
            take = "" if group is None else "f" if x == 0 else "a" if x < DT - 1 else "s"
            plan.add("evac_ff", "ff " + take, m=x, j=mm.j, done=done_of(mm), add=add, group=group)
        return evac

    tile = dict(cols=P, kt=[DT])
    linear(plan, [dict(tile, rhs="merged")] * DT, dict(evac=into_ff(False, POST_MIX)))
    plan.add("post", POST, gain=8)
    norm = plan.add("norm", NORM, gain=16, version=1)
    for half in range(2):
        linear(plan, [dict(tile, rhs="u")] * HALF,
               dict(stat=None if half else norm,
                    evac=lambda x, mm: plan.add("evac_up", "up", m=x, j=mm.j, done=mm.c)))
        linear(plan, [dict(cols=P, kt=[DT, DT], rhs="hidden")] * DT, dict(evac=into_ff(half == 1, POST_FFN if half else None)))
    plan.add("post", POST, gain=24)
    return plan


def conv_ffn_steps(plan, layer, version):
    norm = plan.add("norm", NORM, gain=("ffn", layer), version=version)

    def hidden(x, mm):
        if x % 2 == 0:
            plan.add("evac_gate", "cg", m=x // 2, j=mm.j, done=mm.c, layer=layer)
        else:
            plan.add("evac_cup", "cu", m=x // 2, j=mm.j, done=mm.c)

    linear(plan, [dict(kt=[DT], cols=P, rhs="u")] * (2 * C_TILES), dict(stat=norm, evac=hidden))
    linear(plan, [dict(kt=[8, 8, 6], cols=P, rhs="conv")] * DT,
           dict(evac=lambda x, mm: plan.add("evac_res", "x", m=x, j=mm.j, done=done_of(mm))))


def plan_second():
    plan = Plan()
    tile = dict(kt=[DT], cols=P)
    norm = plan.add("norm", NORM, gain=("mix", 0), version=0)

    def ssm_input(x, mm):
        plan.add("evac_u", "eu", m=x, j=mm.j, done=mm.c)
        if x < 4:
            plan.add(f"s5_params{x}")
        if x >= 4:
            plan.add(f"s5_grid{x - 4}")

    linear(plan, [dict(tile, rhs="u")] * DT, dict(stat=norm, evac=ssm_input))
    plan.add("s5_factors")
    for x in range(PAIRS + 6):
        if x < PAIRS:
            plan.add("s5_table", "tb", p=x)
        if 1 <= x <= PAIRS:
            plan.add("s5_rot", "ro", p=x - 1)
        if 2 <= x <= PAIRS + 1:
            plan.add("s5_scan", "sn", p=x - 2)
        if 3 <= x <= PAIRS + 2:
            plan.add("s5_out", "so", p=x - 3)
        if x >= 7 and (x - 3) % 4 == 0:
            plan.add("s5_gelu0", "", m=(x - 7) // 4)
        if x >= 8 and (x - 4) % 4 == 0:
            plan.add("s5_gelu1", "", m=(x - 8) // 4)
        if x >= 9 and (x - 5) % 4 == 0:
            plan.add("s5_gelu2", "", m=(x - 9) // 4)

    def glu(x, mm):
        if x % 2 == 0:
            plan.add("evac_glu_gate", "gg", m=x // 2, j=mm.j, done=mm.c)
        else:
            plan.add("evac_glu", "x", m=x // 2, j=mm.j, done=mm.c)

    linear(plan, [dict(tile, rhs="s5")] * (2 * DT), dict(evac=glu))
    conv_ffn_steps(plan, 0, 1)
    norm = plan.add("norm", NORM, gain=("kv", 0), version=2)

    turns = {}

    def keys_and_values(x, mm):
        plan.add("evac_k2" if x < DT else "evac_v2", "kv", m=x % DT, j=mm.j, done=mm.c)
        turns[x] = mm.j
        if x > DT:
            plan.add("v2_turn", "v2", m=x - 1 - DT, kv=x - 1, j=turns[x - 1])

    linear(plan, [dict(tile, rhs="u")] * (2 * DT), dict(stat=norm, evac=keys_and_values))
    plan.add("v2_turn", "v2", m=DT - 1, kv=2 * DT - 1, j=turns[2 * DT - 1])
    plan.add("regain", "n:8", gain=("mix", 1))
    linear(plan, [dict(tile, rhs="u")] * DT,
           dict(evac=lambda x, mm: plan.add("evac_q2", "q2", m=x, j=mm.j, done=mm.c)))
    for x in range(H2 + 4):
        if x < H2:
            plan.add("sb_scores", "z", h=x)
        if x >= 4:
            plan.add("sb_out_cut", h=x - 4)
        if 2 <= x <= H2 + 1:
            plan.add("sb_weights_lo", h=x - 2)
        if x < H2:
            plan.add("sb_sum", h=x)
        if 1 <= x <= H2:
            plan.add("sb_weights", "sums", h=x - 1)
        if x < H2:
            plan.add("sb_cut", h=x)
        if 1 <= x <= H2:
            plan.add("sb_weights_hi", h=x - 1)
        if 3 <= x <= H2 + 2:
            plan.add("sb_out", "o", h=x - 3)
    linear(plan, [dict(tile, rhs="y2")] * DT,
           dict(evac=lambda x, mm: plan.add("evac_res", "x", m=x, j=mm.j, done=mm.c)))
    conv_ffn_steps(plan, 1, 3)
    plan.add("final", "f a:4 s:3 g", version=4)
    return plan


LAYER, SECOND = plan_layer(), plan_second()
for st in LAYER.steps:
    if st.kind == "evac_ff" and st.f is not None:
        last_f = st.f
    if st.kind == "evac_ff" and st.a is not None:
        st.last_f, last_a = last_f, st.a
    if st.kind == "evac_ff" and st.s is not None:
        st.last_a, last_s = last_a, st.s
    if st.kind == "post":
        st.last_s = last_s
last_use = None
for st in SECOND.steps:
    if st.kind in ("norm", "regain"):
        st.last_use = last_use
    elif st.kind == "mm" and st.rhs in ("u", "s5"):
        last_use = done_of(st)
turns = {st.rot: st.b for st in LAYER.steps if st.kind == "turn"}
for st in LAYER.steps:
    if st.kind == "turn_in" and st.rot:
        st.turn_before = turns[st.rot - 1]
assert LAYER.total["c"] == CHUNKS_L and LAYER.total["c"] + CHUNKS_L + SECOND.total["c"] == CHUNKS


def words(step):
    if step.kind == "mla_mm":
        return [CQT * QK + CKT * P]
    if step.half is not None:
        return [2 * k * step.cols for k in step.kt]
    return [] if step.at else [k * step.cols for k in step.kt]


LAYER_WORDS = [w for s in LAYER.steps if s.kind in ("mm", "mla_mm") for w in words(s)] + [SLOT]
SECOND_WORDS = [w for s in SECOND.steps if s.kind == "mm" for w in words(s)] + [0]

COL = [0, SEQ, 2 * SEQ, SEQ + 3 * P]
WIDE = [SEQ - P * k for k in range(KT)]

G_BIAS = 32
G_Q, G_K, G_CQ, G_CKV = 48, 49, 50, 53
N_LAYER_PARAMS = 55
S_GAIN = {("mix", 0): 0, ("mix", 1): 8, ("ffn", 0): 16, ("ffn", 1): 24, ("kv", 0): 32, ("final", 0): 40}
S_D, S_CONV, S_A = 48, 56, 56 + 2 * C_TILES * 4
N_SECOND_PARAMS = S_A + 3 * PAIRS
MATS = ("ident", "ones", "ones_head", "rot_a", "rot_b", "neg_tri", "neg_ones", "mask")


def build(nc, weights, x, layer_params, second_params, mats, tables, steps_t, s5_b, s5_c, out):
    ctx = ExitStack()
    with ctx:
        KB = 1024
        start = 16640
        fence = ctx.enter_context(nc.sbuf_tensor("fence", [P, 53120], F32))

        def at(name, kb, shape, dt=F32):
            return nc.alloc_sbuf_tensor_at(name, shape, dt, offset=start + int(kb * KB))

        X = at("X", 0, [P, DT, SEQ])
        RSTD = at("RSTD", 16, [P, SEQ])
        RAWW = at("RAWW", 18, [P, RAW, SLOT])
        WH = at("WH", 34, [P, CUT, SLOT], F32R)
        WL = at("WL", 42, [P, CUT, SLOT], F32R)
        UH = at("UH", 50, [P, DT, SEQ], F32R)
        UL = at("UL", 66, [P, DT, SEQ], F32R)
        PHH = at("PHH", 50, [P, 2, KT, SEQ], F32R)
        PHL = at("PHL", 66, [P, 2, KT, SEQ], F32R)
        FF = at("FF", 82, [P, DT, SEQ])
        TMP = at("TMP", 98, [P, 4, SEQ])
        A0 = 106
        QH = at("QH", A0, [P, QT, SEQ], F32R)
        QL = at("QL", A0 + 8, [P, QT, SEQ], F32R)
        KH = at("KH", A0 + 16, [P, SEQ], F32R)
        KL = at("KL", A0 + 18, [P, SEQ], F32R)
        VH = at("VH", A0 + 20, [P, KT, P], F32R)
        VL = at("VL", A0 + 22, [P, KT, P], F32R)
        CH = at("CH", A0 + 24, [P, CQT + CKT, SEQ], F32R)
        CL = at("CL", A0 + 34, [P, CQT + CKT, SEQ], F32R)
        MQH = at("MQH", A0 + 44, [P, 2, SEQ], F32R)
        MQL = at("MQL", A0 + 48, [P, 2, SEQ], F32R)
        MKH = at("MKH", A0 + 52, [P, 2, SEQ], F32R)
        MKL = at("MKL", A0 + 56, [P, 2, SEQ], F32R)
        MVH = at("MVH", A0 + 60, [P, 2, KT, P], F32R)
        MVL = at("MVL", A0 + 64, [P, 2, KT, P], F32R)
        YBH = at("YBH", A0 + 68, [P, QT, SEQ], F32R)
        YBL = at("YBL", A0 + 76, [P, QT, SEQ], F32R)
        RH = at("RH", A0 + 84, [P, SEQ], F32R)
        RL = at("RL", A0 + 86, [P, SEQ], F32R)
        RKV = at("RKV", A0 + 88, [P, SEQ])
        RCQ = at("RCQ", A0 + 90, [P, SEQ])
        SQUARES = at("SQUARES", A0 + 88, [P, SEQ])
        KVF = at("KVF", A0 + 92, [P, 2, SEQ])
        MH = at("MH", A0 + 24, [P, DT, SEQ], F32R)
        ML = at("ML", A0 + 40, [P, DT, SEQ], F32R)
        HH = at("HH", A0, [P, HALF, SEQ], F32R)
        HL = at("HL", A0 + 32, [P, HALF, SEQ], F32R)
        CHH = at("CHH", A0, [P, C_TILES, SEQ], F32R)
        CHL = at("CHL", A0 + 44, [P, C_TILES, SEQ], F32R)
        GATE = at("GATE", 82, [P, 2, 520])
        S5U = at("S5U", A0, [P, DT, SEQ])
        BBT = at("BBT", A0 + 16, [P, 2, DT, P])
        S5C = at("S5C", A0 + 24, [P, 3, PAIRS, 32])
        S5A = at("S5A", A0 + 36, [P, 24, PAIRS])
        S5AR = at("S5AR", A0 + 39, [P, PAIRS], F32R)
        S5N = at("S5N", A0 + 40, [P, COARSE + FINE])
        GRID = at("GRID", 100, [P, PAIRS, COARSE + FINE])
        GRIDA = at("GRIDA", A0 + 68, [P, PAIRS, COARSE + FINE])
        GRIDB = at("GRIDB", A0 + 74, [P, PAIRS, COARSE + FINE])
        S5B = at("S5B", A0 + 44, [P, 2, PAIRS, 32])
        S5BB = at("S5BB", A0 + 52, [P, 2, PAIRS, 32])
        S5BT = at("S5BT", A0 + 60, [P, 2, PAIRS, 32])
        S5T = at("S5T", A0 + 44, [P, 26, SEQ])
        K2H = at("K2H", A0, [P, DT, SEQ], F32R)
        K2L = at("K2L", A0 + 16, [P, DT, SEQ], F32R)
        V2H = at("V2H", A0 + 32, [P, KT, DM], F32R)
        V2L = at("V2L", A0 + 48, [P, KT, DM], F32R)
        Q2H = at("Q2H", A0 + 64, [P, DT, SEQ], F32R)
        Q2L = at("Q2L", A0 + 80, [P, DT, SEQ], F32R)
        TRI = SEQ * (KT + 1) * KT // 2 // KT
        SPH = at("SPH", 50, [P, TRI], F32R)
        SBS = at("SBS", 87, [P, TRI])
        SPL = at("SPL", 87, [P, TRI], F32R)
        SBZ = at("SBZ", 82, [P, TRI])
        SBP = at("SBP", 70, [P, TRI])
        WTH = [at(f"WTH{k}", kb, [P, TRI], F32R) for k, kb in enumerate((55, 60, 98))]
        SBW = [at(f"SBW{k}", kb, [P, TRI]) for k, kb in enumerate((65, 75, 92))]
        WTL = [at(f"WTL{k}", kb, [P, TRI], F32R) for k, kb in enumerate((65, 75, 92))]
        MAT = at("MAT", 202, [P, 3, P])
        MATR = at("MATR", 203.5, [P, 4, P], F32R)
        LP = at("LP", 205.5, [P, N_LAYER_PARAMS])
        MASK = at("MASK", 207.1875, [P, P])
        STAT = at("STAT", 205.8125, [P, 3, 4])
        SP_ = at("SP_", 205.875, [P, N_SECOND_PARAMS])
        IDENT, ONES, ONES_HEAD = (MAT[:, k, :] for k in range(3))
        ROT_A, ROT_B, NEG_TRI, NEG_ONES = (MATR[:, k, :] for k in range(4))

        BANK = [ctx.enter_context(nc.psum_tensor(f"bank{k}", [P, SEQ], F32)) for k in range(8)]
        OUTB, TURN = BANK[6], BANK[7]

        def stat_bank(g):
            return BANK[6 if g % 2 == 0 else 3]

        def signal(name, kind, slots=0):
            return Signal(ctx.enter_context(nc.semaphore(name)), LAYER.total.get(kind, 0), slots)

        raw_in = [ctx.enter_context(nc.semaphore(f"raw_in{k}")) for k in range(RAW)]
        hi = signal("hi", "c")
        lo = signal("lo", "c", RAW)
        used = signal("used", "c", CUT)
        half = signal("half", "hf")
        bank_free = signal("bank_free", "j", 2)
        x_in, par_in, mat_in, tab_in, s5_in, y_out = (ctx.enter_context(nc.semaphore(k)) for k in (
            "x_in", "par_in", "mat_in", "tab_in", "s5_in", "y_out"))
        mats_cut = ctx.enter_context(nc.semaphore("mats_cut"))
        mv_zero = ctx.enter_context(nc.semaphore("mv_zero"))
        x_done = signal("x_done", "x", DT)
        uh, ul = signal("uh", "n"), signal("ul", "n")
        sq = signal("sq", "s")
        summed = signal("summed", "s", 2)
        first_sq, sq_in = signal("first_sq", "f"), signal("sq_in", "a")
        added = signal("added", "a", 2)
        logged, rstd = signal("logged", "g"), signal("rstd", "g")
        scaled, scaled_pool = signal("scaled", "sc"), signal("scaled_pool", "sp")
        turned_in = signal("turned_in", "qk")
        rh, rl, rcos, rdone = signal("rh", "rot"), signal("rl", "rot"), signal("rcos", "rot"), signal("rdone", "rot")
        rot_h, rot_l = signal("rot_h", "rot"), signal("rot_l", "rot")
        turn, turn_free = signal("turn", "b"), signal("turn_free", "b", 1)
        v_h, c_h, c_l = signal("v_h", "vh"), signal("c_h", "cn"), signal("c_l", "cn")
        mk_h, mk_l = signal("mk_h", "mk"), signal("mk_l", "mk")
        scores, row_max = signal("scores", "u"), signal("row_max", "u")
        expd, recip = signal("expd", "u", 2), signal("recip", "u")
        normed, probs_t = signal("normed", "u"), signal("probs_t", "u", 4)
        probs_h, probs_l = signal("probs_h", "u"), signal("probs_l", "u", 2)
        pv, y_h, y_l = signal("pv", "pv"), signal("y_h", "pv"), signal("y_l", "pv")
        gate = signal("gate", "ge")
        merged, merged_h, merged_l = (signal(k, "mt") for k in ("merged", "merged_h", "merged_l"))
        hid_h, hid_f, hid_l = (signal(k, "up") for k in ("hid_h", "hid_f", "hid_l"))
        conv_sum, conv_gate, conv_prod, conv_h, conv_l = (signal(k, "") for k in (
            "conv_sum", "conv_gate", "conv_prod", "conv_h", "conv_l"))
        sp_pool, sp_act, sp_dve, sp_pe = (signal(k, "") for k in ("sp_pool", "sp_act", "sp_dve", "sp_pe"))
        grid, tb, trig, sine_done = (signal(k, "") for k in ("grid", "tb", "trig", "sine_done"))
        state_in, ro, rotated_in, sn = (signal(k, "") for k in ("state_in", "ro", "rotated_in", "sn"))
        out_pool, out_dve, s5_sum, s5_y = (signal(k, "") for k in ("out_pool", "out_dve", "s5_sum", "s5_y"))
        ge_a, ge_p, ge_f, ge_h, ge_l, glu_gate = (signal(k, "") for k in ("ge_a", "ge_p", "ge_f", "ge_h", "ge_l", "glu_gate"))
        kv_h, kv_l, v2_pe, v2_h, v2_l = (signal(k, "") for k in ("kv_h", "kv_l", "v2_pe", "v2_h", "v2_l"))
        q2_h, q2_l = (signal(k, "") for k in ("q2_h", "q2_l"))
        z, z_pos, z_negabs, z_exp, z_log, softplus_done, z_h, z_l = (signal(k, "") for k in (
            "z", "z_pos", "z_negabs", "z_exp", "z_log", "softplus_done", "z_h", "z_l"))
        w, w_exp, w_h, w_l = (signal(k, "") for k in ("w", "w_exp", "w_h", "w_l"))
        o, o_h, o_l = (signal(k, "") for k in ("o", "o_h", "o_l"))
        outs = signal("outs", "")

        def rotation_ready(l, st):
            if st.what in "qk":
                return turned_in.sem, turned_in.after(l, st.qk)
            return bank_free.sem, bank_free.after(l, st.j)

        def sine(st):
            return FF[:, st.rot % 2, :] if st.what == "mla" else KVF[:, st.rot % 2, :]

        def total_of(st):
            return FF[:, 3, :] if st.version == 3 else SQUARES[:]

        def f32(ap):
            return ap.bitcast(F32)

        def slot_words(ap, slot, n):
            return ap[:, slot, 0:n]

        def s5a(k):
            return S5A[:, k, :]

        block = ctx.enter_context(nc.Block())

        @block.sync
        def _(sp):
            sp.dma_start(MAT[:], mats[:, 0:3 * P].rearrange("p (k n) -> p k n", k=3)).then_inc(mat_in, 16)
            sp.dma_start(FF[:, 0, 0:4 * P], mats[:, 3 * P:7 * P]).then_inc(mat_in, 16)
            sp.dma_start(MASK[:], mats[:, 7 * P:8 * P]).then_inc(mat_in, 16)
            sp.dma_start(SP_[:], second_params).then_inc(mat_in, 16)
            for k in range(DT):
                sp.dma_start(X[:, k, :], x[k]).then_inc(x_in, 16)
            with sp.Fori(0, CHUNKS // RAW) as it:
                for k in range(RAW):
                    sp.wait_ge(lo.sem, it * RAW + (k + 1))
                    sp.dma_start(RAWW[:, k, :], weights[bass.ds(it * RAW + k, 1)].rearrange("a p n -> (a p) n")
                                 ).then_inc(raw_in[k], 16)
            for k in range(DT):
                sp.wait_ge(outs.sem, k + 1)
                sp.dma_start(out[k], FF[:, k, :]).then_inc(y_out, 16)
            sp.wait_ge(y_out, 16 * DT)

        @block.gpsimd
        def _(pool):
            def layer_inputs(l):
                pool.wait_ge(x_done.sem, x_done.room(l, DT - 1))
                pool.wait_ge(mats_cut, 1)
                pool.dma_start(LP[:, 0:N_LAYER_PARAMS], layer_params[bass.ds(l, 1)].rearrange("a p n -> (a p) n")
                               ).then_inc(par_in, 16)
                pool.dma_start(FF[:, 0:4, :], tables.rearrange("k p n -> p k n")).then_inc(tab_in, 16)
                for k in range(2):
                    for v in (MVH, MVL):
                        ins = pool.memset(f32(v[:, k, :, HD - k * HD:P - k * HD]), 0.0)
                ins.then_inc(mv_zero, 1)

            def add_squares(l, total, st, n):
                pool.wait_ge(first_sq.sem, first_sq.after(l, st.f))
                for k in range(st.a, st.a + n):
                    add_squared(l, total, k, k > st.a)

            def add_squared(l, total, k, again):
                if again:
                    pool.wait_ge(added.sem, added.after(l, k - 1))
                pool.wait_ge(sq_in.sem, sq_in.after(l, k))
                pool.tensor_tensor(total, total, TMP[:, 2 + k % 2, :], ALU.add).then_inc(added.sem, 1)

            def step(l, st):
                if st.kind == "stat":
                    add_squares(l, SQUARES[:], st, ADDED)
                elif st.kind == "post":
                    pool.wait_ge(rstd.sem, rstd.after(l, st.g))
                    for k in range(SCALED, DT):
                        pool.tensor_tensor(FF[:, k, :], FF[:, k, :], RCQ[:], ALU.mult).then_inc(scaled_pool.sem, 1)
                elif st.kind == "evac_ff" and st.a is not None:
                    if st.m == 1:
                        pool.wait_ge(first_sq.sem, first_sq.after(l, st.last_f))
                    add_squared(l, SQUARES[:], st.a, st.m > 1)
                elif st.kind == "turn_in":
                    pool.wait_ge(*rotation_ready(l, st))
                    if st.rot == 0:
                        pool.wait_ge(tab_in, l * 16 + 16)
                    cos = 0 if st.what in "qk" else 2
                    pool.tensor_tensor(FF[0:st.rows, 4 + st.rot % 2, :], FF[0:st.rows, 6 + st.rot % 2, :],
                                       FF[0:st.rows, cos, :], ALU.mult).then_inc(rcos.sem, 1)
                elif st.kind == "turn":
                    rows = slice(0, st.rows)
                    pool.wait_ge(rcos.sem, rcos.after(l, st.rot))
                    pool.wait_ge(turn_free.sem, turn_free.after(l, st.b))
                    pool.tensor_tensor(FF[rows, 6 + st.rot % 2, :], FF[rows, 4 + st.rot % 2, :], sine(st)[rows, :], ALU.add
                                       ).then_inc(rdone.sem, 1)
                elif st.kind == "mla_k":
                    pool.wait_ge(mk_h.sem, mk_h.after(l, st.mk))
                    pool.tensor_tensor(MKL[0:HD, st.h % 2, :], KVF[0:HD, st.h % 2, :], f32(MKH[0:HD, st.h % 2, :]), ALU.subtract
                                       ).then_inc(mk_l.sem, 1)
                elif st.kind == "att_normalise":
                    pool.wait_ge(recip.sem, recip.after(l, st.u))
                    pool.tensor_tensor(TMP[:, st.u % 4, :], TMP[:, st.u % 4, :],
                                       STAT[:, 2, st.u % 4:st.u % 4 + 1].to_broadcast([P, SEQ]), ALU.mult
                                       ).then_inc(normed.sem, 1)
                elif st.kind == "evac_br_b":
                    pool.wait_ge(bank_free.sem, bank_free.after(l, st.j))
                    pool.tensor_tensor(FF[:, 4 + st.m % 2, :], FF[:, 4 + st.m % 2, :], FF[:, 6 + st.m % 2, :],
                                       ALU.add).then_inc(merged.sem, 1)
                elif st.kind == "evac_up":
                    pool.wait_ge(bank_free.sem, bank_free.after(l, st.j))
                    pool.tensor_tensor(TMP[:, st.m % 2, :], TMP[:, 2 + st.m % 2, :], TMP[:, 2 + st.m % 2, :],
                                       ALU.mult).then_inc(hid_f.sem, 1)
                    pool.wait_ge(hid_f.sem, hid_f.after(l, st.up))
                    pool.wait_ge(hid_h.sem, hid_h.after(l, st.up))
                    pool.tensor_tensor(HL[:, st.m, :], TMP[:, st.m % 2, :], f32(HH[:, st.m, :]),
                                       ALU.subtract).then_inc(hid_l.sem, 1)

            def second_block():
                (A_RE, A_IM, LDT) = (SP_[:, S_A + k * PAIRS:S_A + (k + 1) * PAIRS] for k in range(3))
                n = [0]

                def chain(ins):
                    ins.then_inc(sp_pool.sem, 1)
                    n[0] += 1
                    pool.wait_ge(sp_pool.sem, n[0])

                def tt(out_, a, b, op):
                    chain(pool.tensor_tensor(out_, a, b, op))

                def ts(out_, a, s1, s2, op0, op1=None):
                    if op1 is None:
                        chain(pool.tensor_scalar(out_, a, s1, None, op0))
                    else:
                        chain(pool.tensor_scalar(out_, a, s1, s2, op0, op1))

                def wide(k):
                    return s5a(k).unsqueeze(2).to_broadcast([P, PAIRS, 32])

                for st in SECOND.steps:
                    if st.kind in ("stat", "final"):
                        add_squares(2, total_of(st), st, ADDED)
                    elif st.kind == "s5_params0":
                        pool.wait_ge(x_done.sem, x_done.room(2, DT - 1))
                        pool.dma_start(S5B[:], s5_b.rearrange("k p (j h) -> p k j h", h=32)).then_inc(s5_in, 16)
                        pool.dma_start(S5C[:, 0:2], s5_c.rearrange("k p (j h) -> p k j h", h=32)).then_inc(s5_in, 16)
                        pool.dma_start(S5N[:], steps_t).then_inc(s5_in, 16)
                        pool.wait_ge(sp_act.sem, 1)
                        tt(s5a(1), A_RE, s5a(0), ALU.mult)
                        tt(s5a(2), A_IM, s5a(0), ALU.mult)
                    elif st.kind == "s5_params1":
                        ts(s5a(3), s5a(2), INV2PI, MAGIC, ALU.mult, ALU.add)
                        ts(s5a(3), s5a(3), MAGIC, None, ALU.subtract)
                        for part in (PI_A, PI_B, PI_C):
                            ts(s5a(4), s5a(3), part, None, ALU.mult)
                            tt(s5a(2), s5a(2), s5a(4), ALU.subtract)
                        ts(s5a(2), s5a(2), 3.1415925, -3.1415925, ALU.min, ALU.max)
                        ts(s5a(5), s5a(2), INV2PI, None, ALU.mult)
                    elif st.kind == "s5_params2":
                        pool.wait_ge(sp_act.sem, 6)
                        tt(s5a(6), s5a(5), f32(S5AR[:]), ALU.subtract)
                        tt(s5a(11), s5a(7), s5a(10), ALU.mult)
                        tt(s5a(12), s5a(7), s5a(8), ALU.mult)
                        tt(s5a(13), A_RE, A_RE, ALU.mult)
                        tt(s5a(14), A_IM, A_IM, ALU.mult)
                        tt(s5a(13), s5a(13), s5a(14), ALU.add)
                        ts(s5a(11), s5a(11), 1.0, None, ALU.subtract)
                        tt(s5a(15), s5a(11), A_RE, ALU.mult)
                        tt(s5a(16), s5a(12), A_IM, ALU.mult)
                        tt(s5a(15), s5a(15), s5a(16), ALU.add)
                        tt(s5a(16), s5a(12), A_RE, ALU.mult)
                        tt(s5a(17), s5a(11), A_IM, ALU.mult)
                        tt(s5a(16), s5a(16), s5a(17), ALU.subtract)
                    elif st.kind == "s5_params3":
                        pool.wait_ge(sp_dve.sem, 1)
                        tt(s5a(15), s5a(15), s5a(18), ALU.mult)
                        tt(s5a(16), s5a(16), s5a(18), ALU.mult)
                        pool.wait_ge(s5_in, 48)
                        tt(S5BB[:, 0], S5B[:, 0], wide(15), ALU.mult)
                        tt(S5BB[:, 1], S5B[:, 1], wide(15), ALU.mult)
                        tt(S5BT[:, 0], S5B[:, 1], wide(16), ALU.mult)
                        tt(S5BT[:, 1], S5B[:, 0], wide(16), ALU.mult)
                        tt(S5BB[:, 0], S5BB[:, 0], S5BT[:, 0], ALU.subtract)
                        tt(S5BB[:, 1], S5BB[:, 1], S5BT[:, 1], ALU.add)
                        ts(S5C[:, 2], S5C[:, 1], -1.0, None, ALU.mult)
                    elif st.kind == "s5_rot":
                        pool.wait_ge(ro.sem, ro.after(2, 4 * st.p + 3))
                        a = [S5T[:, 4 * (st.p % 3) + k, :] for k in range(4)]
                        pool.tensor_tensor(a[0], a[0], a[1], ALU.add).then_inc(rotated_in.sem, 1)
                        pool.tensor_tensor(a[2], a[3], a[2], ALU.subtract).then_inc(rotated_in.sem, 1)
                    elif st.kind == "s5_scan":
                        pool.wait_ge(sn.sem, sn.after(2, 2 * st.p + 1))
                        a = [S5T[:, 4 * (st.p % 3) + k, :] for k in range(4)]
                        r = [S5T[:, 12 + 2 * (st.p % 2) + k, :] for k in range(2)]
                        c, s = (S5T[:, 16 + 2 * (st.p % 3) + k, :] for k in range(2))
                        pool.tensor_tensor(a[0], r[0], c, ALU.mult).then_inc(out_pool.sem, 1)
                        pool.tensor_tensor(a[1], r[1], s, ALU.mult).then_inc(out_pool.sem, 1)
                    elif st.kind == "s5_gelu0":
                        f = [FF[:, 4 * (st.m % 2) + k, :] for k in range(4)]
                        pool.wait_ge(ge_a.sem, ge_a.after(2, 2 * st.m))
                        pool.tensor_scalar(f[1], f[1], 0.044715, 1.0, ALU.mult, ALU.add).then_inc(ge_p.sem, 1)
                        pool.wait_ge(ge_p.sem, ge_p.after(2, 2 * st.m))
                        pool.tensor_tensor(f[1], f[1], f[0], ALU.mult).then_inc(ge_p.sem, 1)
                    elif st.kind == "evac_cup":
                        u = (FF[:, 7, :], TMP[:, 2, :])[st.m % 2]
                        pool.wait_ge(bank_free.sem, bank_free.after(2, st.j))
                        pool.wait_ge(conv_gate.sem, conv_gate.after(2, st.cu))
                        pool.tensor_tensor(u, u, FF[:, 5 + st.m % 2, :], ALU.mult).then_inc(conv_prod.sem, 1)
                        pool.wait_ge(conv_h.sem, conv_h.after(2, st.cu))
                        pool.tensor_tensor(CHL[:, st.m, :], u, f32(CHH[:, st.m, :]), ALU.subtract).then_inc(conv_l.sem, 1)
                    elif st.kind == "sb_weights_lo":
                        pool.wait_ge(w_h.sem, w_h.after(2, st.h))
                        pool.tensor_tensor(WTL[st.h % 3][:], SBW[st.h % 3][:], f32(WTH[st.h % 3][:]), ALU.subtract
                                           ).then_inc(w_l.sem, 1)

            pool.sem_inc(added.sem, 2)
            with pool.Fori(0, LAYERS) as l:
                layer_inputs(l)
                for st in LAYER.steps:
                    step(l, st)
            second_block()

        def pv_place(h):
            if h < HEADS:
                a = h // QT * HD
                return QH, QL, slice(a, a + HD), h % QT
            m = h - HEADS
            return YBH, YBL, slice(m % 2 * HD, m % 2 * HD + HD), m // 2

        def small_input(st):
            k = st.i if st.kind == "evac_cq" else CQT + st.i
            return k, LP[:, G_CQ + k:G_CQ + k + 1]

        def rot_dest(st):
            if st.what == "q":
                return [(QH[:, st.i, :], QL[:, st.i, :])], slice(0, P)
            if st.what == "k":
                return [(KH[:], KL[:])], slice(0, P)
            if st.what == "mla":
                return [(MQH[0:QK, st.h % 2, :], MQL[0:QK, st.h % 2, :])], slice(0, QK)
            return [(MKH[HD:QK, k, :], MKL[HD:QK, k, :]) for k in range(2)], slice(HD, QK)

        @block.scalar
        def _(act):
            def cut_next(l, st, sizes):
                for n in range(0 if st.at else len(st.kt)):
                    c = st.c + n + 1
                    if sizes[c]:
                        cut(l, c, sizes[c])

            def cut(l, c, size):
                act.wait_ge(raw_in[c % RAW], l * (CHUNKS_L // RAW * 16) + 16 * (c // RAW + 1))
                act.wait_ge(used.sem, used.room(l, c))
                act.activation(slot_words(WH, c % CUT, size), slot_words(RAWW, c % RAW, size), ACT.Copy
                               ).then_inc(hi.sem, 1)

            def square(l, s, src):
                act.wait_ge(summed.sem, summed.room(l, s))
                act.activation(TMP[0:src.shape[0], s % 2, :], src, ACT.Square).then_inc(sq.sem, 1)

            def factor(l, g, last_s, dst, scale, bias):
                act.wait_ge(summed.sem, summed.after(l, last_s))
                act.activation(dst, stat_bank(g)[:], ACT.Ln, bias=bias, scale=scale).then_inc(logged.sem, 1)
                act.wait_ge(logged.sem, logged.after(l, g))
                act.activation(dst, dst, ACT.Exp, scale=-0.5).then_inc(rstd.sem, 1)

            def gains(l, st, gain):
                for k in range(DT):
                    act.activation(UH[:, k, :], X[:, k, :], ACT.Copy, scale=gain[:, k:k + 1]).then_inc(uh.sem, 1)

            def square_for_pool(l, a, src):
                act.wait_ge(added.sem, added.room(l, a))
                act.activation(TMP[:, 2 + a % 2, :], src, ACT.Square).then_inc(sq_in.sem, 1)

            def norm(l, st, gain, total):
                for k in range(DT):
                    act.wait_ge(x_done.sem, x_done.room(l, DT * st.version + k))
                    if gain is not None:
                        act.activation(UH[:, k, :], X[:, k, :], ACT.Copy, scale=gain[:, k:k + 1]).then_inc(uh.sem, 1)
                    if k == 0:
                        act.activation(total, X[:, k, :], ACT.Square).then_inc(first_sq.sem, 1)
                    elif k <= ADDED:
                        square_for_pool(l, st.a + k - 1, X[:, k, :])
                    else:
                        square(l, st.s + k - ADDED - 1, X[:, k, :])

            def stat(l, st):
                factor(l, st.g, st.s + DT - 2 - ADDED, RSTD[:], 1.0 / DM, EPS)

            def step(l, st):
                kind = st.kind
                if kind in ("mm", "mla_mm"):
                    cut_next(l, st, LAYER_WORDS)
                elif kind == "norm":
                    if st.gain == 0:
                        act.wait_ge(par_in, l * 16 + 16)
                    norm(l, st, LP[:, st.gain:st.gain + DT], SQUARES[:])
                elif kind == "stat":
                    stat(l, st)
                elif kind == "regain":
                    gains(l, st, LP[:, st.gain:st.gain + DT])
                elif kind in ("evac_q", "evac_k"):
                    act.wait_ge(bank_free.sem, bank_free.after(l, st.j))
                    square(l, st.s, TMP[:, 2 + st.x % 2, :])
                elif kind in ("evac_cq", "evac_ckv"):
                    k, gain = small_input(st)
                    act.wait_ge(bank_free.sem, bank_free.after(l, st.j))
                    act.activation(CH[:, k, :], TMP[:, 2 + st.x % 2, :], ACT.Copy, scale=gain).then_inc(c_h.sem, 1)
                    square(l, st.s, TMP[:, 2 + st.x % 2, :])
                elif kind == "rc_cq":
                    factor(l, st.g, st.s, RCQ[:], 1.0 / Q_RANK, EPS)
                elif kind == "rc_ckv":
                    factor(l, st.g, st.s, RKV[:], 1.0 / KV_RANK, EPS)
                elif kind == "turn_in":
                    if st.what == "q":
                        factor(l, st.g, st.s, FF[:, 4 + st.rot % 2, :], 1.0, HD * EPS)
                    elif st.what == "k":
                        factor(l, st.g, st.s, FF[:, 4 + st.rot % 2, :], 1.0 / HD, EPS)
                    act.wait_ge(*rotation_ready(l, st))
                    if st.rot:
                        act.wait_ge(turn.sem, turn.after(l, st.turn_before))
                    act.activation(RH[0:st.rows, :], FF[0:st.rows, 6 + st.rot % 2, :], ACT.Copy).then_inc(rh.sem, 1)
                elif kind == "turn_out":
                    dests, rows = rot_dest(st)
                    act.wait_ge(rdone.sem, rdone.after(l, st.rot))
                    for n, (h, _) in enumerate(dests):
                        ins = act.activation(h, FF[rows, 6 + st.rot % 2, :], ACT.Copy)
                    ins.then_inc(rot_h.sem, 1)
                elif kind == "gqa_v":
                    act.wait_ge(turn.sem, turn.after(l, st.b))
                    act.activation(VH[:].rearrange("p k n -> p (k n)"), TURN[:], ACT.Copy).then_inc(v_h.sem, 1)
                elif kind == "mla_k":
                    act.wait_ge(bank_free.sem, bank_free.after(l, st.j + 1))
                    act.activation(MKH[0:HD, st.h % 2, :], KVF[0:HD, st.h % 2, :], ACT.Copy).then_inc(mk_h.sem, 1)
                elif kind == "mla_v":
                    act.wait_ge(turn.sem, turn.after(l, st.b))
                    a = st.h % 2 * HD
                    act.activation(MVH[:, st.h % 2, :, a:a + HD], TURN[:].rearrange("p (k n) -> p k n", k=KT)[:, :, HD:P],
                                   ACT.Copy).then_inc(v_h.sem, 1)
                elif kind == "att_scores":
                    act.wait_ge(row_max.sem, row_max.after(l, st.u))
                    act.wait_ge(probs_t.sem, probs_t.room(l, st.u))
                    r = st.u % 4
                    act.activation(TMP[:, r, :], BANK[2 + st.u % 2][:], ACT.Exp, bias=STAT[:, 0, r:r + 1],
                                   accum_out=STAT[:, 1, r:r + 1]).then_inc(expd.sem, 1)
                elif kind == "att_transpose":
                    act.wait_ge(probs_t.sem, probs_t.after(l, st.u))
                    act.activation(PHH[:, st.h % 2, :, st.t * P:(st.t + 1) * P],
                                   BANK[4 + st.u % 2][:].rearrange("p (k q) -> p k q", k=KT), ACT.Copy
                                   ).then_inc(probs_h.sem, 1)
                elif kind == "att_out_hi":
                    h, _, rows, k = pv_place(st.h)
                    act.wait_ge(pv.sem, pv.after(l, st.pv))
                    act.activation(h[rows, k, :], OUTB[rows, :], ACT.Copy).then_inc(y_h.sem, 1)
                elif kind in ("evac_ga", "evac_gb"):
                    b = kind == "evac_gb"
                    t = FF[:, 2 * b + st.m % 2, :]
                    act.wait_ge(bank_free.sem, bank_free.after(l, st.j))
                    bias = G_BIAS + DT * b + st.m
                    act.activation(t, t, ACT.Sigmoid, bias=LP[:, bias:bias + 1]).then_inc(gate.sem, 1)
                elif kind == "merge":
                    act.wait_ge(merged.sem, merged.after(l, st.mg))
                    act.activation(MH[:, st.m, :], FF[:, 4 + st.m % 2, :], ACT.Copy).then_inc(merged_h.sem, 1)
                    if st.m == DT - 1:
                        act.preload_act_table_set(LOG_EXP)
                elif kind == "evac_ff" and st.group is not None:
                    act.wait_ge(bank_free.sem, bank_free.after(l, st.j))
                    if st.m == 0:
                        act.activation(SQUARES[:], FF[:, st.m, :], ACT.Square).then_inc(first_sq.sem, 1)
                    elif st.a is not None:
                        square_for_pool(l, st.a, FF[:, st.m, :])
                    else:
                        square(l, st.s, FF[:, st.m, :])
                elif kind == "post":
                    factor(l, st.g, st.last_s, RCQ[:], 1.0 / DM, EPS)
                elif kind == "evac_up":
                    act.wait_ge(bank_free.sem, bank_free.after(l, st.j))
                    act.activation(HH[:, st.m, :], TMP[:, 2 + st.m % 2, :], ACT.Square).then_inc(hid_h.sem, 1)

            def second(st):
                kind = st.kind
                copy = ACT.Copy
                if kind == "mm":
                    cut_next(2, st, SECOND_WORDS)
                elif kind in ("norm", "regain"):
                    g = S_GAIN[st.gain]
                    if st.last_use is not None:
                        act.wait_ge(used.sem, used.after(2, st.last_use))
                    if kind == "norm":
                        act.preload_act_table_set(LOG_EXP)
                        norm(2, st, SP_[:, g:g + DT], total_of(st))
                    else:
                        gains(2, st, SP_[:, g:g + DT])
                elif kind == "stat":
                    stat(2, st)
                elif kind == "s5_params0":
                    act.activation(s5a(0), SP_[:, S_A + 2 * PAIRS:S_A + 3 * PAIRS], ACT.Exp).then_inc(sp_act.sem, 1)
                elif kind == "s5_params1":
                    act.wait_ge(sp_pool.sem, 2)
                    act.activation(s5a(7), s5a(1), ACT.Exp).then_inc(sp_act.sem, 1)
                elif kind == "s5_params2":
                    act.wait_ge(sp_pool.sem, 12)
                    act.activation(s5a(8), s5a(2), ACT.Sin).then_inc(sp_act.sem, 1)
                    act.activation(s5a(9), s5a(2), ACT.Abs).then_inc(sp_act.sem, 1)
                    act.activation(S5AR[:], s5a(5), copy).then_inc(sp_act.sem, 1)
                    act.wait_ge(sp_act.sem, 5)
                    act.activation(s5a(10), s5a(9), ACT.Sin, bias=math.pi / 2, scale=-1.0).then_inc(sp_act.sem, 1)
                elif kind == "s5_factors":
                    act.preload_act_table_set(SIN_TANH)
                    for k in range(4):
                        act.wait_ge(sp_pe.sem, k + 1)
                        act.activation(BBT[:, k // 2, 4 * (k % 2):4 * (k % 2) + 4, :].rearrange("p t n -> p (t n)"),
                                       BANK[2 + k][:], copy).then_inc(sp_act.sem, 1)
                elif kind == "s5_table":
                    g, half = S5T[:, 22 + st.p % 2, :], S5T[:, 24 + st.p % 2, :]
                    c = S5T[:, 16 + 2 * (st.p % 3), :]
                    act.wait_ge(tb.sem, tb.after(2, st.p))
                    if st.p >= 2:
                        act.wait_ge(sine_done.sem, sine_done.after(2, st.p - 2))
                    act.activation(half, g, ACT.Sin, scale=math.pi).then_inc(trig.sem, 1)
                    act.wait_ge(trig.sem, trig.after(2, 5 * st.p))
                    act.activation(g, g, ACT.Abs).then_inc(trig.sem, 1)
                    if st.p >= 3:
                        act.wait_ge(out_pool.sem, out_pool.after(2, 2 * (st.p - 3) + 1))
                        act.wait_ge(out_dve.sem, out_dve.after(2, 2 * (st.p - 3) + 1))
                    act.activation(c, half, ACT.Square).then_inc(trig.sem, 1)
                    act.wait_ge(trig.sem, trig.after(2, 5 * st.p + 1))
                    act.activation(g, g, ACT.Sin, bias=math.pi / 2, scale=-math.pi).then_inc(trig.sem, 1)
                    act.wait_ge(trig.sem, trig.after(2, 5 * st.p + 2))
                    act.activation(c, c, copy, bias=1.0, scale=-2.0).then_inc(trig.sem, 1)
                elif kind == "s5_gelu0":
                    f = [FF[:, 4 * (st.m % 2) + k, :] for k in range(4)]
                    act.wait_ge(s5_y.sem, s5_y.after(2, st.m))
                    act.activation(f[1], f[0], ACT.Square).then_inc(ge_a.sem, 1)
                    act.wait_ge(ge_p.sem, ge_p.after(2, 2 * st.m + 1))
                    act.activation(f[2], f[1], ACT.Tanh, scale=math.sqrt(2.0 / math.pi)).then_inc(ge_a.sem, 1)
                elif kind == "s5_gelu1":
                    act.wait_ge(ge_f.sem, ge_f.after(2, st.m))
                    act.activation(UH[:, st.m, :], FF[:, 4 * (st.m % 2) + 3, :], copy, scale=0.5).then_inc(ge_h.sem, 1)
                elif kind == "evac_glu_gate":
                    t = FF[:, st.m % 2, :]
                    act.wait_ge(bank_free.sem, bank_free.after(2, st.j))
                    act.activation(t, t, ACT.Sigmoid).then_inc(glu_gate.sem, 1)
                elif kind == "evac_gate":
                    act.wait_ge(conv_sum.sem, conv_sum.after(2, 3 * st.cg + 2))
                    if st.cg >= 2:
                        act.wait_ge(conv_prod.sem, conv_prod.after(2, st.cg - 2))
                    act.activation(FF[:, 5 + st.m % 2, :], FF[:, 3 + st.m % 2, :], ACT.Silu).then_inc(conv_gate.sem, 1)
                elif kind == "evac_cup":
                    act.wait_ge(conv_prod.sem, conv_prod.after(2, st.cu))
                    act.activation(CHH[:, st.m, :], (FF[:, 7, :], TMP[:, 2, :])[st.m % 2], copy).then_inc(conv_h.sem, 1)
                elif kind == "evac_k2":
                    act.wait_ge(bank_free.sem, bank_free.after(2, st.j))
                    act.activation(K2H[:, st.m, :], TMP[:, 2 + st.kv % 2, :], copy).then_inc(kv_h.sem, 1)
                elif kind == "v2_turn":
                    act.wait_ge(v2_pe.sem, v2_pe.after(2, st.v2))
                    act.activation(V2H[:, :, st.m * P:(st.m + 1) * P], BANK[2 + st.m % 2][:].rearrange("p (k n) -> p k n", k=KT),
                                   copy).then_inc(v2_h.sem, 1)
                elif kind == "evac_q2":
                    act.wait_ge(bank_free.sem, bank_free.after(2, st.j))
                    act.activation(Q2H[:, st.m, :], TMP[:, 2 + st.m % 2, :], copy).then_inc(q2_h.sem, 1)
                elif kind == "sb_scores":
                    act.wait_ge(z_negabs.sem, z_negabs.after(2, 3 * st.h))
                    act.activation(SBZ[:, 0:SEQ], SBZ[:, 0:SEQ], ACT.Exp).then_inc(z_exp.sem, 1)
                    act.wait_ge(z_exp.sem, z_exp.after(2, 2 * st.h))
                    act.activation(SBZ[:, 0:SEQ], SBZ[:, 0:SEQ], ACT.Ln, bias=1.0).then_inc(z_log.sem, 1)
                elif kind == "sb_sum":
                    act.wait_ge(z_negabs.sem, z_negabs.after(2, 3 * st.h + 2))
                    act.activation(SBZ[:, SEQ:], SBZ[:, SEQ:], ACT.Exp).then_inc(z_exp.sem, 1)
                    act.wait_ge(z_exp.sem, z_exp.after(2, 2 * st.h + 1))
                    act.activation(SBZ[:, SEQ:], SBZ[:, SEQ:], ACT.Ln, bias=1.0).then_inc(z_log.sem, 1)
                elif kind == "sb_cut":
                    act.wait_ge(softplus_done.sem, softplus_done.after(2, st.h))
                    if st.h:
                        act.wait_ge(w.sem, w.after(2, st.h - 1))
                    act.activation(SPH[:], SBS[:], copy).then_inc(z_h.sem, 1)
                elif kind == "sb_weights":
                    act.wait_ge(w.sem, w.after(2, st.h))
                    if st.h >= 3:
                        act.wait_ge(o.sem, o.after(2, st.h - 3))
                    for k, n in enumerate((SEQ, SEQ, SEQ // 2)):
                        ins = act.activation(SBW[st.h % 3][:, SEQ * k:SEQ * k + n], BANK[3 * (st.h % 2) + k][:, 0:n], ACT.Exp)
                    ins.then_inc(w_exp.sem, 1)
                elif kind == "sb_weights_hi":
                    act.wait_ge(w_exp.sem, w_exp.after(2, st.h))
                    act.activation(WTH[st.h % 3][:], SBW[st.h % 3][:], copy).then_inc(w_h.sem, 1)
                elif kind == "sb_out_cut":
                    rows = slice(st.h % 2 * HD, st.h % 2 * HD + HD)
                    act.wait_ge(o.sem, o.after(2, st.h))
                    act.activation(Q2H[rows, st.h // 2, :], BANK[6 + st.h % 2][rows, :], copy).then_inc(o_h.sem, 1)
                elif kind == "final":
                    act.preload_act_table_set(LOG_EXP)
                    norm(2, st, None, total_of(st))
                    stat(2, st)

            act.preload_act_table_set(LOG_EXP)
            act.wait_ge(mat_in, 64)
            act.activation(MATR[:].rearrange("p k n -> p (k n)"), FF[:, 0, 0:4 * P], ACT.Copy).then_inc(mats_cut, 1)
            act.sem_inc(expd.sem, 2)
            cut(0, 0, SLOT)
            with act.Fori(0, LAYERS) as l:
                for st in LAYER.steps:
                    step(l, st)
            for st in SECOND.steps:
                second(st)

        @block.vector
        def _(dve):
            def cut_next(l, st, sizes):
                for n in range(0 if st.at else len(st.kt)):
                    c = st.c + n + 1
                    if sizes[c]:
                        cut(l, c, sizes[c])

            def cut(l, c, size):
                dve.wait_ge(hi.sem, hi.after(l, c))
                dve.tensor_tensor(slot_words(WL, c % CUT, size), slot_words(RAWW, c % RAW, size),
                                  f32(slot_words(WH, c % CUT, size)), ALU.subtract).then_inc(lo.sem, 1)

            def rest(dst, src, h):
                return dve.tensor_tensor(dst, src, f32(h), ALU.subtract)

            def gained_rest(l, st, gain):
                for k in range(DT):
                    dve.wait_ge(uh.sem, uh.after(l, st.n + k))
                    dve.scalar_tensor_tensor(UL[:, k, :], X[:, k, :], gain[:, k:k + 1], f32(UH[:, k, :]),
                                             ALU.mult, ALU.subtract).then_inc(ul.sem, 1)

            def from_bank(l, st):
                dve.wait_ge(used.sem, used.after(l, st.done))
                return BANK[st.j % 2]

            def times_rstd(l, st, dst, rows=P):
                b = from_bank(l, st)
                return dve.tensor_tensor(dst, b[0:rows, :], RSTD[0:rows, :], ALU.mult).then_inc(bank_free.sem, 1)

            def step(l, st):
                kind = st.kind
                if kind in ("mm", "mla_mm"):
                    cut_next(l, st, LAYER_WORDS)
                elif kind in ("norm", "regain"):
                    gained_rest(l, st, LP[:, st.gain:st.gain + DT])
                elif kind == "stat":
                    dve.wait_ge(rstd.sem, rstd.after(l, st.g))
                elif kind in ("evac_q", "evac_k", "evac_v"):
                    times_rstd(l, st, TMP[:, 2 + st.x % 2, :])
                elif kind in ("evac_cq", "evac_ckv"):
                    t = TMP[:, 2 + st.x % 2, :]
                    times_rstd(l, st, t)
                    k, gain = small_input(st)
                    dve.wait_ge(c_h.sem, c_h.after(l, st.cn))
                    dve.wait_ge(bank_free.sem, bank_free.after(l, st.j))
                    dve.scalar_tensor_tensor(CL[:, k, :], t, gain, f32(CH[:, k, :]), ALU.mult, ALU.subtract
                                             ).then_inc(c_l.sem, 1)
                elif kind == "evac_kr":
                    b = from_bank(l, st)
                    dve.wait_ge(rot_l.sem, rot_l.after(l, st.rot - 2))
                    dve.tensor_tensor(FF[0:QK, 6 + st.rot % 2, :], b[0:QK, :], RSTD[0:QK, :], ALU.mult
                                      ).then_inc(bank_free.sem, 1)
                elif kind == "mla_evac":
                    dve.wait_ge(used.sem, used.after(l, st.done))
                    if st.h == 0:
                        dve.wait_ge(rstd.sem, rstd.after(l, RC_LAST))
                    dve.wait_ge(rot_l.sem, rot_l.after(l, st.rot - 2))
                    dve.scalar_tensor_tensor(FF[0:QK, 6 + st.rot % 2, :], BANK[st.j % 2][0:QK, :], QK ** -0.5, RCQ[0:QK, :],
                                             ALU.mult, ALU.mult).then_inc(bank_free.sem, 1)
                    dve.tensor_tensor(KVF[:, st.h % 2, :], BANK[(st.j + 1) % 2][:], RKV[:], ALU.mult
                                      ).then_inc(bank_free.sem, 1)
                elif kind == "turn_in":
                    rows = slice(0, st.rows)
                    src, a = FF[rows, 6 + st.rot % 2, :], FF[rows, 4 + st.rot % 2, :]
                    if st.what in "qk":
                        gain = G_Q if st.what == "q" else G_K
                        dve.wait_ge(rstd.sem, rstd.after(l, st.g))
                        if st.rot >= 2:
                            dve.wait_ge(rot_l.sem, rot_l.after(l, st.rot - 2))
                        dve.scalar_tensor_tensor(src, TMP[:, 2 + st.x % 2, :], LP[:, gain:gain + 1], a, ALU.mult, ALU.mult
                                                 ).then_inc(turned_in.sem, 1)
                elif kind == "turn_rest":
                    rows = slice(0, st.rows)
                    src = FF[rows, 6 + st.rot % 2, :]
                    dve.wait_ge(rh.sem, rh.after(l, st.rot))
                    rest(RL[rows, :], src, RH[rows, :]).then_inc(rl.sem, 1)
                elif kind == "turn":
                    rows = slice(0, st.rows)
                    b = sine(st)[rows, :]
                    dve.wait_ge(turn.sem, turn.after(l, st.b))
                    if st.rot == 0:
                        dve.wait_ge(tab_in, l * 16 + 16)
                    sin = FF[rows, 1 if st.what in "qk" else 3, :]
                    dve.tensor_tensor(b, TURN[rows, :], sin, ALU.mult).then_inc(turn_free.sem, 1)
                elif kind == "turn_out":
                    dests, rows = rot_dest(st)
                    dve.wait_ge(rdone.sem, rdone.after(l, st.rot))
                    dve.wait_ge(rot_h.sem, rot_h.after(l, st.rot))
                    for h, lo_ in dests:
                        ins = rest(lo_, FF[rows, 6 + st.rot % 2, :], h)
                    ins.then_inc(rot_l.sem, 1)
                elif kind == "gqa_v":
                    dve.wait_ge(v_h.sem, v_h.after(l, st.vh))
                    rest(VL[:].rearrange("p k n -> p (k n)"), TURN[:], VH[:].rearrange("p k n -> p (k n)")
                         ).then_inc(turn_free.sem, 1)
                elif kind == "mla_v":
                    dve.wait_ge(v_h.sem, v_h.after(l, st.vh))
                    a = st.h % 2 * HD
                    rest(MVL[:, st.h % 2, :, a:a + HD], TURN[:].rearrange("p (k n) -> p k n", k=KT)[:, :, HD:P],
                         MVH[:, st.h % 2, :, a:a + HD]).then_inc(turn_free.sem, 1)
                elif kind == "att_scores":
                    r = st.u % 4
                    dve.wait_ge(scores.sem, scores.after(l, st.u))
                    dve.tensor_reduce(STAT[:, 0, r:r + 1], BANK[2 + st.u % 2][:], AX_X, ALU.max, negate=True
                                      ).then_inc(row_max.sem, 1)
                elif kind == "att_normalise":
                    r = st.u % 4
                    dve.wait_ge(expd.sem, expd.after(l, st.u))
                    dve.reciprocal(STAT[:, 2, r:r + 1], STAT[:, 1, r:r + 1]).then_inc(recip.sem, 1)
                elif kind == "att_lo":
                    dve.wait_ge(probs_h.sem, probs_h.after(l, st.u))
                    at_ = (slice(None), st.h % 2, slice(None), slice(st.t * P, (st.t + 1) * P))
                    rest(PHL[at_], BANK[4 + st.u % 2][:].rearrange("p (k q) -> p k q", k=KT), PHH[at_]
                         ).then_inc(probs_l.sem, 1)
                elif kind == "att_out_lo":
                    h, lo_, rows, k = pv_place(st.h)
                    dve.wait_ge(y_h.sem, y_h.after(l, st.pv))
                    rest(lo_[rows, k, :], OUTB[rows, :], h[rows, k, :]).then_inc(y_l.sem, 1)
                elif kind in ("evac_ga", "evac_gb"):
                    b = from_bank(l, st)
                    dve.tensor_tensor(FF[:, 2 * (kind == "evac_gb") + st.m % 2, :], b[:], RSTD[:], ALU.mult
                                      ).then_inc(bank_free.sem, 1)
                elif kind in ("evac_br_a", "evac_br_b"):
                    n = kind == "evac_br_b"
                    if n:
                        b = from_bank(l, st)
                    else:
                        dve.wait_ge(half.sem, half.after(l, st.hf))
                        b = BANK[st.j % 2]
                    g = FF[:, 2 * n + st.m % 2, :]
                    dve.wait_ge(gate.sem, gate.after(l, 2 * st.m + n))
                    dve.tensor_tensor(FF[:, 4 + 2 * n + st.m % 2, :], b[:], g, ALU.mult).then_inc(bank_free.sem, 1)
                elif kind == "merge":
                    dve.wait_ge(merged_h.sem, merged_h.after(l, st.mg))
                    rest(ML[:, st.m, :], FF[:, 4 + st.m % 2, :], MH[:, st.m, :]).then_inc(merged_l.sem, 1)
                elif kind == "evac_ff":
                    b = from_bank(l, st)
                    if st.add:
                        dve.tensor_tensor(FF[:, st.m, :], b[:], FF[:, st.m, :], ALU.add).then_inc(bank_free.sem, 1)
                    else:
                        dve.tensor_copy(FF[:, st.m, :], b[:]).then_inc(bank_free.sem, 1)
                elif kind == "post":
                    dve.wait_ge(rstd.sem, rstd.after(l, st.g))
                    for k in range(DT + 1):
                        if k < SCALED:
                            dve.tensor_tensor(FF[:, k, :], FF[:, k, :], RCQ[:], ALU.mult).then_inc(scaled.sem, 1)
                        if k >= 1:
                            t = k - 1
                            if t < SCALED:
                                dve.wait_ge(scaled.sem, scaled.after(l, st.sc + t))
                            else:
                                dve.wait_ge(scaled_pool.sem, scaled_pool.after(l, st.sp + t - SCALED))
                            dve.scalar_tensor_tensor(X[:, t, :], FF[:, t, :], LP[:, st.gain + t:st.gain + t + 1], X[:, t, :],
                                                     ALU.mult, ALU.add).then_inc(x_done.sem, 1)
                elif kind == "evac_up":
                    b = from_bank(l, st)
                    t = TMP[:, 2 + st.m % 2, :]
                    if st.up >= 2:
                        dve.wait_ge(hid_f.sem, hid_f.after(l, st.up - 2))
                        dve.wait_ge(hid_h.sem, hid_h.after(l, st.up - 2))
                    dve.scalar_tensor_tensor(t, b[:], 0.0, RSTD[:], ALU.max, ALU.mult).then_inc(bank_free.sem, 1)

            def second(st):
                kind = st.kind
                if kind == "mm":
                    cut_next(2, st, SECOND_WORDS)
                elif kind in ("norm", "regain"):
                    g = S_GAIN[st.gain]
                    gained_rest(2, st, SP_[:, g:g + DT])
                elif kind == "stat":
                    dve.wait_ge(rstd.sem, rstd.after(2, st.g))
                elif kind == "evac_u":
                    times_rstd(2, st, S5U[:, st.m, :])
                elif kind == "s5_params2":
                    dve.wait_ge(sp_pool.sem, 18)
                    dve.reciprocal(s5a(18), s5a(13)).then_inc(sp_dve.sem, 1)
                elif kind == "s5_grid0":
                    number = S5N[:].unsqueeze(1).to_broadcast([P, PAIRS, COARSE + FINE])
                    k, kh, kl = (a.unsqueeze(2).to_broadcast([P, PAIRS, COARSE + FINE]) for a in (s5a(5), f32(S5AR[:]), s5a(6)))
                    dve.wait_ge(s5_in, 48)
                    dve.wait_ge(sp_pool.sem, 13)
                    dve.tensor_tensor(GRIDA[:], number, k, ALU.mult).then_inc(grid.sem, 1)
                    dve.tensor_tensor(GRID[:], number, kh, ALU.mult).then_inc(grid.sem, 1)
                    dve.tensor_tensor(GRIDB[:], number, kl, ALU.mult).then_inc(grid.sem, 1)
                elif kind == "s5_grid1":
                    dve.wait_ge(grid.sem, 1)
                    dve.tensor_scalar(GRIDA[:], GRIDA[:], MAGIC, None, ALU.add).then_inc(grid.sem, 1)
                    dve.wait_ge(grid.sem, 4)
                    dve.tensor_scalar(GRIDA[:], GRIDA[:], MAGIC, None, ALU.subtract).then_inc(grid.sem, 1)
                elif kind == "s5_grid2":
                    dve.wait_ge(grid.sem, 5)
                    dve.tensor_tensor(GRID[:], GRID[:], GRIDA[:], ALU.subtract).then_inc(grid.sem, 1)
                    dve.wait_ge(grid.sem, 6)
                    dve.tensor_tensor(GRID[:], GRID[:], GRIDB[:], ALU.add).then_inc(grid.sem, 1)
                elif kind == "s5_grid3":
                    dve.wait_ge(grid.sem, 7)
                    dve.tensor_scalar(GRID[:], GRID[:], 0.5, -0.5, ALU.min, ALU.max).then_inc(grid.sem, 1)
                    dve.wait_ge(grid.sem, 8)
                elif kind == "s5_table":
                    if st.p >= 2:
                        dve.wait_ge(sine_done.sem, sine_done.after(2, st.p - 2))
                    dve.tensor_tensor(S5T[:, 22 + st.p % 2, :].rearrange("p (a b) -> p a b", a=COARSE),
                                      GRID[:, st.p, 0:COARSE].unsqueeze(2).to_broadcast([P, COARSE, FINE]),
                                      GRID[:, st.p, COARSE:].unsqueeze(1).to_broadcast([P, COARSE, FINE]), ALU.add
                                      ).then_inc(tb.sem, 1)
                elif kind == "s5_rot":
                    a = [S5T[:, 4 * (st.p % 3) + k, :] for k in range(4)]
                    c, s = (S5T[:, 16 + 2 * (st.p % 3) + k, :] for k in range(2))
                    re, im = (BANK[2 + 2 * (st.p % 2) + k][:] for k in range(2))
                    dve.wait_ge(trig.sem, trig.after(2, 5 * st.p + 4))
                    if st.p >= 3:
                        dve.wait_ge(out_pool.sem, out_pool.after(2, 2 * (st.p - 3) + 1))
                        dve.wait_ge(out_dve.sem, out_dve.after(2, 2 * (st.p - 3) + 1))
                    dve.scalar_tensor_tensor(s, S5T[:, 24 + st.p % 2, :], 2.0, S5T[:, 22 + st.p % 2, :], ALU.mult, ALU.mult
                                             ).then_inc(sine_done.sem, 1)
                    dve.wait_ge(sine_done.sem, sine_done.after(2, st.p))
                    dve.wait_ge(state_in.sem, state_in.after(2, st.p))
                    if st.p >= 3:
                        dve.wait_ge(s5_sum.sem, s5_sum.after(2, st.p - 3))
                    for k, (b, v) in enumerate(((re, c), (im, s), (im, c), (re, s))):
                        dve.tensor_tensor(a[k], b, v, ALU.mult).then_inc(ro.sem, 1)
                elif kind == "s5_scan":
                    a = [S5T[:, 4 * (st.p % 3) + k, :] for k in range(4)]
                    r = [S5T[:, 12 + 2 * (st.p % 2) + k, :] for k in range(2)]
                    c, s = (S5T[:, 16 + 2 * (st.p % 3) + k, :] for k in range(2))
                    mag = s5a(7)[:, st.p:st.p + 1].to_broadcast([P, SEQ])
                    if st.p >= 2:
                        dve.wait_ge(out_pool.sem, out_pool.after(2, 2 * (st.p - 2) + 1))
                    for k in range(2):
                        dve.wait_ge(rotated_in.sem, rotated_in.after(2, 2 * st.p + k))
                        dve.tensor_tensor_scan(r[k], mag, a[2 * k], 0.0, ALU.mult, ALU.add).then_inc(sn.sem, 1)
                    dve.wait_ge(sn.sem, sn.after(2, 2 * st.p + 1))
                    dve.tensor_tensor(a[2], r[0], s, ALU.mult).then_inc(out_dve.sem, 1)
                    dve.tensor_tensor(a[3], r[1], c, ALU.mult).then_inc(out_dve.sem, 1)
                elif kind == "s5_gelu0":
                    dve.wait_ge(s5_sum.sem, s5_sum.after(2, 4 * st.m + 3))
                    dve.scalar_tensor_tensor(FF[:, 4 * (st.m % 2), :], S5U[:, st.m, :], SP_[:, S_D + st.m:S_D + st.m + 1],
                                             BANK[6 + st.m % 2][:], ALU.mult, ALU.add).then_inc(s5_y.sem, 1)
                elif kind == "s5_gelu1":
                    f = [FF[:, 4 * (st.m % 2) + k, :] for k in range(4)]
                    dve.wait_ge(ge_a.sem, ge_a.after(2, 2 * st.m + 1))
                    dve.scalar_tensor_tensor(f[3], f[2], 1.0, f[0], ALU.add, ALU.mult).then_inc(ge_f.sem, 1)
                elif kind == "s5_gelu2":
                    dve.wait_ge(ge_h.sem, ge_h.after(2, st.m))
                    dve.scalar_tensor_tensor(UL[:, st.m, :], FF[:, 4 * (st.m % 2) + 3, :], 0.5, f32(UH[:, st.m, :]),
                                             ALU.mult, ALU.subtract).then_inc(ge_l.sem, 1)
                elif kind == "evac_glu_gate":
                    b = from_bank(2, st)
                    dve.tensor_copy(FF[:, st.m % 2, :], b[:]).then_inc(bank_free.sem, 1)
                elif kind == "evac_glu":
                    b, t = from_bank(2, st), FF[:, st.m % 2, :]
                    dve.wait_ge(glu_gate.sem, glu_gate.after(2, st.m))
                    dve.tensor_tensor(t, b[:], t, ALU.mult).then_inc(bank_free.sem, 1)
                    dve.wait_ge(bank_free.sem, bank_free.after(2, st.j))
                    dve.tensor_tensor(X[:, st.m, :], X[:, st.m, :], t, ALU.add).then_inc(x_done.sem, 1)
                elif kind == "evac_gate":
                    g, t = GATE[:, st.m % 2, :], FF[:, 3 + st.m % 2, :]
                    w_ = [SP_[:, S_CONV + (st.layer * C_TILES + st.m) * 4 + k:][:, 0:1] for k in range(4)]
                    if st.m < 2:
                        dve.memset(g[:, 0:2], 0.0)
                    times_rstd(2, st, g[:, 2:2 + SEQ])
                    dve.wait_ge(bank_free.sem, bank_free.after(2, st.j))
                    if st.cg >= 2:
                        dve.wait_ge(conv_gate.sem, conv_gate.after(2, st.cg - 2))
                    dve.tensor_scalar(t, g[:, 2:2 + SEQ], w_[2], w_[3], ALU.mult, ALU.add).then_inc(conv_sum.sem, 1)
                    dve.wait_ge(conv_sum.sem, conv_sum.after(2, 3 * st.cg))
                    dve.scalar_tensor_tensor(t, g[:, 1:1 + SEQ], w_[1], t, ALU.mult, ALU.add).then_inc(conv_sum.sem, 1)
                    dve.wait_ge(conv_sum.sem, conv_sum.after(2, 3 * st.cg + 1))
                    dve.scalar_tensor_tensor(t, g[:, 0:SEQ], w_[0], t, ALU.mult, ALU.add).then_inc(conv_sum.sem, 1)
                elif kind == "evac_cup":
                    u = (FF[:, 7, :], TMP[:, 2, :])[st.m % 2]
                    if st.cu >= 2:
                        dve.wait_ge(conv_l.sem, conv_l.after(2, st.cu - 2))
                    times_rstd(2, st, u)
                elif kind == "evac_res":
                    b = from_bank(2, st)
                    dve.tensor_tensor(X[:, st.m, :], b[:], X[:, st.m, :], ALU.add).then_inc(x_done.sem, 1)
                    dve.wait_ge(x_done.sem, x_done.after(2, st.x))
                    dve.sem_inc(bank_free.sem, 1)
                elif kind in ("evac_k2", "evac_v2"):
                    if 2 <= st.kv < DT + 2:
                        dve.wait_ge(kv_l.sem, kv_l.after(2, st.kv - 2))
                    elif st.kv >= DT + 2:
                        dve.wait_ge(v2_pe.sem, v2_pe.after(2, st.kv - 2 - DT))
                    times_rstd(2, st, TMP[:, 2 + st.kv % 2, :])
                    if kind == "evac_k2":
                        dve.wait_ge(kv_h.sem, kv_h.after(2, st.m))
                        rest(K2L[:, st.m, :], TMP[:, 2 + st.kv % 2, :], K2H[:, st.m, :]).then_inc(kv_l.sem, 1)
                elif kind == "v2_turn":
                    dst = (slice(None), slice(None), slice(st.m * P, (st.m + 1) * P))
                    dve.wait_ge(v2_h.sem, v2_h.after(2, st.v2))
                    rest(V2L[dst], BANK[2 + st.m % 2][:].rearrange("p (k n) -> p k n", k=KT), V2H[dst]).then_inc(v2_l.sem, 1)
                elif kind == "evac_q2":
                    b, t = from_bank(2, st), TMP[:, 2 + st.m % 2, :]
                    if st.q2 >= 2:
                        dve.wait_ge(q2_l.sem, q2_l.after(2, st.q2 - 2))
                    else:
                        dve.wait_ge(v2_pe.sem, v2_pe.after(2, DT - 2 + st.q2))
                    dve.scalar_tensor_tensor(t, b[:], HD ** -0.5, RSTD[:], ALU.mult, ALU.mult).then_inc(bank_free.sem, 1)
                    dve.wait_ge(q2_h.sem, q2_h.after(2, st.q2))
                    rest(Q2L[:, st.m, :], t, Q2H[:, st.m, :]).then_inc(q2_l.sem, 1)
                elif kind == "sb_scores":
                    dve.wait_ge(z.sem, z.after(2, st.h))
                    if st.h:
                        dve.wait_ge(softplus_done.sem, softplus_done.after(2, st.h - 1))
                    pieces = [(slice(SEQ * k, SEQ * k + n), BANK[3 * (st.h % 2) + k][:, 0:n])
                              for k, n in enumerate((SEQ, SEQ, SEQ // 2))]
                    for k, (cols, b) in enumerate(pieces):
                        dve.tensor_scalar(SBP[:, cols], b, 0.0, None, ALU.max).then_inc(z_pos.sem, 1)
                        dve.wait_ge(z_pos.sem, z_pos.after(2, 3 * st.h + k))
                        dve.scalar_tensor_tensor(SBZ[:, cols], SBP[:, cols], -2.0, b, ALU.mult, ALU.add).then_inc(z_negabs.sem, 1)
                elif kind == "sb_sum":
                    dve.wait_ge(z_log.sem, z_log.after(2, 2 * st.h + 1))
                    if st.h:
                        dve.wait_ge(w.sem, w.after(2, st.h - 1))
                    dve.tensor_tensor(SBS[:], SBP[:], SBZ[:], ALU.add).then_inc(softplus_done.sem, 1)
                elif kind == "sb_cut":
                    dve.wait_ge(z_h.sem, z_h.after(2, st.h))
                    rest(SPL[:], SBS[:], SPH[:]).then_inc(z_l.sem, 1)
                elif kind == "sb_out_cut":
                    rows = slice(st.h % 2 * HD, st.h % 2 * HD + HD)
                    dve.wait_ge(o_h.sem, o_h.after(2, st.h))
                    rest(Q2L[rows, st.h // 2, :], BANK[6 + st.h % 2][rows, :], Q2H[rows, st.h // 2, :]).then_inc(o_l.sem, 1)
                elif kind == "final":
                    g = S_GAIN["final", 0]
                    dve.wait_ge(rstd.sem, rstd.after(2, st.g))
                    for k in range(DT):
                        dve.scalar_tensor_tensor(FF[:, k, :], X[:, k, :], SP_[:, g + k:g + k + 1], RSTD[:], ALU.mult, ALU.mult
                                                 ).then_inc(outs.sem, 1)

            dve.sem_inc(lo.sem, RAW)
            dve.sem_inc(bank_free.sem, 2)
            dve.sem_inc(turn_free.sem, 1)
            dve.sem_inc(probs_l.sem, 2)
            dve.wait_ge(x_in, 16 * DT)
            dve.sem_inc(x_done.sem, DT)
            cut(0, 0, SLOT)
            with dve.Fori(0, LAYERS) as l:
                for st in LAYER.steps:
                    step(l, st)
            for st in SECOND.steps:
                second(st)

        @block.tensor
        def _(pe):
            def product(out_, w, x_, start, stop, **how):
                nc.tensor.matmul(out_, w[0], x_[0], start=start, stop=False, **how)
                nc.tensor.matmul(out_, w[0], x_[1], start=False, stop=False, **how)
                return nc.tensor.matmul(out_, w[1], x_[0], start=False, stop=stop, **how)

            inputs = {"u": (UH, UL), "merged": (MH, ML), "ya": (QH, QL), "yb": (YBH, YBL), "hidden": (HH, HL),
                      "s5": (UH, UL), "conv": (CHH, CHL), "y2": (Q2H, Q2L)}

            def linear_job(l, st, ready):
                xh, xl = inputs[st.rhs]
                pe.wait_ge(bank_free.sem, bank_free.room(l, st.j))
                n = len(st.kt)
                k0 = 0
                for i, kt in enumerate(st.kt):
                    c = st.c + i
                    pe.wait_ge(lo.sem, lo.after(l, c))
                    for k in range(kt):
                        if st.first:
                            pe.wait_ge(*ready(k0 + k))
                        cols = slice(((st.at or 0) + k) * st.cols, ((st.at or 0) + k + 1) * st.cols)
                        ins = product(BANK[st.j % 2][0:st.cols, :], (WH[:, c % CUT, cols], WL[:, c % CUT, cols]),
                                      (xh[:, k0 + k, :], xl[:, k0 + k, :]), k0 + k == 0, i == n - 1 and k == kt - 1)
                    if st.half is None:
                        ins.then_inc(used.sem, 1)
                    else:
                        ins.then_inc(half.sem, 1)
                    k0 += kt

            def small_job(l, j, c, at_, kt, cols, k0):
                pe.wait_ge(bank_free.sem, bank_free.room(l, j))
                for k in range(kt):
                    w_ = slice(at_ + k * cols, at_ + (k + 1) * cols)
                    ins = product(BANK[j % 2][0:cols, :], (WH[:, c % CUT, w_], WL[:, c % CUT, w_]),
                                  (CH[:, k0 + k, :], CL[:, k0 + k, :]), k == 0, k == kt - 1)
                return ins

            def add_square(l, s, g, ones, first, last):
                if first and g >= 2:
                    pe.wait_ge(logged.sem, logged.after(l, g - 2))
                pe.wait_ge(sq.sem, sq.after(l, s))
                nc.tensor.matmul(stat_bank(g)[:], ones, TMP[:, s % 2, :], start=first, stop=last).then_inc(summed.sem, 1)

            def add_total(l, a, g, total, first):
                if first and g >= 2:
                    pe.wait_ge(logged.sem, logged.after(l, g - 2))
                pe.wait_ge(added.sem, added.after(l, a))
                nc.tensor.matmul(stat_bank(g)[:], ONES, total, start=first, stop=False)

            def stat(l, st, total):
                n = DT - 1 - ADDED
                for k in range(n):
                    if k == n - 1:
                        add_total(l, st.a + ADDED - 1, st.g, total, False)
                    add_square(l, st.s + k, st.g, ONES, k == 0, k == n - 1)

            state = {}

            def step(l, st):
                kind = st.kind
                if kind in ("norm", "regain"):
                    state["n"] = st.n
                elif kind == "mm":
                    n = state["n"]
                    ready = {"u": lambda k: (ul.sem, ul.after(l, n + k)),
                             "merged": lambda k: (merged_l.sem, merged_l.after(l, k)),
                             "ya": lambda k: (y_l.sem, y_l.after(l, 2 * HEADS - 1)),
                             "yb": lambda k: (y_l.sem, y_l.after(l, 2 * HEADS - 1)),
                             "hidden": lambda k: (hid_l.sem, hid_l.after(l, state["up"] - HALF + 1 + k))}[st.rhs]
                    linear_job(l, st, ready)
                elif kind == "evac_up":
                    state["up"] = st.up
                elif kind == "stat":
                    stat(l, st, SQUARES[:])
                elif kind in ("evac_q", "evac_k"):
                    add_square(l, st.s, st.group, ONES_HEAD, True, True)
                elif kind in ("evac_cq", "evac_ckv"):
                    add_square(l, st.s, st.group, ONES, st.i == 0, st.i == (CQT if kind == "evac_cq" else CKT) - 1)
                elif kind == "evac_ff" and st.s is not None:
                    add_total(l, st.last_a, st.group, SQUARES[:], True)
                    add_square(l, st.s, st.group, ONES, False, True)
                elif kind == "turn":
                    rot = ROT_A if st.what in "qk" else ROT_B
                    rows = slice(0, st.rows)
                    pe.wait_ge(rl.sem, rl.after(l, st.rot))
                    pe.wait_ge(turn_free.sem, turn_free.room(l, st.b))
                    nc.tensor.matmul(TURN[rows, :], rot[rows, rows], RH[rows, :], start=True, stop=False)
                    nc.tensor.matmul(TURN[rows, :], rot[rows, rows], RL[rows, :], start=False, stop=True
                                     ).then_inc(turn.sem, 1)
                elif kind == "gqa_v":
                    pe.wait_ge(bank_free.sem, bank_free.after(l, st.j))
                    pe.wait_ge(turn_free.sem, turn_free.room(l, st.b))
                    for k in range(KT):
                        ins = nc.tensor.transpose(TURN[:, k * P:(k + 1) * P], TMP[:, 2 + st.x % 2, k * P:(k + 1) * P], IDENT)
                    ins.then_inc(turn.sem, 1)
                elif kind == "mla_mm":
                    pe.wait_ge(lo.sem, lo.after(l, st.c))
                    if st.h == 0:
                        pe.wait_ge(c_l.sem, c_l.after(l, CQT + CKT - 1))
                    small_job(l, st.j, st.c, 0, CQT, QK, 0)
                    small_job(l, st.j + 1, st.c, CQT * QK, CKT, P, CQT).then_inc(used.sem, 1)
                elif kind == "mla_v":
                    pe.wait_ge(bank_free.sem, bank_free.after(l, st.j + 1))
                    pe.wait_ge(turn_free.sem, turn_free.room(l, st.b))
                    for k in range(KT):
                        ins = nc.tensor.transpose(TURN[:, k * P:(k + 1) * P], KVF[:, st.h % 2, k * P:(k + 1) * P], IDENT)
                    ins.then_inc(turn.sem, 1)
                elif kind == "att_scores":
                    q = slice(st.t * P, (st.t + 1) * P)
                    if st.u == 0:
                        pe.wait_ge(rot_l.sem, rot_l.after(l, QT))
                        pe.wait_ge(logged.sem, logged.after(l, RC_LAST))
                    if st.h >= HEADS and st.t == 0:
                        pe.wait_ge(rot_l.sem, rot_l.after(l, QT + 2 + st.h - HEADS))
                        pe.wait_ge(mk_l.sem, mk_l.after(l, st.h - HEADS))
                    pe.wait_ge(expd.sem, expd.room(l, st.u))
                    if st.h < HEADS:
                        rows, i = slice(st.h // QT * HD, st.h // QT * HD + HD), st.h % QT
                        qs = QH[rows, i, q], QL[rows, i, q]
                        ks = KH[rows, :], KL[rows, :]
                    else:
                        i = st.h % 2
                        qs = MQH[0:QK, i, q], MQL[0:QK, i, q]
                        ks = MKH[0:QK, i, :], MKL[0:QK, i, :]
                    product(BANK[2 + st.u % 2][:], qs, ks, True, True).then_inc(scores.sem, 1)
                elif kind == "att_transpose":
                    pe.wait_ge(normed.sem, normed.after(l, st.u))
                    pe.wait_ge(probs_l.sem, probs_l.room(l, st.u))
                    for k in range(KT):
                        ins = nc.tensor.transpose(BANK[4 + st.u % 2][:, k * P:(k + 1) * P],
                                                  TMP[:, st.u % 4, k * P:(k + 1) * P], IDENT)
                    ins.then_inc(probs_t.sem, 1)
                elif kind == "att_values":
                    if st.keys[0] == 0:
                        pe.wait_ge(probs_l.sem, probs_l.after(l, KT * st.h + KT - 1))
                        if st.h:
                            pe.wait_ge(y_l.sem, y_l.after(l, st.h - 1))
                        if st.h == HEADS:
                            pe.wait_ge(mv_zero, l + 1)
                    for k in st.keys:
                        v = (VH[:, k, :], VL[:, k, :]) if st.h < HEADS else (MVH[:, st.h % 2, k, :], MVL[:, st.h % 2, k, :])
                        ins = product(OUTB[:], v, (PHH[:, st.h % 2, k, :], PHL[:, st.h % 2, k, :]), k == 0, k == KT - 1)
                    if k == KT - 1:
                        ins.then_inc(pv.sem, 1)

            def second_pe(st):
                kind = st.kind
                if kind in ("norm", "regain"):
                    state["n"] = st.n
                elif kind == "mm":
                    n = state["n"]
                    ready = {"u": lambda k: (ul.sem, ul.after(2, n + k)),
                             "s5": lambda k: (ge_l.sem, ge_l.after(2, k)),
                             "conv": lambda k: (conv_l.sem, conv_l.after(2, state["cu"] - C_TILES + 1 + k)),
                             "y2": lambda k: (o_l.sem, o_l.after(2, 2 * k + 1))}[st.rhs]
                    linear_job(2, st, ready)
                    state["j"] = st.j
                elif kind == "evac_cup":
                    state["cu"] = st.cu
                elif kind in ("stat", "final"):
                    stat(2, st, total_of(st))
                elif kind == "s5_factors":
                    pe.wait_ge(sp_pool.sem, 34)
                    for k in range(4):
                        for t in range(4):
                            j = 4 * (4 * (k % 2) + t)
                            ins = nc.tensor.transpose(BANK[2 + k][:, t * P:(t + 1) * P],
                                                      S5BB[:, k // 2, j:j + 4, :].rearrange("p j h -> p (j h)"), IDENT)
                        ins.then_inc(sp_pe.sem, 1)
                elif kind == "s5_table":
                    rows = slice(32 * (st.p % 4), 32 * (st.p % 4) + 32)
                    if st.p == 0:
                        pe.wait_ge(sp_act.sem, 10)
                        pe.wait_ge(bank_free.sem, bank_free.after(2, DT - 1))
                    if st.p >= 2:
                        pe.wait_ge(ro.sem, ro.after(2, 4 * (st.p - 2) + 3))
                    for k in range(2):
                        ins = nc.tensor.matmul(BANK[2 + 2 * (st.p % 2) + k][:], BBT[rows, k, st.p // 4, :], S5U[rows, st.p // 4, :],
                                               start=True, stop=True)
                    ins.then_inc(state_in.sem, 1)
                elif kind == "s5_out":
                    rows = slice(32 * (st.p % 4), 32 * (st.p % 4) + 32)
                    t = st.p // 4
                    a = [S5T[:, 4 * (st.p % 3) + k, :] for k in range(4)]
                    if st.p % 4 == 0 and t >= 2:
                        pe.wait_ge(s5_y.sem, s5_y.after(2, t - 2))
                    pe.wait_ge(out_pool.sem, out_pool.after(2, 2 * st.p + 1))
                    pe.wait_ge(out_dve.sem, out_dve.after(2, 2 * st.p + 1))
                    for n, (k, part) in enumerate(((0, 0), (1, 0), (2, 2), (3, 1))):
                        ins = nc.tensor.matmul(BANK[6 + t % 2][rows, :], S5C[:, part, st.p, :], a[k],
                                               start=n == 0, stop=n == 3)
                    ins.then_inc(s5_sum.sem, 1)
                elif kind == "v2_turn":
                    pe.wait_ge(bank_free.sem, bank_free.after(2, st.j))
                    if st.m >= 2:
                        pe.wait_ge(v2_l.sem, v2_l.after(2, st.m - 2))
                    for k in range(KT):
                        ins = nc.tensor.transpose(BANK[2 + st.m % 2][:, k * P:(k + 1) * P],
                                                  TMP[:, 2 + st.kv % 2, k * P:(k + 1) * P], IDENT)
                    ins.then_inc(v2_pe.sem, 1)
                elif kind == "sb_scores":
                    rows = slice(st.h % 2 * HD, st.h % 2 * HD + HD)
                    i = st.h // 2
                    if st.h == 0:
                        pe.wait_ge(bank_free.sem, bank_free.after(2, state["j"]))
                        pe.wait_ge(v2_l.sem, v2_l.after(2, DT - 1))
                    pe.wait_ge(q2_l.sem, q2_l.after(2, i))
                    if st.h >= 2:
                        pe.wait_ge(w_exp.sem, w_exp.after(2, st.h - 2))
                    for k in (0, 1, 3, 2):
                        b, c = divmod(COL[k], SEQ)
                        product(BANK[3 * (st.h % 2) + b][:, c:c + WIDE[k]],
                                (K2H[rows, i, k * P:(k + 1) * P], K2L[rows, i, k * P:(k + 1) * P]),
                                (Q2H[rows, i, k * P:], Q2L[rows, i, k * P:]), k != 3, False, skip_group_check=True)
                        ins = nc.tensor.matmul(BANK[3 * (st.h % 2) + b][:, c:c + P], IDENT, MASK[:], start=False, stop=False,
                                               skip_group_check=True)
                    ins.then_inc(z.sem, 1)
                elif kind == "sb_weights":
                    pe.wait_ge(z_l.sem, z_l.after(2, st.h))
                    for k in range(KT):
                        b, c = divmod(COL[k], SEQ)
                        for k2 in range(k, KT):
                            mat = NEG_TRI if k2 == k else NEG_ONES
                            d = c + (k2 - k) * P
                            for part in (SPH, SPL):
                                ins = nc.tensor.matmul(BANK[3 * (st.h % 2) + b][:, d:d + WIDE[k2]], mat,
                                                       part[:, COL[k2]:COL[k2] + WIDE[k2]], start=False, stop=False,
                                                       skip_group_check=True)
                    ins.then_inc(w.sem, 1)
                elif kind == "sb_out":
                    pe.wait_ge(w_l.sem, w_l.after(2, st.h))
                    if st.h >= 2:
                        pe.wait_ge(o_l.sem, o_l.after(2, st.h - 2))
                    i = st.h // 2
                    for k in range(KT):
                        cols = slice(COL[k], COL[k] + WIDE[k])
                        ins = product(BANK[6 + st.h % 2][:, k * P:], (V2H[:, k, i * P:(i + 1) * P], V2L[:, k, i * P:(i + 1) * P]),
                                      (WTH[st.h % 3][:, cols], WTL[st.h % 3][:, cols]), k == 0, k == KT - 1, skip_group_check=True)
                    ins.then_inc(o.sem, 1)
            pe.wait_ge(mat_in, 64)
            pe.wait_ge(mats_cut, 1)
            pe.sem_inc(used.sem, CUT)
            pe.sem_inc(summed.sem, 2)
            pe.sem_inc(probs_t.sem, 4)
            with pe.Fori(0, LAYERS) as l:
                for st in LAYER.steps:
                    step(l, st)
            for st in SECOND.steps:
                second_pe(st)


def packed(w, k0, kt, c0, cols, rows=None):
    part = w[k0 * P:(k0 + kt) * P] if rows is None else w[rows]
    return part[:, c0:c0 + cols].reshape(kt, P, cols).transpose(1, 0, 2).reshape(P, kt * cols)


def weight_stream(w):
    chunks = []

    def whole(matrix, c0, n, cols=P):
        for m in range(n):
            chunks.append(packed(matrix, 0, matrix.shape[0] // P, c0 + m * cols, cols))

    paired = np.concatenate([np.arange(h * HD, h * HD + HD) for i in range(QT) for h in (i, QT + i)])
    for l in range(LAYERS):
        w_in = w["w_in"][l]
        q_pairs = w_in[:, paired]
        whole(q_pairs, 0, QT)
        kv0 = HEADS * HD
        low0 = kv0 + 2 * KV_HEADS * HD
        rope0 = low0 + Q_RANK + KV_RANK
        gate0 = rope0 + ROPE
        whole(w_in, kv0, 2)
        whole(w_in, low0, CQT + CKT)
        whole(w_in, rope0 - HD, 1, QK)
        for h in range(HEADS):
            chunks.append(np.concatenate([packed(w["w_q_up"][l], 0, CQT, h * QK, QK),
                                          packed(w["w_kv_up"][l], 0, CKT, h * P, P)], axis=1))
        for m in range(DT):
            whole(w_in, gate0 + m * P, 1)
            whole(w_in, gate0 + DM + m * P, 1)
            chunks.append(np.concatenate([packed(w["w_branch_a"][l], 0, QT, m * P, P, rows=paired),
                                          packed(w["w_branch_b"][l], 0, QT, m * P, P)], axis=1))
        whole(w["w_o"][l], 0, DT)
        for half in range(2):
            whole(w["w_ffn_up"][l], half * HALF * P, HALF)
            for m in range(DT):
                for k in range(2):
                    chunks.append(packed(w["w_ffn_down"][l], half * HALF + k * DT, DT, m * P, P))

    def conv_ffn(layer):
        up, down = w["ffn_w_up_2"][layer], w["ffn_w_down_2"][layer]
        for m in range(C_TILES):
            whole(up, m * P, 1)
            whole(up, (C_TILES + m) * P, 1)
        for m in range(DT):
            for k0 in range(0, C_TILES, DT):
                chunks.append(packed(down, k0, min(DT, C_TILES - k0), m * P, P))

    whole(w["ssm_w_in_2"][0], 0, DT)
    for m in range(DT):
        whole(w["ssm_w_glu_2"][0], DM + m * P, 1)
        whole(w["ssm_w_glu_2"][0], m * P, 1)
    conv_ffn(0)
    whole(w["kv_w_2"], 0, 2 * DT)
    whole(w["attn_w_q_2"][0], 0, DT)
    whole(w["attn_w_o_2"][0], 0, DT)
    conv_ffn(1)
    stream = np.zeros((CHUNKS, P, SLOT), np.float32)
    assert len(chunks) == CHUNKS
    for c, chunk in enumerate(chunks):
        stream[c, :, :chunk.shape[1]] = chunk
    return stream


def by_tile(v):
    return v.reshape(-1, P).T


def layer_parameters(w):
    rows = []
    for l in range(LAYERS):
        cols = [by_tile(w[k][l]) for k in ("pre_mix_g", "post_mix_g", "pre_ffn_g", "post_ffn_g", "b_gate")]
        cols += [np.tile(w[k][l], 2)[:, None] for k in ("q_norm_g", "k_norm_g")]
        cols += [by_tile(w[k][l]) for k in ("q_a_norm_g", "kv_a_norm_g")]
        rows.append(np.concatenate(cols, axis=1))
    return np.stack(rows)


def by_pair(v):
    return v.reshape(PAIRS, 2 * STATE).T


def second_parameters(w):
    cols = [by_tile(w["norm_mix_2"][0]), by_tile(w["norm_mix_2"][1]), by_tile(w["norm_ffn_2"][0]),
            by_tile(w["norm_ffn_2"][1]), by_tile(w["norm_kv_2"]), by_tile(w["norm_final_2"]),
            by_tile(w["ssm_d_2"][0].reshape(-1))]
    for layer in range(LAYERS):
        taps = [by_tile(w["ffn_conv_w_2"][layer, k, 0]) for k in range(3)] + [by_tile(w["ffn_conv_b_2"][layer])]
        cols.append(np.stack(taps, axis=2).reshape(P, C_TILES * 4))
    cols += [by_pair(w["ssm_a_re_2"][0]), by_pair(w["ssm_a_im_2"][0]),
             by_pair(np.repeat(w["ssm_log_dt_2"][0][:, None], STATE, axis=1))]
    return np.concatenate(cols, axis=1)


def pair_blocks(v):
    wide = np.zeros((2, STATE, PAIRS, 2, GH), np.float32)
    for g in range(2):
        wide[g, :, :, g, :] = v[g::2].transpose(1, 0, 2)
    return wide.reshape(P, PAIRS * 2 * GH)


def rotation(dim, at_):
    m = np.zeros((P, P), np.float32)
    quarter = dim // 4
    for a in at_:
        for half in (a, a + dim // 2):
            for k in range(quarter):
                m[half + quarter + k, half + k] = -1.0
                m[half + k, half + quarter + k] = 1.0
    return m


def angles(dim):
    token = np.arange(SEQ)
    row, col = (token // GRID_W).astype(np.float32), (token % GRID_W).astype(np.float32)
    half = dim // 2
    inv = np.float32(ROPE_THETA) ** (-np.arange(0, half, 2, dtype=np.float32) / np.float32(half))
    ar, ac = row[:, None] * inv[None], col[:, None] * inv[None]
    a = np.concatenate([ar, ar, ac, ac], axis=1).T
    return np.cos(a).astype(np.float32), np.sin(a).astype(np.float32)


def constants():
    eye, ones = np.eye(P, dtype=np.float32), np.ones((P, P), np.float32)
    ones_head = np.kron(np.eye(2, dtype=np.float32), np.ones((HD, HD), np.float32))
    mats = [eye, ones, ones_head, rotation(HD, (0, HD)), rotation(ROPE, (HD,)), -np.tril(ones), -ones,
            HIDDEN * np.tril(ones)]
    cos_a, sin_a = angles(HD)
    tables = np.zeros((4, P, SEQ), np.float32)
    tables[0], tables[1] = np.tile(cos_a, (2, 1)), np.tile(sin_a, (2, 1))
    tables[2] = 1.0
    tables[2, HD:QK], tables[3, HD:QK] = angles(ROPE)
    steps = np.tile(np.concatenate([FINE * np.arange(COARSE), np.arange(FINE)]).astype(np.float32), (P, 1))
    return np.concatenate(mats, axis=1), tables, steps


def kernel(**inputs):
    import concourse.bacc as _bacc
    from concourse.bass_utils import run_bass_kernel_spmd as _run

    w = {name: np.asarray(a) for name, a in inputs.items()}
    mats, tables, steps = constants()
    arrays = {
        "weights": weight_stream(w),
        "x": np.ascontiguousarray(w["x"][0].T).reshape(DT, P, SEQ),
        "layer_params": layer_parameters(w),
        "second_params": second_parameters(w),
        "mats": mats,
        "tables": tables,
        "steps_t": steps,
        "s5_b": np.stack([pair_blocks(w["ssm_b_re_2"][0]), pair_blocks(w["ssm_b_im_2"][0])]),
        "s5_c": np.stack([pair_blocks(w[k][0].transpose(0, 2, 1)) for k in ("ssm_c_re_2", "ssm_c_im_2")]),
    }
    arrays = {name: np.ascontiguousarray(a, dtype=np.float32) for name, a in arrays.items()}
    nc = _bacc.Bacc("TRN2", target_bir_lowering=False, num_devices=1)
    args = {name: nc.dram_tensor(name, a.shape, F32, kind="ExternalInput").ap() for name, a in arrays.items()}
    out = nc.dram_tensor("out", (DT, P, SEQ), F32, kind="ExternalOutput").ap()
    build(nc, out=out, **args)
    r = _run(nc, [arrays], core_ids=[0])
    return np.ascontiguousarray(r.results[0]["out"].reshape(DM, SEQ).T)[None]
```
